# Optimizing a Trainium2 kernel written in Bass

```python
import math
import jax
import jax.numpy as jnp
from jax import lax
import numpy as np

D_MODEL = 1024
BATCH = 1
SEQ = 1024
DEPTH = 2

GRID_W = 64
CTX_LEN = 256
N_GROUPS = 4
GROUP_W = D_MODEL // N_GROUPS
MIX_W = N_GROUPS * GROUP_W
N_H = 4
HEAD_DIM = GROUP_W // N_H
ROT_DIM = HEAD_DIM // 2
ROPE_THETA = 10000.0
Q_BLOCK = 128
DIFF_QK = HEAD_DIM // 2
MLA_Q_RANK = D_MODEL // 4
MLA_KV_RANK = D_MODEL // 8
MLA_NOPE = HEAD_DIM
MLA_ROPE = ROT_DIM
GLA_DK = HEAD_DIM // 2
GLA_GATE_RANK = 16
GLA_GATE_NORM = 16.0
RET_DK = HEAD_DIM // 2
CHUNK = 64
FFN_HIDDEN = -(-8 * D_MODEL // (3 * 256)) * 256
RMS_EPS = 1e-6

IN_SIZES = (
    N_H * 2 * DIFF_QK, N_H * 2 * DIFF_QK, N_H * HEAD_DIM,
    MLA_Q_RANK, MLA_KV_RANK, MLA_ROPE,
    N_H * GLA_DK, N_H * GLA_DK, N_H * HEAD_DIM, N_H * HEAD_DIM,
    GLA_GATE_RANK, GLA_GATE_RANK,
    N_H * RET_DK, N_H * RET_DK, N_H * HEAD_DIM, N_H * HEAD_DIM,
)
IN_WIDTH = sum(IN_SIZES)
IN_SPLITS = tuple(int(s) for s in np.cumsum(IN_SIZES)[:-1])

kernel_name = 'hybrid_parallel_group_dit_trunk'

def rms_norm(x, g):
    xf = x.astype(jnp.float32)
    y = xf * lax.rsqrt(jnp.mean(xf * xf, axis=-1, keepdims=True) + RMS_EPS)
    return (y * g.astype(jnp.float32)).astype(x.dtype)

def modulate(h, shift, scale):
    return h * (1.0 + scale) + shift

def axial_rope(rows, rot_dim):
    row = jnp.repeat(jnp.arange(rows, dtype=jnp.float32), GRID_W)
    col = jnp.tile(jnp.arange(GRID_W, dtype=jnp.float32), rows)
    n_freq = rot_dim // 4
    freqs = ROPE_THETA ** (-jnp.arange(n_freq, dtype=jnp.float32) / n_freq)
    ang = jnp.concatenate([row[:, None] * freqs, col[:, None] * freqs], axis=-1)
    return jnp.cos(ang), jnp.sin(ang)

def apply_rope(t, cos, sin):
    t1, t2 = jnp.split(t, 2, axis=-1)
    c, s = cos[:, None, :], sin[:, None, :]
    return jnp.concatenate([t1 * c - t2 * s, t1 * s + t2 * c], axis=-1).astype(t.dtype)

def attend(q, k, v, map_w):
    s = jnp.einsum('bqhmd,bkhmd->bhmqk', q, k).astype(jnp.float32)
    p = jax.nn.softmax(s, axis=-1)
    w = jnp.einsum('bhmqk,mh->bhqk', p, map_w.astype(jnp.float32))
    return jnp.einsum('bhqk,bkhd->bqhd', w.astype(v.dtype), v)

def blocked_attend(q, k, v, map_w):
    B, Lq = q.shape[:2]
    qb = q.reshape((B, Lq // Q_BLOCK, Q_BLOCK) + q.shape[2:]).swapaxes(0, 1)
    ob = lax.map(lambda qi: attend(qi, k, v, map_w), qb)
    return ob.swapaxes(0, 1).reshape((B, Lq) + ob.shape[3:])

def _chunks(t):
    B, L, H, d = t.shape
    return t.reshape(B, L // CHUNK, CHUNK, H, d).transpose(1, 0, 3, 2, 4)

def _unchunk(t):
    n, B, H, C, d = t.shape
    return t.transpose(1, 0, 3, 2, 4).reshape(B, n * C, H, d)

def gla_chunk_scan(q, k, v, log_a, state0):
    causal = jnp.tril(jnp.ones((CHUNK, CHUNK), dtype=bool))[:, :, None]

    def step(S, blk):
        qc, kc, vc, ac = blk
        b = jnp.cumsum(ac, axis=2)
        rel = jnp.where(causal, b[:, :, :, None, :] - b[:, :, None, :, :], -jnp.inf)
        scores = jnp.einsum('bhid,bhjd,bhijd->bhij', qc, kc, jnp.exp(rel))
        b_end = b[:, :, -1:, :]
        o = (jnp.einsum('bhij,bhje->bhie', scores, vc)
             + jnp.einsum('bhid,bhde->bhie', qc * jnp.exp(b), S))
        S_new = (jnp.exp(b_end)[:, :, 0, :, None] * S
                 + jnp.einsum('bhjd,bhje->bhde', kc * jnp.exp(b_end - b), vc))
        return S_new, o

    S_fin, out = lax.scan(step, state0, (_chunks(q), _chunks(k), _chunks(v), _chunks(log_a)))
    return _unchunk(out).astype(v.dtype), S_fin

def retention_chunk_scan(q, k, v, log_gamma, state0):
    pos = jnp.arange(CHUNK, dtype=jnp.float32)
    rel = pos[:, None] - pos[None, :]
    decay_in = jnp.exp(jnp.where(rel >= 0, rel * log_gamma[:, None, None], -jnp.inf))
    decay_q = jnp.exp((pos[None, :] + 1.0) * log_gamma[:, None])[None, :, :, None]
    decay_k = jnp.exp((CHUNK - 1.0 - pos[None, :]) * log_gamma[:, None])[None, :, :, None]
    decay_chunk = jnp.exp(CHUNK * log_gamma)[None, :, None, None]

    def step(S, blk):
        qc, kc, vc = blk
        inner = jnp.einsum('bhid,bhjd->bhij', qc, kc) * decay_in
        o = (jnp.einsum('bhij,bhje->bhie', inner, vc)
             + jnp.einsum('bhid,bhde->bhie', qc, S) * decay_q)
        S_new = decay_chunk * S + jnp.einsum('bhjd,bhje->bhde', kc * decay_k, vc)
        return S_new, o

    S_fin, out = lax.scan(step, state0, (_chunks(q), _chunks(k), _chunks(v)))
    return _unchunk(out).astype(v.dtype), S_fin

def bidirectional_scan(scan, ctx_in, lat_in, with_ctx):
    def rev(t):
        return jnp.flip(t, 1) if t.ndim == 4 else t
    qc, kc, vc, dcf, dcb = ctx_in
    ql, kl, vl, dlf, dlb = lat_in
    s0 = jnp.zeros((qc.shape[0], qc.shape[2], qc.shape[3], vc.shape[3]), jnp.float32)
    oc_f, sc_f = scan(qc, kc, vc, dcf, s0)
    oc_b, sc_b = scan(rev(qc), rev(kc), rev(vc), rev(dcb), s0)
    ol_f, _ = scan(ql, kl, vl, dlf, sc_f)
    ol_b, _ = scan(rev(ql), rev(kl), rev(vl), rev(dlb), sc_b)
    o_ctx = (oc_f + rev(oc_b)) if with_ctx else None
    return o_ctx, ol_f + rev(ol_b)

def diff_attention(p_ctx, p_lat, rope, lam_vecs, sub_g, lambda_init, with_ctx):
    def prep(q, k, v, rotate):
        B, L = q.shape[:2]
        q = q.reshape(B, L, 2 * N_H, DIFF_QK)
        k = k.reshape(B, L, 2 * N_H, DIFF_QK)
        if rotate:
            q, k = apply_rope(q, *rope), apply_rope(k, *rope)
        return (q.reshape(B, L, N_H, 2, DIFF_QK) * DIFF_QK ** -0.5,
                k.reshape(B, L, N_H, 2, DIFF_QK),
                v.reshape(B, L, N_H, HEAD_DIM))

    lq1, lk1, lq2, lk2 = lam_vecs.astype(jnp.float32)
    lam = jnp.exp(jnp.sum(lq1 * lk1)) - jnp.exp(jnp.sum(lq2 * lk2)) + lambda_init
    map_w = jnp.stack([jnp.ones((N_H,), jnp.float32), jnp.broadcast_to(-lam, (N_H,))])

    def finish(o):
        return (rms_norm(o, sub_g) * (1.0 - lambda_init)).reshape(o.shape[0], o.shape[1], GROUP_W)

    qc, kc, vc = prep(*p_ctx, False)
    ql, kl, vl = prep(*p_lat, True)
    o_lat = blocked_attend(ql, jnp.concatenate([kc, kl], 1), jnp.concatenate([vc, vl], 1), map_w)
    o_ctx = finish(attend(qc, kc, vc, map_w)) if with_ctx else None
    return o_ctx, finish(o_lat)

def latent_attention(p_ctx, p_lat, rope, q_g, kv_g, w_uq, w_ukv, with_ctx):
    scale = (MLA_NOPE + MLA_ROPE) ** -0.5

    def prep(q_c, kv_c, k_r, rotate):
        B, L = q_c.shape[:2]
        q = (rms_norm(q_c, q_g) @ w_uq).reshape(B, L, N_H, MLA_NOPE + MLA_ROPE)
        kv = (rms_norm(kv_c, kv_g) @ w_ukv).reshape(B, L, N_H, MLA_NOPE + HEAD_DIM)
        q_nope, q_rope = q[..., :MLA_NOPE], q[..., MLA_NOPE:]
        k_nope, v = kv[..., :MLA_NOPE], kv[..., MLA_NOPE:]
        k_rope = k_r[:, :, None, :]
        if rotate:
            q_rope, k_rope = apply_rope(q_rope, *rope), apply_rope(k_rope, *rope)
        k_rope = jnp.broadcast_to(k_rope, (B, L, N_H, MLA_ROPE))
        q = jnp.concatenate([q_nope, q_rope], -1)[:, :, :, None, :] * scale
        k = jnp.concatenate([k_nope, k_rope], -1)[:, :, :, None, :]
        return q, k, v

    map_w = jnp.ones((1, N_H), jnp.float32)
    qc, kc, vc = prep(*p_ctx, False)
    ql, kl, vl = prep(*p_lat, True)
    o_lat = blocked_attend(ql, jnp.concatenate([kc, kl], 1), jnp.concatenate([vc, vl], 1), map_w)

    def flat(o):
        return o.reshape(o.shape[0], o.shape[1], GROUP_W)
    o_ctx = flat(attend(qc, kc, vc, map_w)) if with_ctx else None
    return o_ctx, flat(o_lat)

def gated_linear_attention(p_ctx, p_lat, w_gate, b_gate, out_g, with_ctx):
    def prep(q, k, v, r, g_f, g_b):
        B, L = q.shape[:2]
        gates = [jax.nn.log_sigmoid((g @ w_gate[d] + b_gate[d]).astype(jnp.float32))
                 .reshape(B, L, N_H, GLA_DK) / GLA_GATE_NORM for d, g in enumerate((g_f, g_b))]
        return (q.reshape(B, L, N_H, GLA_DK) * GLA_DK ** -0.5, k.reshape(B, L, N_H, GLA_DK),
                v.reshape(B, L, N_H, HEAD_DIM), gates[0], gates[1]), r

    def finish(o, r):
        B, L = o.shape[:2]
        return (rms_norm(o, out_g) * jax.nn.silu(r).reshape(B, L, N_H, HEAD_DIM)).reshape(B, L, GROUP_W)

    ctx_in, r_c = prep(*p_ctx)
    lat_in, r_l = prep(*p_lat)
    o_ctx, o_lat = bidirectional_scan(gla_chunk_scan, ctx_in, lat_in, with_ctx)
    return (finish(o_ctx, r_c) if with_ctx else None), finish(o_lat, r_l)

def retention(p_ctx, p_lat, rope, decay_logits, out_g, with_ctx):
    log_gamma = jax.nn.log_sigmoid(decay_logits.astype(jnp.float32))

    def prep(q, k, v, g, rotate):
        B, L = q.shape[:2]
        q = q.reshape(B, L, N_H, RET_DK)
        k = k.reshape(B, L, N_H, RET_DK) * RET_DK ** -0.5
        if rotate:
            q, k = apply_rope(q, *rope), apply_rope(k, *rope)
        return (q, k, v.reshape(B, L, N_H, HEAD_DIM), log_gamma[0], log_gamma[1]), g

    def finish(o, g):
        B, L = o.shape[:2]
        return (rms_norm(o, out_g) * jax.nn.silu(g).reshape(B, L, N_H, HEAD_DIM)).reshape(B, L, GROUP_W)

    ctx_in, g_c = prep(*p_ctx, False)
    lat_in, g_l = prep(*p_lat, True)
    o_ctx, o_lat = bidirectional_scan(retention_chunk_scan, ctx_in, lat_in, with_ctx)
    return (finish(o_ctx, g_c) if with_ctx else None), finish(o_lat, g_l)

def hybrid_mixer(hc, hl, rope, lambda_init, with_ctx, w_in, diff_lam, diff_norm,
                 mla_q_norm, mla_kv_norm, mla_w_uq, mla_w_ukv,
                 gla_w_gate, gla_b_gate, gla_norm, ret_decay, ret_norm, w_out):
    pc = jnp.split(hc @ w_in, IN_SPLITS, axis=-1)
    pl = jnp.split(hl @ w_in, IN_SPLITS, axis=-1)
    dc, dl = diff_attention(pc[0:3], pl[0:3], rope, diff_lam, diff_norm, lambda_init, with_ctx)
    mc, ml = latent_attention(pc[3:6], pl[3:6], rope, mla_q_norm, mla_kv_norm, mla_w_uq, mla_w_ukv, with_ctx)
    gc, gl = gated_linear_attention(pc[6:12], pl[6:12], gla_w_gate, gla_b_gate, gla_norm, with_ctx)
    rc, rl = retention(pc[12:16], pl[12:16], rope, ret_decay, ret_norm, with_ctx)
    out_l = jnp.concatenate([dl, ml, gl, rl], axis=-1) @ w_out
    out_c = (jnp.concatenate([dc, mc, gc, rc], axis=-1) @ w_out) if with_ctx else None
    return out_c, out_l

def swiglu(h, w_in, w_out):
    gate, up = jnp.split(h @ w_in, 2, axis=-1)
    return (jax.nn.silu(gate) * up) @ w_out

def setup_inputs(seed: int = 0) -> dict:
    key = jax.random.key(seed)
    ks = jax.random.split(key, 22)

    def nrm(k, shape, s):
        return jax.random.normal(k, shape, jnp.float32) * s

    eps = 2.0 ** (-5.0 - np.arange(N_H))
    ret_logit = jnp.asarray(np.log((1.0 - eps) / eps).astype(np.float32))
    return {
        'x': nrm(ks[0], (BATCH, SEQ, D_MODEL), 1.0),
        'c': nrm(ks[1], (BATCH, D_MODEL), 1.0),
        'ctx': nrm(ks[2], (BATCH, CTX_LEN, D_MODEL), 1.0),
        'c_ctx': nrm(ks[3], (D_MODEL,), 1.0),
        'ada_w': nrm(ks[4], (DEPTH, D_MODEL, 6 * D_MODEL), 0.5 * D_MODEL ** -0.5),
        'ada_b': nrm(ks[5], (DEPTH, 6 * D_MODEL), 0.02),
        'norm_g': 1.0 + nrm(ks[6], (DEPTH, 4, D_MODEL), 0.02),
        'w_in': nrm(ks[7], (DEPTH, D_MODEL, IN_WIDTH), D_MODEL ** -0.5),
        'diff_lam': nrm(ks[8], (DEPTH, 4, DIFF_QK), 0.1),
        'diff_norm': 1.0 + nrm(ks[9], (DEPTH, HEAD_DIM), 0.02),
        'mla_q_norm': 1.0 + nrm(ks[10], (DEPTH, MLA_Q_RANK), 0.02),
        'mla_kv_norm': 1.0 + nrm(ks[11], (DEPTH, MLA_KV_RANK), 0.02),
        'mla_w_uq': nrm(ks[12], (DEPTH, MLA_Q_RANK, N_H * (MLA_NOPE + MLA_ROPE)), MLA_Q_RANK ** -0.5),
        'mla_w_ukv': nrm(ks[13], (DEPTH, MLA_KV_RANK, N_H * (MLA_NOPE + HEAD_DIM)), MLA_KV_RANK ** -0.5),
        'gla_w_gate': nrm(ks[14], (DEPTH, 2, GLA_GATE_RANK, N_H * GLA_DK), GLA_GATE_RANK ** -0.5),
        'gla_b_gate': nrm(ks[15], (DEPTH, 2, N_H * GLA_DK), 0.1),
        'gla_norm': 1.0 + nrm(ks[16], (DEPTH, HEAD_DIM), 0.02),
        'ret_decay': ret_logit + nrm(ks[17], (DEPTH, 2, N_H), 0.01),
        'ret_norm': 1.0 + nrm(ks[18], (DEPTH, HEAD_DIM), 0.02),
        'w_out': nrm(ks[19], (DEPTH, MIX_W, D_MODEL), MIX_W ** -0.5),
        'ffn_w_in': nrm(ks[20], (DEPTH, D_MODEL, 2 * FFN_HIDDEN), D_MODEL ** -0.5),
        'ffn_w_out': nrm(ks[21], (DEPTH, FFN_HIDDEN, D_MODEL), FFN_HIDDEN ** -0.5),
    }

def reference(x, c, ctx, c_ctx, ada_w, ada_b, norm_g, w_in, diff_lam, diff_norm,
              mla_q_norm, mla_kv_norm, mla_w_uq, mla_w_ukv, gla_w_gate, gla_b_gate,
              gla_norm, ret_decay, ret_norm, w_out, ffn_w_in, ffn_w_out):
    rows = x.shape[1] // GRID_W
    rope = axial_rope(rows, ROT_DIM)
    s_lat = jax.nn.silu(c)
    s_ctx = jax.nn.silu(c_ctx)
    xl, xc = x, ctx
    for l in range(DEPTH):
        with_ctx = l < DEPTH - 1
        lambda_init = 0.8 - 0.6 * math.exp(-0.3 * l)
        mod_l = jnp.split((s_lat @ ada_w[l] + ada_b[l])[:, None, :], 6, axis=-1)
        mod_c = jnp.split(s_ctx @ ada_w[l] + ada_b[l], 6, axis=-1)
        g = norm_g[l]
        hl = modulate(rms_norm(xl, g[0]), mod_l[0], mod_l[1])
        hc = modulate(rms_norm(xc, g[0]), mod_c[0], mod_c[1])
        mc, ml = hybrid_mixer(hc, hl, rope, lambda_init, with_ctx, w_in[l], diff_lam[l], diff_norm[l],
                              mla_q_norm[l], mla_kv_norm[l], mla_w_uq[l], mla_w_ukv[l],
                              gla_w_gate[l], gla_b_gate[l], gla_norm[l], ret_decay[l], ret_norm[l], w_out[l])
        xl = xl + mod_l[2] * rms_norm(ml, g[1])
        hl = modulate(rms_norm(xl, g[2]), mod_l[3], mod_l[4])
        xl = xl + mod_l[5] * rms_norm(swiglu(hl, ffn_w_in[l], ffn_w_out[l]), g[3])
        if with_ctx:
            xc = xc + mod_c[2] * rms_norm(mc, g[1])
            hc = modulate(rms_norm(xc, g[2]), mod_c[3], mod_c[4])
            xc = xc + mod_c[5] * rms_norm(swiglu(hc, ffn_w_in[l], ffn_w_out[l]), g[3])
    return xl


_drawn_inputs = setup_inputs


def setup_inputs(seed=0):
    import zlib

    import numpy as np

    out = dict(_drawn_inputs(seed))
    spreads = {}
    factors = {'diff_lam': 5.914,
     'diff_norm': 8.0,
     'mla_q_norm': 8.0,
     'mla_kv_norm': 8.0,
     'gla_b_gate': 5.286,
     'gla_norm': 8.0,
     'ret_norm': 8.0}
    for name, (base, spread) in spreads.items():
        noise = np.random.default_rng([zlib.crc32(name.encode()), seed]).standard_normal(out[name].shape)
        drawn = base * np.exp(spread * noise) if base else spread * noise
        out[name] = jnp.asarray(drawn.astype(out[name].dtype))
    for name, factor in factors.items():
        out[name] = (out[name] * factor).astype(out[name].dtype)
    return out
```

```python
from contextlib import ExitStack

import concourse.bass as bass
from concourse import mybir

F32 = mybir.dt.float32
ALU = mybir.AluOpType
ACT = mybir.ActivationFunctionType
AX = mybir.AxisListType

P = 128
BANK = 512
D = 1024
KD = D // P
CTX, LAT = 256, 1024
N = CTX + LAT
NT = N // P
CT = CTX // P
DEPTH = 2
NH = 4
HD = 64
DK = 32
QR, KVR = 256, 128
MQ = HD + DK
GR = 16
CH = 64
NC = N // CH
CC = CTX // CH
HID = 2816
KH = HID // P
EPS = 1e-6
GATE_NORM = 16.0
LIMIT = 80.0

SIZES = (("dq", 256), ("dk", 256), ("dv", 256), ("mq", QR), ("mkv", KVR), ("mr", DK), ("gq", 128), ("gk", 128),
         ("gv", 256), ("gr", 256), ("gf", GR), ("gb", GR), ("rq", 128), ("rk", 128), ("rv", 256), ("rg", 256))
COL = {}
IN_W = 0
for _name, _size in SIZES:
    COL[_name] = IN_W
    IN_W += _size
IN_CHUNKS = 8
IN_C = IN_W // IN_CHUNKS
ADA_CHUNKS = 12
ADA_M = 6 * KD // ADA_CHUNKS

MAPS = 3 * NH

R_H = 0
R_A = KD * N
R_QKD = R_A
R_GR = R_QKD + 4 * N
R_QM = R_GR + 4 * N
R_KM = R_QM + 4 * N
R_VM = R_KM + 4 * N
R_VD = R_VM + NT * 256
R_GZ = R_VD + NT * 256
R_B = R_GZ + 2 * N
ARENA = R_B + 9800


def lambda_init(layer):
    import math
    return 0.8 - 0.6 * math.exp(-0.3 * layer)


def build(nc, t):
    ctx = ExitStack()
    with ctx:
        def sb(name, shape):
            return ctx.enter_context(nc.sbuf_tensor(name, shape, F32))

        made = {}

        def sem(name):
            if name not in made:
                made[name] = ctx.enter_context(nc.semaphore(name))
            return made[name]

        proj = nc.dram_tensor("proj", [N, IN_W], F32).ap()
        att = nc.dram_tensor("att", [N, 512], F32).ap()
        scans = nc.dram_tensor("scans", [2, N, 512], F32).ap()
        xdram = nc.dram_tensor("xdram", [P, KD, N], F32).ap()

        arena = sb("arena", [P, ARENA])

        def region(start, *dims, parts=P):
            size = 1
            for d in dims:
                size *= d
            assert start + size <= ARENA
            a = arena[0:parts, start:start + size]
            if len(dims) == 2:
                a = a.rearrange("p (a b) -> p a b", a=dims[0])
            if len(dims) == 3:
                a = a.rearrange("p (a b c) -> p a b c", a=dims[0], b=dims[1])
            if len(dims) == 4:
                a = a.rearrange("p (a b c d) -> p a b c d", a=dims[0], b=dims[1], c=dims[2])
            return a

        psum = ctx.enter_context(nc.psum_tensor("psum", [P, 8 * BANK], F32))

        def bank(b, n=BANK, parts=P):
            return psum[0:parts, b * BANK:b * BANK + n]

        ident = sb("ident", [P, P])
        ones = sb("ones", [P, P])
        eps = sb("eps", [P, 1])
        rope = sb("rope", [P, NT * 2 * DK])
        rope_t = rope[:].rearrange("p (t w d) -> p t w d", t=NT, w=2)
        heads = sb("heads", [P, NH])
        causal = sb("causal", [CH, 2 * NH * CH])
        rel = sb("rel", [CH, 2 * CH])
        steps = sb("steps", [P, 4 * CH])
        sil = sb("sil", [P, KD * 2])
        sil_in = sb("sil_in", [P, KD * 2])
        mods = sb("mods", [P, DEPTH * 6 * KD * 2])
        mods_v = mods[:].rearrange("p (l w k s) -> p l w k s", l=DEPTH, w=6, k=KD)
        gains = sb("gains", [P, DEPTH * 4 * KD])
        gains_v = gains[:].rearrange("p (l w k) -> p l w k", l=DEPTH, w=4)
        ada_b = sb("ada_b", [P, DEPTH * 6 * KD])
        ada_b_v = ada_b[:].rearrange("p (l m) -> p l m", l=DEPTH)
        wuq = region(R_B, 2, NH * MQ)
        wukv = region(R_B + 2 * NH * MQ, NH * 2 * HD)
        wgate = region(R_B + 2 * NH * MQ + NH * 2 * HD, 2, P, parts=2 * GR)
        bgate = sb("bgate", [P, 2])
        qnorm = sb("qnorm", [P, 2])
        kvnorm = sb("kvnorm", [P, 1])
        lam_v = sb("lam_v", [P, 4 * DK])
        lam_p = sb("lam_p", [P, 2 * DK])
        lam_s = sb("lam_s", [P, 2])
        lam_e = sb("lam_e", [P, 2])
        neg_lam = sb("neg_lam", [P, 1])
        dec_in = sb("dec_in", [P, 10])
        dec_t = sb("dec_t", [P, 10])
        log_dec = sb("log_dec", [P, 10])
        mask = sb("mask", [CH, 2 * NH * CH])
        chunk_dec = sb("chunk_dec", [P, 2 * NC])
        dec_v = chunk_dec[:].rearrange("p (d c) -> p d c", d=2)
        edge = sb("edge", [P, 4 * CH])

        turn = {e: 0 for e in ("pe", "act", "dve", "pool", "sp")}

        def handover(who, eng):
            turn[who] += 1
            eng.drain().then_inc(sem("stage_done"), 1)
            eng.wait_ge(sem("stage_done"), 5 * turn[who])

        def first_token(layer, last_part):
            return CTX if last_part and layer == DEPTH - 1 else 0

        def spans(c0):
            return [(c, min(BANK, N - c)) for c in range(c0, N, BANK)]

        def streams(c0):
            return ([(1, 0, CTX)] if c0 == 0 else []) + [(0, CTX, N)]

        Y1 = R_A + KD * N
        X_AT = R_A + 2 * KD * N
        NORMS = [dict(y=None, pre=0, layer=0, c0=0)]
        for _l in range(DEPTH):
            NORMS.append(dict(y=Y1, gate=2, gain=1, pre=3, layer=_l, c0=first_token(_l, True)))
            NORMS.append(dict(y=R_H, gate=5, gain=3, pre=0 if _l < DEPTH - 1 else None, layer=_l,
                              c0=first_token(_l, True)))
        for _n in NORMS:
            _n["pre_layer"] = _n["layer"] + (_n.get("gate") == 5)
        sq_count = []
        rs_count = []
        _a = _b = 0
        for _n in NORMS:
            sq_count.append(_a)
            rs_count.append(_b)
            _a += KD * ((_n["y"] is not None) + (_n["pre"] is not None))
            _b += (_n["y"] is not None) + (_n["pre"] is not None)
        N_SQ, N_TMP, N_RS = R_A, R_A + 2 * N, R_A + 4 * N


        SCANS = ((0, CC), (CC, NC))

        def in_turn(x, d, a, b):
            if d == 0:
                return x[:, a:b]
            return x[:, b - 1:a - 1:-1] if a else x[:, b - 1::-1]

        _at = [R_H + 2 * IN_W]

        def take(*dims, parts=P):
            size = 1
            for d in dims:
                size *= d
            _at[0] += size
            return region(_at[0] - size, *dims, parts=parts)
        T_IN = [region(R_H + s * IN_W, IN_W) for s in range(2)]
        T_RD, T_RM, T_RR = take(16, DK), take(1, DK), take(8, DK)
        T_S = [(take(n, DK), take(n, DK)) for n in (16, 1, 8, NH)]
        T_QN, T_QNT, T_GT = take(3, P), take(3, P), take(P, parts=2 * GR)
        T_MQ, T_MK = take(NH, MQ), take(NH, MQ)
        T_SS = sb("ss", [P, 2])
        T_RS = sb("rs", [P, 2])
        assert _at[0] <= R_A

        E = [region(R_H + d * 4 * N, NC, 4, CH) for d in range(2)]
        KS, KDE, QD, QS = range(4)
        R_O = R_B
        RESET = region(R_B, N)
        R_T = R_B + NC * 256
        T1, T2, T3 = (region(R_T + i * N, N) for i in range(3))
        _at[0] = R_T
        R_V = R_T
        _at[0] += 4 * 256
        V = [[region(R_V + (2 * d + p) * 256, NH * HD, parts=CH) for p in range(2)] for d in range(2)]
        EST = [[take(3, CH) for p in range(2)] for d in range(2)]
        QBD = [[take(NH, CH) for p in range(2)] for d in range(2)]
        SCM = [take(NH, CH, parts=CH) for d in range(2)]
        UM = [take(NH, HD) for d in range(2)]
        STATE = [take(NH * HD) for d in range(2)]
        KDT = [take(P, parts=CH) for d in range(2)]

        _at[0] = R_H
        A_QD, A_QM = take(2, P), take(NH, P, parts=MQ)
        A_P = [take(N) for _ in range(2)]
        A_PT = [take(NT, P) for _ in range(2)]
        A_OUT = take(512)
        A_CM, A_NM, A_L, A_RL = take(3), take(MAPS), take(MAPS), take(MAPS)
        NSEG = len(spans(0))

        def att_loops(l):
            lat = 0 if l == 0 else CT * MAPS + (NT - CT) * MAPS * NSEG
            loops = [] if l else [(0, CT, 0, 0, CT)]
            return loops + [(CT, NT - CT, CT if l == 0 else NT, CT * MAPS if l == 0 else lat, NT)]

        _at[0] = R_A
        F_HM = [take(D) for _ in range(2)]
        F_SB = [take(512) for _ in range(2)]
        F_G = [take(512) for _ in range(2)]
        F_SQ, F_SG, F_OUTG = take(D), take(512), take(D)
        F_SS, F_RS = take(16), take(16)

        def fin_loop(l):
            return (0, NT, 0) if l == 0 else (CT, NT - CT, NT // 2)

        FREE = {
            "pe": dict(ada_made0=1, ada_made1=1, in_made1=10, turned1=2, made2=1, turned3=1, o_made0=2, o_made1=2,
                       u_made0=1, u_made1=1, scored=1, turned=2, pv_made=2, fin_turned0=1, fin_turned1=1, y_made0=1,
                       y_made1=1, up_made0=1, up_made1=1),
            "act": dict(in_kept0=2, qn_ready=2, kept12=1, mk_ready=1, kept7=1, kd_kept0=1, kd_kept1=1, o_kept0=1,
                        o_kept1=1, exp_done=1, pt_act=1, fin_kept_a0=1, fin_kept_a1=1, y_kept_a0=1, y_kept_a1=1,
                        silu_done=1, proj_out0=16, proj_out1=16),
            "dve": dict(ada_kept0=1, ada_kept1=1, in_kept1=2, roped=2, kept0=1, mq_ready=1, kept6=1, scm_ready0=1,
                        scm_ready1=1, pt_dve=1, att_kept=2, fin_kept_v0=1, fin_kept_v1=1, y_kept_v0=1, y_kept_v1=1,
                        up_done=2, fin_ready=1),
            "sp": dict(att_out=16),
        }

        def free(who, eng):
            for name, n in FREE[who].items():
                eng.sem_inc(sem(name), n)

        block = ctx.enter_context(nc.Block())

        @block.sync
        def _(sp):
            free("sp", sp)
            for dst, name in ((ident, "c_ident"), (rope, "c_rope"), (heads, "c_heads"), (causal, "c_causal"),
                              (rel, "c_rel"), (steps, "c_steps"), (sil_in, "cond")):
                sp.dma_start(dst[:], t[name]).then_inc(sem("const_in"), 16)

            for dst, name in ((gains, "norm_g"), (ada_b, "ada_b")):
                sp.dma_start(dst[:], t[name]).then_inc(sem("const_in"), 16)

            def modulation(l):
                with sp.Fori(0, ADA_CHUNKS // 2) as u:
                    for s in range(2):
                        sp.wait_ge(sem(f"ada_made{s}"), l * (ADA_CHUNKS // 2) + u + 1)
                        sp.dma_start(region(R_A + s * KD * ADA_M * P, KD * ADA_M * P),
                                     t["ada_w"][l, 2 * u + s]).then_inc(sem(f"ada_in{s}"), 16)
                handover("sp", sp)

            def small(l):
                for dst, src in ((wuq, t["w_uq"][l]), (wukv, t["w_ukv"][l]), (bgate[:], t["b_gate"][l]),
                                 (qnorm[:], t["q_norm"][l]), (kvnorm[:], t["kv_norm"][l]),
                                 (dec_in[:, 8:10], t["decay_col"][l]), (lam_v[:], t["lam"][l].partition_broadcast(P)),
                                 (dec_in[:, 0:8], t["decay"][l].partition_broadcast(P))):
                    sp.dma_start(dst, src).then_inc(sem("small_in"), 16)
                sp.wait_ge(sem("wgate_zero"), l + 1)
                for d in range(2):
                    sp.dma_start(wgate[d * GR:(d + 1) * GR, d, :], t["w_gate"][l, :, d, :]).then_inc(sem("small_in"), 16)

            def norm(i):
                n = NORMS[i]
                c0 = n["c0"]
                src = t["x"] if i <= 1 else xdram
                for k in range(KD):
                    sp.dma_start(region(X_AT, KD, N)[:, k, c0:N], src[:, k, c0:N]).then_inc(sem(f"x_in{k}"), 16)
                if n["y"] is not None:
                    last = n["pre"] is None
                    for k in range(KD):
                        sp.wait_ge(sem("x_new"), (i - 1) * KD + k + 1)
                        xk = region(X_AT, KD, N)[:, k, c0:N]
                        dst = t["out"][:, k, :] if last else xdram[:, k, c0:N]
                        sp.dma_start(dst, xk).then_inc(sem("x_out"), 16)
                    sp.wait_ge(sem("x_out"), 16 * KD * i)
                handover("sp", sp)

            def project(l):
                small(l)
                with sp.Fori(0, IN_CHUNKS // 2) as u:
                    for s in range(2):
                        sp.wait_ge(sem("in_made1"), l * 40 + u * 10 + 5 * (s + 1))
                        sp.dma_start(region(R_A + s * KD * IN_C, KD * IN_C),
                                     t["w_in"][l, 2 * u + s]).then_inc(sem(f"win_in{s}"), 16)
                handover("sp", sp)

            def prepare(l):
                sp.dma_start(region(R_VD, NT, 256), proj.rearrange("(t p) c -> p t c", p=P)[:, :, COL["dv"]:COL["dv"] + 256]
                             ).then_inc(sem("vd_in"), 16)
                with sp.Fori(0, NT // 2) as u:
                    for s in range(2):
                        for read in ("roped", "qn_ready", "turned1"):
                            sp.wait_ge(sem(read), l * NT + 2 * u + s + 1)
                        sp.dma_start(region(R_H + s * IN_W, IN_W), proj.rearrange("(t p) c -> p t c", p=P)[:, 2 * u + s, :]
                                     ).then_inc(sem(f"tile_in{s}"), 16)
                sp.wait_ge(sem("vd_in"), 16 * (l + 1))
                handover("sp", sp)

            def scan(l, g):
                inst = 2 * l + g
                col = COL["rv" if g else "gv"]
                for a, b in SCANS:
                    with sp.Fori(0, (b - a) // 2) as pair:
                        i = a + 2 * pair
                        for p in range(2):
                            for d in range(2):
                                sp.wait_ge(sem(f"o_made{d}"), inst * NC + i + p + 1)
                                sp.dma_start(region(R_V + (2 * d + p) * 256, 256, parts=CH),
                                             in_turn(proj.rearrange("(c p) f -> p c f", p=CH)[:, :, col:col + 256], d, a, b)[:, 2 * pair + p, :]
                                             ).then_inc(sem(f"v_in{d}{p}"), 16)
                for d in range(2):
                    sp.wait_ge(sem(f"o_kept{d}"), (inst + 1) * NC + 1)
                    sp.dma_start(scans[d].rearrange("(c p) f -> p c f", p=CH)[:, :, g * 256:(g + 1) * 256],
                                 region(R_O, NC, 256)[d * CH:(d + 1) * CH]).then_inc(sem("o_out"), 16)
                sp.wait_ge(sem("o_out"), 32 * (inst + 1))
                handover("sp", sp)

            def attend(l):
                for first, count, base, _, _ in att_loops(l):
                    with sp.Fori(0, count) as i:
                        sp.wait_ge(sem("att_kept"), (base + i) * MAPS + MAPS + 2)
                        sp.dma_start(att.rearrange("(t p) c -> p t c", p=P)[:, first + i, :], A_OUT
                                     ).then_inc(sem("att_out"), 16)
                    sp.wait_ge(sem("att_out"), 16 * (base + count) + 16)
                handover("sp", sp)

            def finish(l):
                c0, count, base = fin_loop(l)
                sp.dma_start(F_OUTG, t["out_g"][l].partition_broadcast(P)).then_inc(sem("outg_in"), 16)
                with sp.Fori(0, count // 2) as u:
                    for s in range(2):
                        sp.wait_ge(sem(f"fin_turned{s}"), base + u + 1)
                        tok = c0 + 2 * u + s

                        def rows(a):
                            return a.rearrange("(t p) c -> p t c", p=P)[:, tok, :]
                        for dst, src in ((F_HM[s][:, 0:512], rows(att)), (F_HM[s][:, 512:1024], rows(scans[0])),
                                         (F_SB[s], rows(scans[1])),
                                         (F_G[s][:, 0:256], rows(proj)[:, COL["gr"]:COL["gr"] + 256]),
                                         (F_G[s][:, 256:512], rows(proj)[:, COL["rg"]:COL["rg"] + 256])):
                            sp.dma_start(dst, src).then_inc(sem(f"fin_in{s}"), 16)
                handover("sp", sp)

            def columns(l, j):
                kk, w_at = (KD, R_A) if j == 0 else (KH, R_B)
                w = t["w_out"] if j == 0 else t["ffn_out"]
                with sp.Fori(0, KD // 2) as u:
                    for s in range(2):
                        sp.wait_ge(sem(f"y_made{s}"), (2 * l + j) * (KD // 2) + u + 1)
                        sp.dma_start(region(w_at + s * kk * P, kk * P), w[l, 2 * u + s]).then_inc(sem(f"wy_in{s}"), 16)
                handover("sp", sp)

            def hidden(l):
                with sp.Fori(0, KH // 2) as u:
                    for s in range(2):
                        sp.wait_ge(sem(f"up_made{s}"), l * (KH // 2) + u + 1)
                        sp.dma_start(region(R_B + s * KD * 2 * P, KD * 2 * P), t["ffn_in"][l, 2 * u + s]
                                     ).then_inc(sem(f"wgu_in{s}"), 16)
                handover("sp", sp)

            for l in range(DEPTH):
                modulation(l)
            norm(0)
            for l in range(DEPTH):
                project(l)
                prepare(l)
                for g in range(2):
                    handover("sp", sp)
                    scan(l, g)
                attend(l)
                finish(l)
                columns(l, 0)
                norm(2 * l + 1)
                hidden(l)
                columns(l, 1)
                norm(2 * l + 2)

        @block.tensor
        def _(pe):
            mm = nc.tensor.matmul
            free("pe", pe)
            pe.wait_ge(sem("const_in"), 16 * 9)
            pe.wait_ge(sem("const_set"), 1)

            def modulation(l):
                if l == 0:
                    pe.wait_ge(sem("sil_ready"), 1)
                with pe.Fori(0, ADA_CHUNKS // 2) as u:
                    for s in range(2):
                        w = region(R_A + s * KD * ADA_M * P, KD, ADA_M * P)
                        pe.wait_ge(sem(f"ada_in{s}"), 16 * (l * (ADA_CHUNKS // 2) + u + 1))
                        pe.wait_ge(sem(f"ada_kept{s}"), l * (ADA_CHUNKS // 2) + u + 1)
                        for m in range(ADA_M):
                            for k in range(KD):
                                last = mm(bank(s, 2 * ADA_M)[:, 2 * m:2 * m + 2], w[:, k, m * P:(m + 1) * P],
                                          sil[:, 2 * k:2 * k + 2], start=(k == 0), stop=(k == KD - 1))
                        last.then_inc(sem(f"ada_made{s}"), 1)
                handover("pe", pe)

            def norm(i):
                n = NORMS[i]
                c0 = n["c0"]
                for pas in range((n["y"] is not None) + (n["pre"] is not None)):
                    if pas:
                        pe.wait_ge(sem("rstd_ready"), rs_count[i] + pas)
                    for k in range(KD):
                        at = sq_count[i] + pas * KD + k
                        pe.wait_ge(sem("sq_ready"), at + 1)
                        for c, w in spans(c0):
                            last = mm(psum[:, c - c0:c - c0 + w], ones[:], region(N_SQ, 2, N)[:, k % 2, c:c + w],
                                      start=(k == 0), stop=(k == KD - 1))
                        last.then_inc(sem("sq_read"), 1)
                handover("pe", pe)

            def project(l):
                h = region(R_H, KD, N)
                with pe.Fori(0, IN_CHUNKS // 2) as u:
                    for s in range(2):
                        w = region(R_A + s * KD * IN_C, KD, IN_C)
                        pe.wait_ge(sem(f"win_in{s}"), 16 * (l * (IN_CHUNKS // 2) + u + 1))
                        for tt in range(NT):
                            n, par = 5 * s + tt // 2, tt % 2
                            pe.wait_ge(sem(f"in_kept{par}"), l * 40 + u * 10 + n + 1)
                            for k in range(KD):
                                last = mm(bank(2 * par + n % 2, IN_C), h[:, k, tt * P:(tt + 1) * P], w[:, k, :],
                                          start=(k == 0), stop=(k == KD - 1))
                            last.then_inc(sem(f"in_made{par}"), 1)
                handover("pe", pe)

            def prepare(l):
                pe.wait_ge(sem("small_in"), 160 * (l + 1))
                with pe.Fori(0, NT // 2) as u:
                    for s in range(2):
                        T = l * NT + 2 * u + s
                        tile = T_IN[s]
                        pe.wait_ge(sem(f"tile_in{s}"), 16 * (l * (NT // 2) + u + 1))
                        pe.wait_ge(sem("roped"), T + 3)
                        pe.wait_ge(sem("qn_ready"), T + 3)
                        pe.wait_ge(sem("kept0"), T + 1)
                        pe.wait_ge(sem("kept12"), T + 1)
                        rd = T_RD.rearrange("p (j h) d -> p j (h d)", j=4)
                        rr = T_RR.rearrange("p (j h) d -> p j (h d)", j=2)
                        for j in range(4):
                            nc.tensor.transpose(bank(0)[:, j * P:(j + 1) * P], rd[:, j, :], ident[:])
                        gsrc = [tile[:, COL["gq"]:COL["gq"] + P], tile[:, COL["gk"]:COL["gk"] + P], rr[:, 0, :], rr[:, 1, :]]
                        for j in range(4):
                            nc.tensor.transpose(bank(1)[:, j * P:(j + 1) * P], gsrc[j], ident[:])
                        for j in range(3):
                            nc.tensor.transpose(bank(2)[:, j * P:(j + 1) * P], T_QN[:, j, :], ident[:])
                        nc.tensor.transpose(bank(2)[0:2 * GR, 3 * P:4 * P], tile[:, COL["gf"]:COL["gf"] + 2 * GR], ident[:]
                                            ).then_inc(sem("turned1"), 1)
                        pe.wait_ge(sem("kept12"), T + 2)
                        pe.wait_ge(sem("mq_ready"), T + 1)
                        pe.wait_ge(sem("mk_ready"), T + 1)
                        for k in range(2):
                            mm(bank(3, NH * MQ), T_QNT[:, k, :], wuq[:, k, :], start=(k == 0), stop=(k == 1))
                        mm(bank(4), T_QNT[:, 2, :], wukv, start=True, stop=True)
                        for d in range(2):
                            last = mm(bank(5)[:, d * P:(d + 1) * P], wgate[:, d, :], T_GT, start=True, stop=True)
                        last.then_inc(sem("made2"), 1)
                        pe.wait_ge(sem("mq_ready"), T + 2)
                        pe.wait_ge(sem("mk_ready"), T + 2)
                        pe.wait_ge(sem("kept6"), T + 1)
                        pe.wait_ge(sem("kept7"), T + 1)
                        for b, src in ((6, T_MQ), (7, T_MK)):
                            for h in range(NH):
                                last = nc.tensor.transpose(bank(b)[0:MQ, h * P:(h + 1) * P], src[:, h, :], ident[:])
                        last.then_inc(sem("turned3"), 1)
                handover("pe", pe)

            def scan(l, g):
                inst = 2 * l + g
                for a, b in SCANS:
                    with pe.Fori(0, (b - a) // 2) as pair:
                        i = a + 2 * pair
                        for p in range(2):
                            n = inst * NC + i + p
                            for d in range(2):
                                pe.wait_ge(sem(f"est_ready{d}"), n + 1)
                                pe.wait_ge(sem(f"scm_ready{d}"), n + 1)
                                mm(bank(d, NH * CH, CH), EST[d][p][:, KS, :], QBD[d][p].rearrange("p h i -> p (h i)"),
                                   start=True, stop=True).then_inc(sem(f"sc_made{d}"), 1)
                                pe.wait_ge(sem(f"kd_kept{d}"), n + 1)
                                nc.tensor.transpose(bank(2 + d, P), EST[d][p][:, KDE:QD + 1, :].rearrange("p a b -> p (a b)"), ident[:]
                                                    ).then_inc(sem(f"kd_turned{d}"), 1)
                            for d in range(2):
                                pe.wait_ge(sem(f"state_ready{d}"), n + inst + 1)
                                pe.wait_ge(sem(f"o_kept{d}"), n + 1)
                                mm(bank(4 + d, NH * HD, CH), EST[d][p][:, QD, :], STATE[d], start=True, stop=False,
                                   skip_group_check=True)
                            for d in range(2):
                                pe.wait_ge(sem(f"v_in{d}{p}"), 16 * (inst * (NC // 2) + a // 2 + pair + 1))
                                pe.wait_ge(sem(f"kd_kept{d}"), n + 2)
                                pe.wait_ge(sem(f"scm_ready{d}"), n + 2)
                                mm(bank(6 + d, NH * HD), KDT[d], V[d][p], start=True, stop=True
                                   ).then_inc(sem(f"u_made{d}"), 1)
                            for d in range(2):
                                for h in range(NH):
                                    last = mm(bank(4 + d, NH * HD, CH)[:, h * HD:(h + 1) * HD], SCM[d][:, h, :],
                                              V[d][p][:, h * HD:(h + 1) * HD], start=False, stop=(h == NH - 1),
                                              skip_group_check=True)
                                last.then_inc(sem(f"o_made{d}"), 1)
                handover("pe", pe)

            def attend(l):
                for first, count, base, segs, nk in att_loops(l):
                    pieces = spans(0) if nk == NT else [(0, CTX)]
                    with pe.Fori(0, count) as i:
                        M0 = (base + i) * MAPS

                        def scores(m):
                            if m == 0:
                                pe.wait_ge(sem("q_staged"), base + i + 1)
                            pe.wait_ge(sem("exp_done"), M0 + m + 1)
                            if m < 2 * NH:
                                at = DK * (m % 4)
                                q, k = A_QD[at:at + DK, m // 4, :], region(R_QKD, 4, N)[at:at + DK, 2 + m // 4, :]
                            else:
                                q, k = A_QM[:, m - 8, :], region(R_KM, 4, N, parts=MQ)[:, m - 8, :]
                            for c, w in pieces:
                                mm(psum[:, c:c + w], q, k[:, c:c + w], start=True, stop=True,
                                   ).then_inc(sem("scored"), 1)

                        def turn_probs(m):
                            pe.wait_ge(sem("exp_done"), M0 + m + 2)
                            pe.wait_ge(sem("pt_act"), M0 + m + 1)
                            pe.wait_ge(sem("pt_dve"), M0 + m + 1)
                            for kt in range(nk):
                                b, j = (3 + kt // 4, kt % 4) if nk == NT else (3 + kt, 0)
                                last = nc.tensor.transpose(bank(b)[:, j * P:(j + 1) * P],
                                                           A_P[m % 2][:, kt * P:(kt + 1) * P], ident[:])
                            last.then_inc(sem("turned"), 1)

                        def values(m):
                            pe.wait_ge(sem("pt_act"), M0 + m + 2)
                            pe.wait_ge(sem("pt_dve"), M0 + m + 2)
                            pe.wait_ge(sem("att_kept"), M0 + m + 1)
                            v = region(R_VD if m < 8 else R_VM, NT, 256)
                            h = m // 2 if m < 8 else m - 8
                            for kt in range(nk):
                                last = mm(bank(6 + m % 2, HD), A_PT[m % 2][:, kt, :], v[:, kt, h * HD:(h + 1) * HD],
                                          start=(kt == 0), stop=(kt == nk - 1))
                            last.then_inc(sem("pv_made"), 1)

                        for m in range(MAPS + 2):
                            if m < MAPS:
                                scores(m)
                            if 1 <= m <= MAPS:
                                turn_probs(m - 1)
                            if m >= 2:
                                values(m - 2)
                handover("pe", pe)

            def finish(l):
                c0, count, base = fin_loop(l)
                with pe.Fori(0, count // 2) as u:
                    for s in range(2):
                        pe.wait_ge(sem("fin_ready"), 2 * base + 2 * u + s + 2)
                        pe.wait_ge(sem(f"fin_kept_a{s}"), base + u + 1)
                        pe.wait_ge(sem(f"fin_kept_v{s}"), base + u + 1)
                        for k in range(KD):
                            last = nc.tensor.transpose(bank(2 * s + k // 4)[:, (k % 4) * P:(k % 4 + 1) * P],
                                                       F_HM[s][:, k * P:(k + 1) * P], ident[:])
                        last.then_inc(sem(f"fin_turned{s}"), 1)
                handover("pe", pe)

            def columns(l, j):
                kk, w_at, src_at = (KD, R_A, R_H) if j == 0 else (KH, R_B, R_A)
                src = region(src_at, kk, N)
                c0 = first_token(l, True)
                with pe.Fori(0, KD // 2) as u:
                    for s in range(2):
                        c = (2 * l + j) * (KD // 2) + u
                        w = region(w_at + s * kk * P, kk, P)
                        pe.wait_ge(sem(f"wy_in{s}"), 16 * (c + 1))
                        pe.wait_ge(sem(f"y_kept_a{s}"), c + 1)
                        pe.wait_ge(sem(f"y_kept_v{s}"), c + 1)
                        for a, n in spans(c0):
                            for k in range(kk):
                                last = mm(psum[:, 3 * s * BANK + a - c0:3 * s * BANK + a - c0 + n], w[:, k, :],
                                          src[:, k, a:a + n], start=(k == 0), stop=(k == kk - 1))
                        last.then_inc(sem(f"y_made{s}"), 1)
                handover("pe", pe)

            def hidden(l):
                h = region(R_H, KD, N)
                c0 = first_token(l, True)
                with pe.Fori(0, KH // 2) as u:
                    for s in range(2):
                        w = region(R_B + s * KD * 2 * P, KD, 2, P)
                        n = l * KH + 2 * u + s
                        pe.wait_ge(sem(f"wgu_in{s}"), 16 * (l * (KH // 2) + u + 1))
                        for half in range(2):
                            pe.wait_ge(sem("up_done" if half else "silu_done"), n + (2 if half else 1))
                            for a, c in spans(c0):
                                for k in range(KD):
                                    last = mm(psum[:, 3 * half * BANK + a - c0:3 * half * BANK + a - c0 + c],
                                              w[:, k, half, :], h[:, k, a:a + c], start=(k == 0), stop=(k == KD - 1))
                            last.then_inc(sem(f"up_made{s}" if half else "gate_made"), 1)
                handover("pe", pe)

            for l in range(DEPTH):
                modulation(l)
            norm(0)
            for l in range(DEPTH):
                project(l)
                prepare(l)
                for g in range(2):
                    handover("pe", pe)
                    scan(l, g)
                attend(l)
                finish(l)
                columns(l, 0)
                norm(2 * l + 1)
                hidden(l)
                columns(l, 1)
                norm(2 * l + 2)

        @block.scalar
        def _(act):
            activation = nc.scalar.activation
            free("act", act)
            act.wait_ge(sem("const_in"), 16 * 9)
            act.wait_ge(sem("const_set"), 1)
            activation(sil[:], sil_in[:], ACT.Silu).then_inc(sem("sil_ready"), 1)

            def modulation(l):
                handover("act", act)

            def norm(i):
                n = NORMS[i]
                c0 = n["c0"]
                at, rs = sq_count[i], rs_count[i]
                for pas, (src_at, last) in enumerate(([(n["y"], False)] if n["y"] is not None else []) +
                                                     ([(X_AT, True)] if n["pre"] is not None else [])):
                    for k in range(KD):
                        if src_at == X_AT:
                            if n["y"] is None:
                                act.wait_ge(sem(f"x_in{k}"), 16 * (i + 1))
                            else:
                                act.wait_ge(sem("x_new"), (i - 1) * KD + k + 1)
                        if k >= 2 or pas:
                            act.wait_ge(sem("sq_read"), at + pas * KD + k - 1)
                        activation(region(N_SQ, 2, N)[:, k % 2, c0:N], region(src_at, KD, N)[:, k, c0:N], ACT.Square
                                   ).then_inc(sem("sq_ready"), 1)
                    act.wait_ge(sem("sq_read"), at + pas * KD + KD)
                    r = region(N_RS + pas * N, N)
                    activation(r[:, c0:N], psum[:, 0:N - c0], ACT.Ln, scale=1.0 / D, bias=eps[:, 0:1])
                    act.drain()
                    activation(r[:, c0:N], r[:, c0:N], ACT.Exp, scale=-0.5).then_inc(sem("rstd_ready"), 1)
                if n["pre"] is not None:
                    for k in range(KD):
                        act.wait_ge(sem("h_normed"), KD * i + k + 1)
                        hk = region(R_H, KD, N)[:, k, :]
                        for st, a, b in streams(c0):
                            m = mods_v[:, n["pre_layer"]]
                            activation(hk[:, a:b], hk[:, a:b], ACT.Identity, scale=m[:, n["pre"] + 1, k, st:st + 1],
                                       bias=m[:, n["pre"], k, st:st + 1])
                handover("act", act)

            def project(l):
                with act.Fori(0, IN_CHUNKS // 2) as u:
                    for s in range(2):
                        act.wait_ge(sem(f"proj_out{s}"), 16 * (l * 4 + u + 1))
                        for j in range(5):
                            n = 5 * s + j
                            act.wait_ge(sem("in_made0"), l * 40 + u * 10 + n + 1)
                            nc.scalar.copy(region(R_A + 2 * KD * IN_C + s * NT * IN_C, NT, IN_C)[:, 2 * j, :],
                                           bank(n % 2, IN_C)).then_inc(sem("in_kept0"), 1)
                        for par in range(2):
                            act.wait_ge(sem(f"in_kept{par}"), l * 40 + u * 10 + 5 * (s + 1) + 2)
                        act.dma_start(proj.rearrange("(t p) (c w) -> p t c w", p=P, w=IN_C)[:, :, 2 * u + s, :],
                                      region(R_A + 2 * KD * IN_C + s * NT * IN_C, NT, IN_C)
                                      ).then_inc(sem(f"proj_out{s}"), 16)
                for s in range(2):
                    act.wait_ge(sem(f"proj_out{s}"), 16 * (4 * (l + 1) + 1))
                handover("act", act)

            def prepare(l):
                act.wait_ge(sem("small_in"), 160 * (l + 1))
                act.wait_ge(sem("dec_abs"), l + 1)
                activation(dec_t[:], dec_t[:], ACT.Exp, scale=-1.0)
                act.drain()
                activation(dec_t[:], dec_t[:], ACT.Ln, bias=1.0)
                activation(lam_e[:], lam_s[:], ACT.Exp).then_inc(sem("dec_ln"), 1)
                with act.Fori(0, NT // 2) as u:
                    for s in range(2):
                        T = l * NT + 2 * u + s
                        tok = 2 * u + s
                        tile = T_IN[s]
                        mq, mkv = tile[:, COL["mq"]:COL["mq"] + QR], tile[:, COL["mkv"]:COL["mkv"] + KVR]
                        qn = T_QN.rearrange("p j d -> p (j d)")
                        act.wait_ge(sem(f"tile_in{s}"), 16 * (l * (NT // 2) + u + 1))
                        act.wait_ge(sem("turned1"), T + 2)
                        activation(qn[:, 0:QR], mq, ACT.Square, accum_out=T_SS[:, 0:1])
                        activation(qn[:, QR:QR + KVR], mkv, ACT.Square, accum_out=T_SS[:, 1:2])
                        act.drain()
                        activation(T_RS[:, 0:1], T_SS[:, 0:1], ACT.Ln, scale=1.0 / QR, bias=eps[:, 0:1])
                        activation(T_RS[:, 1:2], T_SS[:, 1:2], ACT.Ln, scale=1.0 / KVR, bias=eps[:, 0:1])
                        act.drain()
                        activation(T_RS[:], T_RS[:], ACT.Exp, scale=-0.5)
                        act.drain()
                        nc.scalar.mul(qn[:, 0:QR], mq, T_RS[:, 0:1])
                        nc.scalar.mul(qn[:, QR:QR + KVR], mkv, T_RS[:, 1:2]).then_inc(sem("qn_ready"), 1)

                        act.wait_ge(sem("turned1"), T + 3)
                        nc.scalar.copy(region(R_GR, 4, NT, P)[:, :, tok, :], bank(1).rearrange("p (j c) -> p j c", j=4))
                        act.wait_ge(sem("made2"), T + 1)
                        for j in range(2):
                            nc.scalar.mul(T_QNT[:, j, :], bank(2)[:, j * P:(j + 1) * P], qnorm[:, j:j + 1])
                        nc.scalar.mul(T_QNT[:, 2, :], bank(2)[:, 2 * P:3 * P], kvnorm[:, 0:1])
                        nc.scalar.copy(T_GT, bank(2)[0:2 * GR, 3 * P:4 * P]).then_inc(sem("kept12"), 1)

                        act.wait_ge(sem("made2"), T + 2)
                        act.wait_ge(sem("turned3"), T + 1)
                        kv = bank(4).rearrange("p (h d) -> p h d", h=NH)
                        nc.scalar.copy(T_MK[:, :, 0:HD], kv[:, :, 0:HD])
                        nc.scalar.copy(region(R_VM, NT, NH, HD)[:, tok, :, :], kv[:, :, HD:2 * HD])
                        for d in range(2):
                            last = activation(region(R_GZ, 2, NT, P)[:, d, tok, :], bank(5)[:, d * P:(d + 1) * P],
                                              ACT.Identity, bias=bgate[:, d:d + 1])
                        last.then_inc(sem("mk_ready"), 1)

                        act.wait_ge(sem("turned3"), T + 2)
                        nc.scalar.copy(region(R_KM, 4, NT, P, parts=MQ)[:, :, tok, :],
                                       bank(7, parts=MQ).rearrange("p (j c) -> p j c", j=4)).then_inc(sem("kept7"), 1)
                handover("act", act)

            def scan_factors(l, g):
                if g == 0:
                    act.wait_ge(sem("gate_abs"), l + 1)
                    a, b = region(R_H, 2 * N), region(R_H + 2 * N, 2 * N)
                    activation(b, a, ACT.Exp, scale=-1.0)
                    act.drain()
                    activation(b, b, ACT.Ln, bias=1.0).then_inc(sem("gate_ln"), 1)
                    for d in range(2):
                        act.wait_ge(sem("exponents"), 2 * l + d + 1)
                        sign = 1.0 if d == 0 else -1.0
                        x1, x2, x3 = (x.rearrange("p (c i) -> p c i", c=NC) for x in (T1, T2, T3))
                        activation(E[d][:, :, QS, :], x2, ACT.Exp, scale=sign)
                        activation(E[d][:, :, KS, :], x2, ACT.Exp, scale=-sign)
                        if d == 0:
                            activation(E[d][:, :, QD, :], x1, ACT.Exp)
                            activation(E[d][:, :, KDE, :], x3, ACT.Exp, scale=-1.0)
                        else:
                            activation(E[d][:, :, QD, :], x3, ACT.Exp, scale=-1.0)
                            activation(E[d][:, :, KDE, :], region(R_GZ, 2, NC, CH)[:, 1], ACT.Exp)
                        activation(dec_v[:, d, :], x1[:, :, CH - 1], ACT.Exp).then_inc(sem("factors"), 1)
                else:
                    act.wait_ge(sem("log_dec_ready"), l + 1)
                    for d in range(2):
                        for h in range(NH):
                            activation(mask[:, (d * NH + h) * CH:(d * NH + h + 1) * CH], rel[:, d * CH:(d + 1) * CH],
                                       ACT.Exp, scale=log_dec[0:CH, d * NH + h:d * NH + h + 1])
                        activation(edge[:, 2 * d * CH:2 * (d + 1) * CH], steps[:, 2 * d * CH:2 * (d + 1) * CH], ACT.Exp,
                                   scale=log_dec[:, 8 + d:9 + d])
                        last = activation(dec_v[:, d, :], log_dec[:, 8 + d:9 + d].to_broadcast([P, NC]), ACT.Exp,
                                          scale=float(CH))
                    last.then_inc(sem("ret_factors"), 1)
                handover("act", act)

            def scan(l, g):
                inst = 2 * l + g
                for a, b in SCANS:
                    with act.Fori(0, (b - a) // 2) as pair:
                        i = a + 2 * pair
                        for p in range(2):
                            n = inst * NC + i + p
                            for d in range(2):
                                act.wait_ge(sem(f"kd_turned{d}"), n + 1)
                                act.wait_ge(sem(f"u_made{d}"), n + 1)
                                nc.scalar.copy(KDT[d], bank(2 + d, P, CH)).then_inc(sem(f"kd_kept{d}"), 1)
                            for d in range(2):
                                act.wait_ge(sem(f"o_made{d}"), n + 3)
                                nc.scalar.copy(in_turn(region(R_O, NC, 256)[d * CH:(d + 1) * CH], d, a, b)[:, 2 * pair + p, :], bank(4 + d, 256, CH)
                                               ).then_inc(sem(f"o_kept{d}"), 1)
                handover("act", act)

            def attend(l):
                for first, count, base, segs, nk in att_loops(l):
                    keys = nk * P
                    with act.Fori(0, count) as i:
                        M0 = (base + i) * MAPS
                        for m in range(MAPS + 1):
                            if m < MAPS:
                                act.wait_ge(sem("max_ready"), M0 + m + 1)
                                act.wait_ge(sem("turned"), M0 + m + 1)
                                activation(A_P[m % 2][:, 0:keys], psum[:, 0:keys], ACT.Exp, bias=A_NM[:, m:m + 1],
                                           accum_out=A_L[:, m:m + 1]).then_inc(sem("exp_done"), 1)
                            if m >= 1:
                                act.wait_ge(sem("turned"), M0 + m - 1 + 3)
                                act.wait_ge(sem("pv_made"), M0 + m - 1 + 1)
                                w = 4 if nk == NT else 1
                                nc.scalar.copy(A_PT[(m - 1) % 2][:, 0:w, :].rearrange("p a b -> p (a b)"),
                                               bank(3, w * P)).then_inc(sem("pt_act"), 1)
                handover("act", act)

            def finish(l):
                c0, count, base = fin_loop(l)
                with act.Fori(0, count // 2) as u:
                    for s in range(2):
                        T = 2 * base + 2 * u + s
                        tok = c0 + 2 * u + s
                        act.wait_ge(sem("fin_sum"), T + 1)
                        act.wait_ge(sem("fin_ready"), T + 1)
                        activation(F_SQ, F_HM[s], ACT.Square).then_inc(sem("fin_sq"), 1)
                        activation(F_SG, F_G[s], ACT.Silu)
                        act.wait_ge(sem("fin_ss"), T + 1)
                        activation(F_RS, F_SS, ACT.Ln, scale=1.0 / HD, bias=eps[:, 0:1])
                        act.drain()
                        activation(F_RS, F_RS, ACT.Exp, scale=-0.5).then_inc(sem("fin_rs"), 1)
                        act.wait_ge(sem(f"fin_turned{s}"), base + u + 2)
                        nc.scalar.copy(region(R_H, KD, NT, P)[:, 0:4, tok, :],
                                       bank(2 * s).rearrange("p (j c) -> p j c", j=4)).then_inc(sem(f"fin_kept_a{s}"), 1)
                handover("act", act)

            def columns(l, j):
                c0 = first_token(l, True)
                dst = region(Y1 if j == 0 else R_H, KD, N)
                with act.Fori(0, KD // 2) as u:
                    for s in range(2):
                        act.wait_ge(sem(f"y_made{s}"), (2 * l + j) * (KD // 2) + u + 2)
                        for q, (a, n) in enumerate(spans(c0)):
                            if q != 1:
                                last = nc.scalar.copy(dst[:, 2 * u + s, a:a + n],
                                                      psum[:, 3 * s * BANK + a - c0:3 * s * BANK + a - c0 + n])
                        last.then_inc(sem(f"y_kept_a{s}"), 1)
                handover("act", act)

            def hidden(l):
                c0 = first_token(l, True)
                with act.Fori(0, KH // 2) as u:
                    for s in range(2):
                        n = l * KH + 2 * u + s
                        act.wait_ge(sem("gate_made"), n + 1)
                        act.wait_ge(sem("up_done"), n + 1)
                        activation(region(R_B + 4 * KD * P + s * N, N)[:, c0:N], psum[:, 0:N - c0], ACT.Silu
                                   ).then_inc(sem("silu_done"), 1)
                handover("act", act)

            for l in range(DEPTH):
                modulation(l)
            norm(0)
            for l in range(DEPTH):
                project(l)
                prepare(l)
                for g in range(2):
                    scan_factors(l, g)
                    scan(l, g)
                attend(l)
                finish(l)
                columns(l, 0)
                norm(2 * l + 1)
                hidden(l)
                columns(l, 1)
                norm(2 * l + 2)

        @block.vector
        def _(dve):
            v = nc.vector
            free("dve", dve)
            v.memset(eps[:], EPS)
            v.memset(ones[:], 1.0).then_inc(sem("const_set"), 1)
            dve.wait_ge(sem("const_in"), 16 * 9)

            def modulation(l):
                with dve.Fori(0, ADA_CHUNKS // 2) as u:
                    for s in range(2):
                        dve.wait_ge(sem(f"ada_made{s}"), l * (ADA_CHUNKS // 2) + u + 2)
                        ch = 2 * u + s
                        out = mods_v[:, l].rearrange("p w k s -> p (w k) s").rearrange("p (c m) s -> p c m s", m=ADA_M)
                        bias = ada_b_v[:, l, :].rearrange("p (c m) -> p c m", m=ADA_M)
                        v.tensor_tensor(out[:, ch, :, :], bank(s, 2 * ADA_M).rearrange("p (m s) -> p m s", s=2),
                                        bias[:, ch, :].unsqueeze(2).to_broadcast([P, ADA_M, 2]), ALU.add
                                        ).then_inc(sem(f"ada_kept{s}"), 1)
                dve.drain()
                for st in range(2):
                    for row, gain in ((1, 0), (4, 2)):
                        m = mods_v[:, l, row, :, st]
                        v.scalar_tensor_tensor(out=m, in0=m, scalar=1.0, in1=gains_v[:, l, gain, :], op0=ALU.add, op1=ALU.mult)
                    for row, gain in ((2, 1), (5, 3)):
                        m = mods_v[:, l, row, :, st]
                        v.tensor_tensor(m, m, gains_v[:, l, gain, :], ALU.mult)
                handover("dve", dve)

            def norm(i):
                n = NORMS[i]
                c0 = n["c0"]
                x, h = region(X_AT, KD, N), region(R_H, KD, N)
                if n["y"] is not None:
                    y, r = region(n["y"], KD, N), region(N_RS, N)
                    dve.wait_ge(sem("rstd_ready"), rs_count[i] + 1)
                    for k in range(KD):
                        tmp = region(N_TMP, 2, N)[:, k % 2, :]
                        v.tensor_tensor(tmp[:, c0:N], y[:, k, c0:N], r[:, c0:N], ALU.mult)
                        dve.wait_ge(sem(f"x_in{k}"), 16 * (i + 1))
                        dve.drain()
                        for st, a, b in streams(c0):
                            last = v.scalar_tensor_tensor(out=x[:, k, a:b], in0=tmp[:, a:b],
                                                          scalar=mods_v[:, n["layer"], n["gate"], k, st:st + 1],
                                                          in1=x[:, k, a:b], op0=ALU.mult, op1=ALU.add)
                        last.then_inc(sem("x_new"), 1)
                if n["pre"] is not None:
                    pas = int(n["y"] is not None)
                    r = region(N_RS + pas * N, N)
                    dve.wait_ge(sem("rstd_ready"), rs_count[i] + pas + 1)
                    for k in range(KD):
                        dve.wait_ge(sem(f"x_in{k}"), 16 * (i + 1))
                        v.tensor_tensor(h[:, k, c0:N], x[:, k, c0:N], r[:, c0:N], ALU.mult).then_inc(sem("h_normed"), 1)
                handover("dve", dve)

            def project(l):
                v.memset(wgate, 0.0).then_inc(sem("wgate_zero"), 1)
                with dve.Fori(0, IN_CHUNKS // 2) as u:
                    for s in range(2):
                        dve.wait_ge(sem(f"proj_out{s}"), 16 * (l * 4 + u + 1))
                        for j in range(5):
                            n = 5 * s + j
                            dve.wait_ge(sem("in_made1"), l * 40 + u * 10 + n + 11)
                            v.tensor_copy(region(R_A + 2 * KD * IN_C + s * NT * IN_C, NT, IN_C)[:, 2 * j + 1, :],
                                          bank(2 + n % 2, IN_C)).then_inc(sem("in_kept1"), 1)
                handover("dve", dve)

            def rotate(out, x, scratch, tok, nh):
                xc, xs = scratch
                half = DK // 2
                cos, sin = (rope_t[:, tok, w:w + 1, :].to_broadcast([P, nh, DK]) for w in range(2))
                v.tensor_tensor(xc, x, cos, ALU.mult)
                v.tensor_tensor(xs, x, sin, ALU.mult)
                dve.drain()
                v.tensor_tensor(out[:, :, 0:half], xc[:, :, 0:half], xs[:, :, half:DK], ALU.subtract)
                return v.tensor_tensor(out[:, :, half:DK], xc[:, :, half:DK], xs[:, :, 0:half], ALU.add)

            def prepare(l):
                dve.wait_ge(sem("small_in"), 160 * (l + 1))
                lam_q = lam_v[:].rearrange("p (m w d) -> p m w d", m=2, w=2)
                v.tensor_tensor(lam_p[:].rearrange("p (m d) -> p m d", m=2), lam_q[:, :, 0, :], lam_q[:, :, 1, :], ALU.mult)
                v.scalar_tensor_tensor(out=dec_t[:], in0=dec_in[:], scalar=-1.0, in1=dec_in[:], op0=ALU.mult, op1=ALU.max)
                dve.drain()
                v.tensor_reduce(lam_s[:], lam_p[:].rearrange("p (m d) -> p m d", m=2), AX.X, ALU.add
                                ).then_inc(sem("dec_abs"), 1)
                dve.wait_ge(sem("dec_ln"), l + 1)
                v.scalar_tensor_tensor(out=neg_lam[:], in0=lam_e[:, 1:2], scalar=-lambda_init(l), in1=lam_e[:, 0:1],
                                       op0=ALU.add, op1=ALU.subtract)
                v.scalar_tensor_tensor(out=log_dec[:], in0=dec_in[:], scalar=0.0, in1=dec_t[:], op0=ALU.min,
                                       op1=ALU.subtract).then_inc(sem("log_dec_ready"), 1)
                with dve.Fori(0, NT // 2) as u:
                    for s in range(2):
                        T = l * NT + 2 * u + s
                        tok = 2 * u + s
                        tile = T_IN[s]

                        def cols(name, n):
                            return tile[:, COL[name]:COL[name] + n * DK].rearrange("p (h d) -> p h d", h=n)
                        dve.wait_ge(sem(f"tile_in{s}"), 16 * (l * (NT // 2) + u + 1))
                        dve.wait_ge(sem("turned1"), T + 2)
                        rotate(T_RD, cols("dq", 16), T_S[0], tok, 16)
                        rotate(T_RM, cols("mr", 1), T_S[1], tok, 1)
                        rotate(T_RR, cols("rq", 8), T_S[2], tok, 8).then_inc(sem("roped"), 1)
                        dve.wait_ge(sem("turned1"), T + 3)
                        qk = region(R_QKD, 4, NT, P)
                        turned = bank(0).rearrange("p (j c) -> p j c", j=4)
                        v.tensor_scalar(qk[:, 0:2, tok, :], turned[:, 0:2, :], DK ** -0.5, None, ALU.mult)
                        v.tensor_copy(qk[:, 2:4, tok, :], turned[:, 2:4, :]).then_inc(sem("kept0"), 1)
                        dve.wait_ge(sem("turned3"), T + 1)
                        v.tensor_copy(T_MK[:, :, HD:MQ], T_RM.to_broadcast([P, NH, DK]))
                        dve.wait_ge(sem("made2"), T + 2)
                        q = bank(3, NH * MQ).rearrange("p (h d) -> p h d", h=NH)
                        v.tensor_copy(T_MQ[:, :, 0:HD], q[:, :, 0:HD])
                        rotate(T_MQ[:, :, HD:MQ], q[:, :, HD:MQ], T_S[3], tok, NH).then_inc(sem("mq_ready"), 1)
                        dve.wait_ge(sem("turned3"), T + 2)
                        v.tensor_scalar(region(R_QM, 4, NT, P, parts=MQ)[:, :, tok, :],
                                        bank(6, parts=MQ).rearrange("p (j c) -> p j c", j=4), MQ ** -0.5, None, ALU.mult
                                        ).then_inc(sem("kept6"), 1)
                handover("dve", dve)

            def scan_factors(l, g):
                q = region(R_GR, 4, NC, CH)[:, 2 * g]
                k = region(R_GR, 4, NC, CH)[:, 2 * g + 1]
                s = DK ** -0.5
                if g == 0:
                    z = region(R_GZ, 2 * N)
                    a, b = region(R_H, 2 * N), region(R_H + 2 * N, 2 * N)
                    v.scalar_tensor_tensor(out=a, in0=z, scalar=-1.0, in1=z, op0=ALU.mult, op1=ALU.max
                                           ).then_inc(sem("gate_abs"), 1)
                    v.memset(RESET, 1.0)
                    dve.drain()
                    v.memset(RESET.rearrange("p (c i) -> p c i", c=NC)[:, :, 0:1], 0.0)
                    v.tensor_copy(mask[:], causal[:])
                    dve.wait_ge(sem("gate_ln"), l + 1)
                    v.scalar_tensor_tensor(out=a, in0=z, scalar=0.0, in1=b, op0=ALU.min, op1=ALU.subtract)
                    dve.drain()
                    v.tensor_scalar(z, a, 1.0 / GATE_NORM, None, ALU.mult)
                    dve.drain()
                    x1, x2, x3 = (x.rearrange("p (c i) -> p c i", c=NC) for x in (T1, T2, T3))
                    for d in range(2):
                        if d:
                            dve.wait_ge(sem("factors"), 2 * l + d)
                        la = region(R_GZ, 2, N)[:, d, :]
                        v.tensor_tensor_scan(T1, RESET, la, 0.0, ALU.mult, ALU.add)
                        dve.drain()
                        if d == 0:
                            e, mid = x1, x1[:, :, CH // 2 - 1:CH // 2]
                        else:
                            v.tensor_tensor(la, T1, la, ALU.subtract)
                            dve.drain()
                            e = la.rearrange("p (c i) -> p c i", c=NC)
                            mid = e[:, :, CH // 2:CH // 2 + 1]
                        v.tensor_tensor(x2, e, mid.to_broadcast([P, NC, CH]), ALU.subtract)
                        v.tensor_tensor(x3, e, x1[:, :, CH - 1:CH].to_broadcast([P, NC, CH]), ALU.subtract)
                        dve.drain()
                        v.tensor_scalar(T2, T2, LIMIT, -LIMIT, ALU.min, ALU.max).then_inc(sem("exponents"), 1)
                        dve.wait_ge(sem("factors"), 2 * l + d + 1)
                        for j, src, f in ((QS, q, s), (KS, k, 1.0), (QD, q, s), (KDE, k, 1.0)):
                            v.scalar_tensor_tensor(out=E[d][:, :, j, :], in0=E[d][:, :, j, :], scalar=f, in1=src,
                                                   op0=ALU.mult, op1=ALU.mult)
                else:
                    dve.wait_ge(sem("ret_factors"), l + 1)
                    v.tensor_tensor(mask[:], mask[:], causal[:], ALU.mult)
                    for d in range(2):
                        eq, ek = (edge[:, (2 * d + w) * CH:(2 * d + w + 1) * CH].unsqueeze(1).to_broadcast([P, NC, CH])
                                  for w in range(2))
                        v.tensor_copy(E[d][:, :, QS, :], q)
                        v.tensor_scalar(E[d][:, :, KS, :], k, s, None, ALU.mult)
                        v.tensor_tensor(E[d][:, :, QD, :], q, eq, ALU.mult)
                        v.scalar_tensor_tensor(out=E[d][:, :, KDE, :], in0=k, scalar=s, in1=ek, op0=ALU.mult, op1=ALU.mult)
                handover("dve", dve)

            def scan(l, g):
                inst = 2 * l + g
                for d in range(2):
                    v.memset(STATE[d], 0.0).then_inc(sem(f"state_ready{d}"), 1)
                own = heads[:].unsqueeze(2).to_broadcast([P, NH, HD])
                for a, b in SCANS:
                    with dve.Fori(0, (b - a) // 2) as pair:
                        i = a + 2 * pair
                        for p in range(2):
                            n = inst * NC + i + p
                            for d in range(2):
                                dve.wait_ge(sem(f"sc_made{d}"), n + 1)
                                dve.wait_ge(sem(f"o_made{d}"), n + 2)
                                v.tensor_tensor(SCM[d].rearrange("p h i -> p (h i)"), bank(d, NH * CH, CH),
                                                mask[:, d * NH * CH:(d + 1) * NH * CH], ALU.mult
                                                ).then_inc(sem(f"scm_ready{d}"), 1)
                            for d in range(2):
                                dve.wait_ge(sem(f"u_made{d}"), n + 2)
                                v.tensor_tensor(UM[d], bank(6 + d, NH * HD).rearrange("p (h e) -> p h e", h=NH), own,
                                                ALU.mult)
                                dve.drain()
                                v.scalar_tensor_tensor(out=STATE[d], in0=STATE[d], scalar=in_turn(dec_v[:, d, :], d, a, b)[:, bass.ds(2 * pair + p, 1)],
                                                       in1=UM[d].rearrange("p h e -> p (h e)"), op0=ALU.mult, op1=ALU.add
                                                       ).then_inc(sem(f"state_ready{d}"), 1)
                handover("dve", dve)

            def attend(l):
                for first, count, base, segs, nk in att_loops(l):
                    pieces = spans(0) if nk == NT else [(0, CTX)]
                    with dve.Fori(0, count) as i:
                        M0 = (base + i) * MAPS
                        for m in range(MAPS + 2):
                            if m < MAPS:
                                for j, (c, w) in enumerate(pieces):
                                    dve.wait_ge(sem("scored"), segs + (i * MAPS + m) * len(pieces) + j + 2)
                                    v.tensor_reduce(A_CM[:, j:j + 1], psum[:, c:c + w], AX.X, ALU.max)
                                dve.drain()
                                v.tensor_reduce(A_NM[:, m:m + 1], A_CM[:, 0:len(pieces)], AX.X, ALU.max, negate=True
                                                ).then_inc(sem("max_ready"), 1)
                            if 1 <= m <= MAPS:
                                dve.wait_ge(sem("turned"), M0 + m - 1 + 3)
                                dve.wait_ge(sem("pv_made"), M0 + m - 1 + 1)
                                w0, w1 = (4, NT) if nk == NT else (1, 2)
                                v.tensor_copy(A_PT[(m - 1) % 2][:, w0:w1, :].rearrange("p a b -> p (a b)"),
                                              psum[:, 4 * BANK:4 * BANK + (w1 - w0) * P]).then_inc(sem("pt_dve"), 1)
                            if m >= 2:
                                o = m - 2
                                if o == 0:
                                    dve.wait_ge(sem("att_out"), 16 * (base + i + 1))
                                rl = A_RL[:, o:o + 1]
                                v.reciprocal(rl, A_L[:, o:o + 1])
                                dve.drain()
                                if o < 8 and o % 2:
                                    v.tensor_tensor(rl, rl, neg_lam[:], ALU.mult)
                                    dve.drain()
                                dve.wait_ge(sem("pv_made"), M0 + o + 3)
                                h = o // 2 if o < 8 else o - 4
                                dst = A_OUT[:, h * HD:(h + 1) * HD]
                                src = bank(6 + o % 2, HD)
                                if o < 8 and o % 2:
                                    last = v.scalar_tensor_tensor(out=dst, in0=src, scalar=rl, in1=dst, op0=ALU.mult,
                                                                  op1=ALU.add)
                                else:
                                    last = v.tensor_scalar(dst, src, rl, None, ALU.mult)
                                last.then_inc(sem("att_kept"), 1)
                handover("dve", dve)

            def finish(l):
                c0, count, base = fin_loop(l)
                dve.wait_ge(sem("outg_in"), 16 * (l + 1))
                v.tensor_scalar(F_OUTG[:, 0:256], F_OUTG[:, 0:256], 1.0 - lambda_init(l), None, ALU.mult)
                dve.drain()
                with dve.Fori(0, count // 2) as u:
                    for s in range(2):
                        T = 2 * base + 2 * u + s
                        tok = c0 + 2 * u + s
                        hm = F_HM[s]
                        dve.wait_ge(sem(f"fin_in{s}"), 80 * (base + u + 1))
                        v.tensor_tensor(hm[:, 512:1024], hm[:, 512:1024], F_SB[s], ALU.add).then_inc(sem("fin_sum"), 1)
                        dve.wait_ge(sem("fin_sq"), T + 1)
                        v.tensor_reduce(F_SS, F_SQ.rearrange("p (h d) -> p h d", h=16), AX.X, ALU.add
                                        ).then_inc(sem("fin_ss"), 1)
                        dve.wait_ge(sem("fin_rs"), T + 1)
                        for a, b in ((0, 4), (8, 16)):
                            hv = hm[:, a * HD:b * HD].rearrange("p (h d) -> p h d", d=HD)
                            v.tensor_tensor(hv, hv, F_RS[:, a:b].unsqueeze(2).to_broadcast([P, b - a, HD]), ALU.mult)
                        dve.drain()
                        v.tensor_tensor(hm[:, 0:256], hm[:, 0:256], F_OUTG[:, 0:256], ALU.mult)
                        v.tensor_tensor(hm[:, 512:1024], hm[:, 512:1024], F_OUTG[:, 512:1024], ALU.mult)
                        dve.drain()
                        v.tensor_tensor(hm[:, 512:1024], hm[:, 512:1024], F_SG, ALU.mult).then_inc(sem("fin_ready"), 1)
                        dve.wait_ge(sem(f"fin_turned{s}"), base + u + 2)
                        v.tensor_copy(region(R_H, KD, NT, P)[:, 4:8, tok, :],
                                      bank(2 * s + 1).rearrange("p (j c) -> p j c", j=4)).then_inc(sem(f"fin_kept_v{s}"), 1)
                handover("dve", dve)

            def columns(l, j):
                c0 = first_token(l, True)
                dst = region(Y1 if j == 0 else R_H, KD, N)
                a, n = spans(c0)[1]
                with dve.Fori(0, KD // 2) as u:
                    for s in range(2):
                        dve.wait_ge(sem(f"y_made{s}"), (2 * l + j) * (KD // 2) + u + 2)
                        v.tensor_copy(dst[:, 2 * u + s, a:a + n],
                                      psum[:, 3 * s * BANK + a - c0:3 * s * BANK + a - c0 + n]).then_inc(sem(f"y_kept_v{s}"), 1)
                handover("dve", dve)

            def hidden(l):
                c0 = first_token(l, True)
                with dve.Fori(0, KH // 2) as u:
                    for s in range(2):
                        n = l * KH + 2 * u + s
                        dve.wait_ge(sem(f"up_made{s}"), l * (KH // 2) + u + 2)
                        dve.wait_ge(sem("silu_done"), n + 2)
                        v.tensor_tensor(region(R_A, KH, N)[:, 2 * u + s, c0:N], region(R_B + 4 * KD * P + s * N, N)[:, c0:N],
                                        psum[:, 3 * BANK:3 * BANK + N - c0], ALU.mult).then_inc(sem("up_done"), 1)
                handover("dve", dve)

            for l in range(DEPTH):
                modulation(l)
            norm(0)
            for l in range(DEPTH):
                project(l)
                prepare(l)
                for g in range(2):
                    scan_factors(l, g)
                    scan(l, g)
                attend(l)
                finish(l)
                columns(l, 0)
                norm(2 * l + 1)
                hidden(l)
                columns(l, 1)
                norm(2 * l + 2)

        @block.gpsimd
        def _(pool):
            def idle():
                handover("pool", pool)

            def scan(l, g):
                inst = 2 * l + g
                own = heads[:].unsqueeze(2).to_broadcast([P, NH, CH])
                for a, b in SCANS:
                    with pool.Fori(0, (b - a) // 2) as pair:
                        i = a + 2 * pair
                        for p in range(2):
                            n = inst * NC + i + p
                            for d in range(2):
                                pool.wait_ge(sem(f"o_made{d}"), n + 1)
                                nc.gpsimd.tensor_copy(EST[d][p], in_turn(E[d], d, a, b)[:, 2 * pair + p, 0:3, :])
                                nc.gpsimd.tensor_tensor(QBD[d][p], in_turn(E[d], d, a, b)[:, 2 * pair + p, QS:QS + 1, :].to_broadcast([P, NH, CH]), own,
                                                        ALU.mult).then_inc(sem(f"est_ready{d}"), 1)
                handover("pool", pool)

            def attend(l):
                for first, count, base, segs, nk in att_loops(l):
                    nseg = NSEG if nk == NT else 1
                    with pool.Fori(0, count) as i:
                        pool.wait_ge(sem("scored"), segs + i * (MAPS * nseg) + 1)
                        nc.gpsimd.tensor_copy(A_QD, region(R_QKD, 4, NT, P)[:, 0:2, first + i, :])
                        nc.gpsimd.tensor_copy(A_QM, region(R_QM, 4, NT, P, parts=MQ)[:, :, first + i, :]
                                              ).then_inc(sem("q_staged"), 1)
                handover("pool", pool)

            for l in range(DEPTH):
                idle()
            idle()
            pool.wait_ge(sem("const_in"), 16 * 9)
            for l in range(DEPTH):
                idle()
                idle()
                for g in range(2):
                    idle()
                    scan(l, g)
                attend(l)
                for _ in range(6):
                    idle()


def constants():
    import numpy as np
    c = {"c_ident": np.eye(P, dtype=np.float32)}
    tok = np.arange(LAT)
    row, col = (tok // 64).astype(np.float32), (tok % 64).astype(np.float32)
    nf = DK // 4
    freqs = (np.float32(10000.0) ** (-np.arange(nf, dtype=np.float32) / nf)).astype(np.float32)
    ang = np.concatenate([row[:, None] * freqs, col[:, None] * freqs], -1).astype(np.float32)
    cos, sin = np.ones((N, DK), np.float32), np.zeros((N, DK), np.float32)
    cos[CTX:] = np.tile(np.cos(ang), (1, 2))
    sin[CTX:] = np.tile(np.sin(ang), (1, 2))
    both = np.stack([cos, sin], 1).reshape(NT, P, 2, DK)
    c["c_rope"] = np.ascontiguousarray(both.transpose(1, 0, 2, 3)).reshape(P, -1)
    part = np.arange(P)
    c["c_heads"] = (part[:, None] // DK == np.arange(NH)[None, :]).astype(np.float32)
    j, i = np.arange(CH)[:, None], np.arange(CH)[None, :]
    dist = np.stack([i - j, j - i], 1)
    seen = (dist >= 0).astype(np.float32)
    c["c_causal"] = np.ascontiguousarray(np.broadcast_to(seen[:, :, None, :], (CH, 2, NH, CH))).reshape(CH, -1)
    c["c_rel"] = np.maximum(dist, 0).astype(np.float32).reshape(CH, -1)
    at = np.arange(CH, dtype=np.float32)
    edges = np.stack([at + 1, CH - 1 - at, CH - at, at])
    c["c_steps"] = np.ascontiguousarray(np.broadcast_to(edges.reshape(1, -1), (P, 4 * CH)))
    return c


def laid_out(i):
    import numpy as np
    a = {k: np.asarray(v) for k, v in i.items()}

    def on_parts(w, lead):
        s = w.shape
        w = w.reshape(s[:lead] + (s[lead] // P, P) + s[lead + 1:])
        return np.moveaxis(w, lead + 1, lead)

    def chunked(w, n_chunks):
        w = on_parts(w, 1)
        w = w.reshape(w.shape[:3] + (n_chunks, -1)).transpose(0, 3, 1, 2, 4)
        return np.ascontiguousarray(w).reshape(DEPTH, n_chunks, P, -1)
    r = constants()
    r["x"] = np.ascontiguousarray(on_parts(np.concatenate([a["ctx"][0], a["x"][0]], 0).T, 0))
    r["cond"] = np.ascontiguousarray(on_parts(np.stack([a["c"][0], a["c_ctx"]], 1), 0)).reshape(P, -1)
    r["norm_g"] = np.ascontiguousarray(a["norm_g"].reshape(DEPTH, 4, KD, P).transpose(3, 0, 1, 2)).reshape(P, -1)
    r["ada_b"] = np.ascontiguousarray(a["ada_b"].reshape(DEPTH, 6 * KD, P).transpose(2, 0, 1)).reshape(P, -1)
    r["ada_w"] = chunked(a["ada_w"], ADA_CHUNKS)
    r["w_in"] = chunked(a["w_in"], IN_CHUNKS)
    r["w_out"] = chunked(a["w_out"], KD)
    r["ffn_out"] = chunked(a["ffn_w_out"], KD)
    g = on_parts(a["ffn_w_in"], 1).reshape(DEPTH, P, KD, 2, KH, P).transpose(0, 4, 1, 2, 3, 5)
    r["ffn_in"] = np.ascontiguousarray(g).reshape(DEPTH, KH, P, -1)
    r["w_uq"] = np.ascontiguousarray(on_parts(a["mla_w_uq"], 1))
    r["w_ukv"] = a["mla_w_ukv"]
    r["w_gate"] = np.ascontiguousarray(a["gla_w_gate"].transpose(0, 2, 1, 3))
    r["b_gate"] = np.ascontiguousarray(a["gla_b_gate"].transpose(0, 2, 1))
    r["q_norm"] = np.ascontiguousarray(a["mla_q_norm"].reshape(DEPTH, 2, P).transpose(0, 2, 1))
    r["kv_norm"] = a["mla_kv_norm"].reshape(DEPTH, P, 1)
    r["decay"] = a["ret_decay"].reshape(DEPTH, 8)
    r["decay_col"] = np.ascontiguousarray(np.repeat(a["ret_decay"].transpose(0, 2, 1), DK, 1))
    r["lam"] = a["diff_lam"].reshape(DEPTH, 4 * DK)
    one = np.ones((DEPTH, 256), np.float32)
    r["out_g"] = np.concatenate([np.tile(a["diff_norm"], (1, NH)), one, np.tile(a["gla_norm"], (1, NH)),
                                 np.tile(a["ret_norm"], (1, NH))], 1)
    return r


def kernel(**inputs):
    import numpy as np
    import concourse.bacc as bacc
    from concourse.bass_utils import run_bass_kernel_spmd

    nc = bacc.Bacc("TRN2", target_bir_lowering=False, num_devices=1)
    arrays = laid_out(inputs)
    t = {n: nc.dram_tensor("in_" + n, a.shape, mybir.dt.from_np(a.dtype), kind="ExternalInput").ap() for n, a in arrays.items()}
    t["out"] = nc.dram_tensor("out_latent", (P, KD, LAT), F32, kind="ExternalOutput").ap()
    build(nc, t)
    r = run_bass_kernel_spmd(nc, [{"in_" + n: a for n, a in arrays.items()}], core_ids=[0])
    out = r.results[0]["out_latent"]
    return np.ascontiguousarray(out.transpose(2, 1, 0)).reshape(1, LAT, D)
```

```python
from contextlib import ExitStack

import concourse.bass as bass
from concourse import mybir

F32 = mybir.dt.float32
F32R = mybir.dt.float32r
ALU = mybir.AluOpType
ACT = mybir.ActivationFunctionType
AX = mybir.AxisListType

P = 128
BANK = 512
D = 1024
KD = D // P
CTX, LAT = 256, 1024
N = CTX + LAT
NT = N // P
CT = CTX // P
DEPTH = 2
NH = 4
HD = 64
DK = 32
QR, KVR = 256, 128
MQ = HD + DK
GR = 16
CH = 64
NC = N // CH
CC = CTX // CH
HID = 2816
KH = HID // P
EPS = 1e-6
GATE_NORM = 16.0
LIMIT = 80.0

SIZES = (("dq", 256), ("dk", 256), ("dv", 256), ("mq", QR), ("mkv", KVR), ("mr", DK), ("gq", 128), ("gk", 128),
         ("gv", 256), ("gr", 256), ("gf", GR), ("gb", GR), ("rq", 128), ("rk", 128), ("rv", 256), ("rg", 256))
COL = {}
IN_W = 0
for _name, _size in SIZES:
    COL[_name] = IN_W
    IN_W += _size
IN_CHUNKS = 8
IN_C = IN_W // IN_CHUNKS
ADA_FIRST = 2 * KD
ADA_M = BANK // P
ADA_T = 2

MAPS = 3 * NH
OUTS = 2 * NH

R_H = 0
R_A = KD * N
R_QKD = R_A
R_GR = R_QKD + 4 * N
R_QM = R_GR + 4 * N
R_KM = R_QM + 4 * N
R_VM = R_KM + 4 * N
R_VD = R_VM + NT * 256
R_GZ = R_VD + NT * 256
R_B = R_GZ + 2 * N
H_LO, H_HI = R_H, R_A
ARENA = 50048
MIX_LO, MIX_HI = R_H, ARENA - KD * N
FFN_T = BANK
ACT_HI = R_A + KD * N
ACT_LO = ACT_HI + KH * FFN_T
W_AT = ACT_LO + KH * FFN_T
UNIT = KH // 2 * P


def lambda_init(layer):
    import math
    return 0.8 - 0.6 * math.exp(-0.3 * layer)


def build(nc, t):
    ctx = ExitStack()
    with ctx:
        def sb(name, shape):
            return ctx.enter_context(nc.sbuf_tensor(name, shape, F32))

        made = {}

        def sem(name):
            if name not in made:
                made[name] = ctx.enter_context(nc.semaphore(name))
            return made[name]

        proj = nc.dram_tensor("proj", [N, IN_W], F32).ap()
        att = nc.dram_tensor("att", [N, 512], F32).ap()
        scans = nc.dram_tensor("scans", [2, N, 512], F32).ap()
        xdram = nc.dram_tensor("xdram", [P, KD, N], F32).ap()

        sb("arena", [P, ARENA])
        arena_at = nc.sbuf_base - 4 * ARENA
        placed = {}

        def region(start, *dims, parts=P, dtype=F32):
            size = 1
            for d in dims:
                size *= d
            assert start + size <= ARENA
            key = (start, size, dtype is F32R)
            if key not in placed:
                name = f"{'part' if dtype is F32R else 'region'}_{start}_{size}"
                placed[key] = nc.alloc_sbuf_tensor_at(name, [P, size], dtype, offset=arena_at + 4 * start)
            a = placed[key][0:parts, :]
            if len(dims) == 2:
                a = a.rearrange("p (a b) -> p a b", a=dims[0])
            if len(dims) == 3:
                a = a.rearrange("p (a b c) -> p a b c", a=dims[0], b=dims[1])
            if len(dims) == 4:
                a = a.rearrange("p (a b c d) -> p a b c d", a=dims[0], b=dims[1], c=dims[2])
            return a

        def region_r(start, *dims):
            return region(start, *dims, dtype=F32R)

        psum = ctx.enter_context(nc.psum_tensor("psum", [P, 8 * BANK], F32))

        def bank(b, n=BANK, parts=P):
            return psum[0:parts, b * BANK:b * BANK + n]

        ident = sb("ident", [P, P])
        ones = sb("ones", [P, P])
        eps = sb("eps", [P, 1])
        rope = sb("rope", [P, NT * 2 * DK])
        rope_t = rope[:].rearrange("p (t w d) -> p t w d", t=NT, w=2)
        heads = sb("heads", [P, NH])
        causal = sb("causal", [CH, 2 * NH * CH])
        rel = sb("rel", [CH, 2 * CH])
        steps = sb("steps", [P, 4 * CH])
        sil = sb("sil", [P, KD * 2])
        sil_in = sb("sil_in", [P, KD * 2])
        mods = sb("mods", [P, DEPTH * 6 * KD * 2])
        mods_v = mods[:].rearrange("p (l w k s) -> p l w k s", l=DEPTH, w=6, k=KD)
        gains = sb("gains", [P, DEPTH * 4 * KD])
        gains_v = gains[:].rearrange("p (l w k) -> p l w k", l=DEPTH, w=4)
        ada_b = sb("ada_b", [P, DEPTH * 6 * KD])
        mods_f = mods[:].rearrange("p (m s) -> p m s", s=2)
        wuq = region(R_B, 2, NH * MQ)
        wukv = region(R_B + 2 * NH * MQ, NH * 2 * HD)
        wgate = region(R_B + 2 * NH * MQ + NH * 2 * HD, 2, P, parts=2 * GR)
        bgate = sb("bgate", [P, 2])
        qnorm = sb("qnorm", [P, 2])
        kvnorm = sb("kvnorm", [P, 1])
        lam_at = R_B + 2 * NH * MQ + NH * 2 * HD + 2 * P
        lam_v, lam_p = region(lam_at, 4 * DK), region(lam_at + 4 * DK, 2 * DK)
        lam_s = sb("lam_s", [P, 2])
        lam_e = sb("lam_e", [P, 2])
        neg_lam = sb("neg_lam", [P, 1])
        dec_in = sb("dec_in", [P, 10])
        dec_t = sb("dec_t", [P, 10])
        log_dec = sb("log_dec", [P, 10])
        mask = sb("mask", [CH, 2 * NH * CH])
        chunk_dec = sb("chunk_dec", [P, 2 * NC])
        dec_v = chunk_dec[:].rearrange("p (d c) -> p d c", d=2)
        edge = sb("edge", [P, 4 * CH])

        turn = {e: 0 for e in ("pe", "act", "dve", "pool", "sp")}

        def handover(who, eng):
            turn[who] += 1
            eng.drain().then_inc(sem("stage_done"), 1)
            eng.wait_ge(sem("stage_done"), 5 * turn[who])

        def first_token(layer, last_part):
            return CTX if last_part and layer == DEPTH - 1 else 0

        def spans(c0):
            return [(c, min(BANK, N - c)) for c in range(c0, N, BANK)]

        def streams(c0):
            return ([(1, 0, CTX)] if c0 == 0 else []) + [(0, CTX, N)]

        Y1 = R_A + KD * N
        X_AT = R_A + 2 * KD * N
        NORMS = [dict(y=None, pre=0, layer=0, c0=0)]
        for _l in range(DEPTH):
            NORMS.append(dict(y=Y1, gate=2, gain=1, pre=3, layer=_l, c0=first_token(_l, True)))
            NORMS.append(dict(y=R_H, gate=5, gain=3, pre=0 if _l < DEPTH - 1 else None, layer=_l,
                              c0=first_token(_l, True)))
        for _n in NORMS:
            _n["pre_layer"] = _n["layer"] + (_n.get("gate") == 5)
        sq_count = []
        rs_count = []
        _a = _b = 0
        for _n in NORMS:
            sq_count.append(_a)
            rs_count.append(_b)
            _a += KD * ((_n["y"] is not None) + (_n["pre"] is not None))
            _b += (_n["y"] is not None) + (_n["pre"] is not None)
        N_SQ, N_TMP, N_RS = X_AT + KD * N, X_AT + (KD + 2) * N, X_AT + (KD + 4) * N


        WIN_LO, WIN_HI, WIN_OUT = Y1, Y1 + 2 * KD * IN_C, Y1 + 4 * KD * IN_C
        assert WIN_OUT + NT * IN_C <= R_B

        def blocks(l):
            b = [(a, n) for a, n in spans(first_token(l, True))]
            before = len(spans(0)) if l else 0
            return [(before + j, a, n) for j, (a, n) in enumerate(b)]

        def back(l, block=None):
            j = 0 if block is None else block[0] - (len(spans(0)) if l else 0) + 1
            done = (l * len(spans(0)) + l + j)
            mixers = l + (j > 0)
            units = KD * (2 * done - mixers)
            if block is None:
                c0 = first_token(l, True)
                return 1, KD, (MIX_HI, MIX_LO), Y1, R_A, units, KD * done, c0, N - c0
            return 2, KH // 2, (ACT_HI, ACT_LO), R_H, W_AT, units, KD * done, block[1], block[2]

        def unit_slots(w_at):
            return w_at, [w_at + (1 + i) * UNIT for i in range(2)], [w_at + (3 + i) * UNIT for i in range(2)]
        assert W_AT + 5 * UNIT <= ARENA

        WF = [[W_AT + (3 * half + i) * KD * P for i in range(3)] for half in range(2)]
        SILU_AT = W_AT + 6 * KD * P
        assert SILU_AT + FFN_T <= ARENA

        SCANS = ((0, CC), (CC, NC))

        def in_turn(x, d, a, b):
            if d == 0:
                return x[:, a:b]
            return x[:, b - 1:a - 1:-1] if a else x[:, b - 1::-1]

        _at = [R_H + 2 * IN_W]

        def take(*dims, parts=P):
            size = 1
            for d in dims:
                size *= d
            start = _at[0]
            _at[0] += -(-size // 8) * 8
            return region(start, *dims, parts=parts)
        T_IN = [region(R_H + s * IN_W, IN_W) for s in range(2)]
        T_RD, T_RM, T_RR = take(16, DK), take(1, DK), take(8, DK)
        T_S = [(take(n, DK), take(n, DK)) for n in (16, 1, 8, NH)]
        T_QN, T_QNT, T_GT = take(3, P), take(3, P), take(P, parts=2 * GR)
        T_MQ, T_MK = take(NH, MQ), take(NH, MQ)
        T_SS = sb("ss", [P, 2])
        T_RS = sb("rs", [P, 2])
        assert _at[0] <= R_A

        E = [region(R_H + d * 4 * N, NC, 4, CH) for d in range(2)]
        KS, KDE, QD, QS = range(4)
        R_O = R_B
        RESET = region(R_B, N)
        R_T = R_B + NC * 256
        T1, T2, T3 = (region(R_T + i * N, N) for i in range(3))
        _at[0] = R_T
        R_V = R_T
        _at[0] += 4 * 256
        V = [[region(R_V + (2 * d + p) * 256, NH * HD, parts=CH) for p in range(2)] for d in range(2)]
        EST = [[take(3, CH) for p in range(2)] for d in range(2)]
        QBD = [[take(NH, CH) for p in range(2)] for d in range(2)]
        SCM = [take(NH, CH, parts=CH) for d in range(2)]
        UM = [take(NH, HD) for d in range(2)]
        STATE = [take(NH * HD) for d in range(2)]
        KDT = [take(P, parts=CH) for d in range(2)]

        _at[0] = R_H
        A_QD, A_QM = take(2, P), take(NH, P, parts=MQ)
        A_P = [take(N) for _ in range(4)]
        A_PT = [take(NT, P) for _ in range(2)]
        A_CM, A_NM, A_L, A_LS = take(3), take(MAPS), take(MAPS, 2), take(MAPS)
        A_RL, A_SC, A_NL = take(OUTS), take(NH), take(NH)
        A_OUT = region(R_B, NT, OUTS * HD)
        assert _at[0] <= R_A

        TURNED = 3 * BANK

        def score_pieces(nk):
            return [(c, w, 1, c > 0) for c, w in spans(0)] if nk == NT else [(0, CTX, 3, True)]

        def exp_parts(nk):
            return (0, BANK, N) if nk == NT else (0, P, CTX)

        VALUES_AT = {4: 0, 6: 1, 8: 2, 10: 3, 11: 4}
        TURN_AT = {3: 0, 5: 1, 7: 2, 9: 3, 10: 4, 11: 5}
        LATE_VALUES_AT = {0: 5, 1: 6, 2: 7}
        LATE_TURN_AT = {0: 6, 1: 7}

        def att_tiles(eng, count, step):
            def tile(i, first):
                for m in range(MAPS):
                    values = (i, VALUES_AT[m]) if m in VALUES_AT else None
                    turn_ = (i, TURN_AT[m]) if m in TURN_AT else None
                    if not first:
                        values = (i - 1, LATE_VALUES_AT[m]) if m in LATE_VALUES_AT else values
                        turn_ = (i - 1, LATE_TURN_AT[m]) if m in LATE_TURN_AT else turn_
                    step(m, i, values, turn_)
            tile(0, True)
            with eng.Fori(1, count) as i:
                tile(i, False)
            for m in range(3):
                step(m, None, (count - 1, LATE_VALUES_AT[m]), (count - 1, LATE_TURN_AT[m]) if m in LATE_TURN_AT else None)

        def att_loops(l):
            return ([] if l else [(0, CT, 0, CT)]) + [(CT, NT - CT, NT if l else CT, NT)]

        _at[0] = R_A
        F_HM = [take(D) for _ in range(2)]
        F_SB = [take(512) for _ in range(2)]
        F_G = [take(512) for _ in range(2)]
        F_SQ, F_SG, F_OUTG = take(D), take(512), take(D)
        F_SS, F_RS = take(16), take(16)
        ADA_ROWS0 = region(R_B, ADA_FIRST * P, parts=2)
        F_ADA = [take(ADA_T, KD, BANK) for _ in range(2)]
        F_ROWS = take(ADA_T * BANK, parts=2)

        def fin_loop(l):
            return (0, NT, 0) if l == 0 else (CT, NT - CT, NT // 2)

        FREE = {
            "pe": dict(rows_made=2, rows_turned=1, in_made1=10, turned1=2, made2=1, turned3=1, o_made0=2, o_made1=2,
                       u_made0=1, u_made1=1, turned=4, pv_made=2, fin_turned0=1, fin_turned1=1, yb_made=2, gate_made=1,
                       up_made=1),
            "act": dict(rows_kept=1, in_kept0=2, qn_ready=2, kept12=1, mk_ready=1, kept7=1, kd_kept0=1, kd_kept1=1, o_kept0=1,
                        o_kept1=1, exp_done=1, head_done=1, pt_act=1, fin_kept_a0=1, fin_kept_a1=1, yb_kept=2,
                        silu_done=1, proj_out=16),
            "dve": dict(ada_kept=1, in_kept1=2, roped=2, kept0=1, mq_ready=1, kept6=1, scm_ready0=1,
                        scm_ready1=1, pt_dve=1, att_kept=2, fin_kept_v0=1, fin_kept_v1=1, wb_ready=1,
                        wf_ready0=1, wf_ready1=1, up_done=1, fin_ready=1),
        }

        def free(who, eng):
            for name, n in FREE[who].items():
                eng.sem_inc(sem(name), n)

        block = ctx.enter_context(nc.Block())

        @block.sync
        def _(sp):
            for dst, name in ((ident, "c_ident"), (rope, "c_rope"), (heads, "c_heads"), (causal, "c_causal"),
                              (rel, "c_rel"), (steps, "c_steps"), (sil_in, "cond")):
                sp.dma_start(dst[:], t[name]).then_inc(sem("const_in"), 16)

            for dst, name in ((gains, "norm_g"), (ada_b, "ada_b")):
                sp.dma_start(dst[:], t[name]).then_inc(sem("const_in"), 16)

            def first_modulation():
                for c in range(ADA_FIRST // ADA_M):
                    sp.dma_start(region(R_H + c * ADA_M * D, ADA_M * D), t["ada_w"][c]).then_inc(sem(f"ada0_in{c}"), 16)
                handover("sp", sp)

            def small(l):
                for dst, src in ((wuq, t["w_uq"][l]), (wukv, t["w_ukv"][l]), (bgate[:], t["b_gate"][l]),
                                 (qnorm[:], t["q_norm"][l]), (kvnorm[:], t["kv_norm"][l]),
                                 (dec_in[:, 8:10], t["decay_col"][l]), (lam_v, t["lam"][l].partition_broadcast(P)),
                                 (dec_in[:, 0:8], t["decay"][l].partition_broadcast(P))):
                    sp.dma_start(dst, src).then_inc(sem("small_in"), 16)
                sp.wait_ge(sem("wgate_zero"), l + 1)
                for d in range(2):
                    sp.dma_start(wgate[d * GR:(d + 1) * GR, d, :], t["w_gate"][l, :, d, :]).then_inc(sem("small_in"), 16)

            def norm(i):
                n = NORMS[i]
                c0 = n["c0"]
                src = t["x"] if i <= 1 else xdram
                for k in range(KD):
                    sp.dma_start(region(X_AT, KD, N)[:, k, c0:N], src[:, k, c0:N]).then_inc(sem(f"x_in{k}"), 16)
                if n["y"] is not None:
                    last = n["pre"] is None
                    for k in range(KD):
                        sp.wait_ge(sem("x_new"), (i - 1) * KD + k + 1)
                        xk = region(X_AT, KD, N)[:, k, c0:N]
                        dst = t["out"][:, k, :] if last else xdram[:, k, c0:N]
                        sp.dma_start(dst, xk).then_inc(sem("x_out"), 16)
                    sp.wait_ge(sem("x_out"), 16 * KD * i)
                handover("sp", sp)

            def project(l):
                small(l)
                with sp.Fori(0, IN_CHUNKS // 2) as u:
                    for s in range(2):
                        sp.wait_ge(sem("in_made1"), l * 40 + u * 10 + 5 * (s + 1))
                        sp.dma_start(region(WIN_LO + s * KD * IN_C, KD * IN_C),
                                     t["w_in"][l, 2 * u + s]).then_inc(sem(f"win_in{s}"), 16)
                handover("sp", sp)

            def prepare(l):
                sp.dma_start(region(R_VD, NT, 256), proj.rearrange("(t p) c -> p t c", p=P)[:, :, COL["dv"]:COL["dv"] + 256]
                             ).then_inc(sem("vd_in"), 16)
                with sp.Fori(0, NT // 2) as u:
                    for s in range(2):
                        for read in ("roped", "qn_ready", "turned1"):
                            sp.wait_ge(sem(read), l * NT + 2 * u + s + 1)
                        sp.dma_start(region(R_H + s * IN_W, IN_W), proj.rearrange("(t p) c -> p t c", p=P)[:, 2 * u + s, :]
                                     ).then_inc(sem(f"tile_in{s}"), 16)
                sp.wait_ge(sem("vd_in"), 16 * (l + 1))
                handover("sp", sp)

            def scan(l, g):
                inst = 2 * l + g
                col = COL["rv" if g else "gv"]
                for a, b in SCANS:
                    with sp.Fori(0, (b - a) // 2) as pair:
                        i = a + 2 * pair
                        for p in range(2):
                            for d in range(2):
                                sp.wait_ge(sem(f"o_made{d}"), inst * NC + i + p + 1)
                                sp.dma_start(region(R_V + (2 * d + p) * 256, 256, parts=CH),
                                             in_turn(proj.rearrange("(c p) f -> p c f", p=CH)[:, :, col:col + 256], d, a, b)[:, 2 * pair + p, :]
                                             ).then_inc(sem(f"v_in{d}{p}"), 16)
                for d in range(2):
                    sp.wait_ge(sem(f"o_kept{d}"), (inst + 1) * NC + 1)
                    sp.dma_start(scans[d].rearrange("(c p) f -> p c f", p=CH)[:, :, g * 256:(g + 1) * 256],
                                 region(R_O, NC, 256)[d * CH:(d + 1) * CH]).then_inc(sem("o_out"), 16)
                sp.wait_ge(sem("o_out"), 32 * (inst + 1))
                handover("sp", sp)

            def attend(l):
                for first, count, base, nk in att_loops(l):
                    with sp.Fori(0, count) as i:
                        sp.wait_ge(sem("att_kept"), (base + i) * OUTS + OUTS + 2)
                        sp.dma_start(att.rearrange("(t p) c -> p t c", p=P)[:, first + i, :], A_OUT[:, first + i, :]
                                     ).then_inc(sem("att_out"), 16)
                    sp.wait_ge(sem("att_out"), 16 * (base + count))
                handover("sp", sp)

            def finish(l):
                c0, count, base = fin_loop(l)
                sp.dma_start(F_OUTG, t["out_g"][l].partition_broadcast(P)).then_inc(sem("outg_in"), 16)
                with sp.Fori(0, count // 2) as u:
                    for s in range(2):
                        sp.wait_ge(sem(f"fin_turned{s}"), base + u + 1)
                        if l == 0:
                            for j in range(ADA_T):
                                sp.dma_start(F_ADA[s][:, j, :, :].rearrange("p k n -> p (k n)"),
                                             t["ada_w"][ADA_FIRST // ADA_M + ADA_T * (2 * u + s) + j]
                                             ).then_inc(sem(f"ada_in{s}"), 16)
                        tok = c0 + 2 * u + s

                        def rows(a):
                            return a.rearrange("(t p) c -> p t c", p=P)[:, tok, :]
                        for dst, src in ((F_HM[s][:, 0:512], rows(att)), (F_HM[s][:, 512:1024], rows(scans[0])),
                                         (F_SB[s], rows(scans[1])),
                                         (F_G[s][:, 0:256], rows(proj)[:, COL["gr"]:COL["gr"] + 256]),
                                         (F_G[s][:, 256:512], rows(proj)[:, COL["rg"]:COL["rg"] + 256])):
                            sp.dma_start(dst, src).then_inc(sem(f"fin_in{s}"), 16)
                handover("sp", sp)

            def project_back(l, block=None):
                per, kk, _, _, w_at, units, _, _, _ = back(l, block)
                w = t["w_out"] if block is None else t["ffn_out"]
                with sp.Fori(0, KD) as c:
                    for j in range(per):
                        sp.wait_ge(sem("wb_ready"), units + per * c + j + 1)
                        sp.dma_start(region(w_at, kk * P), w[l, c, :, j * kk * P:(j + 1) * kk * P]
                                     ).then_inc(sem("wb_in"), 16)
                handover("sp", sp)

            def hidden(l, block):
                with sp.Fori(0, KH) as u:
                    for half in range(2):
                        sp.wait_ge(sem(f"wf_ready{half}"), block[0] * KH + u + 1)
                        sp.dma_start(region(WF[half][0], KD * P), t["ffn_in"][l, u, half]
                                     ).then_inc(sem(f"wf_in{half}"), 16)
                handover("sp", sp)

            first_modulation()
            norm(0)
            for l in range(DEPTH):
                project(l)
                prepare(l)
                for g in range(2):
                    handover("sp", sp)
                    scan(l, g)
                attend(l)
                finish(l)
                project_back(l)
                norm(2 * l + 1)
                for block_ in blocks(l):
                    hidden(l, block_)
                    project_back(l, block_)
                norm(2 * l + 2)

        @block.tensor
        def _(pe):
            mm = nc.tensor.matmul

            def mm3(out, a, b, start, stop):
                mm(out, a[0], b[0], start=start, stop=False)
                mm(out, a[0], b[1], start=False, stop=False)
                return mm(out, a[1], b[0], start=False, stop=stop)
            free("pe", pe)
            pe.wait_ge(sem("const_in"), 16 * 9)
            pe.wait_ge(sem("const_set"), 1)

            def modulation_rows(b, w):
                for k in range(KD):
                    last = mm(bank(b, parts=2), sil[:, 2 * k:2 * k + 2], w[:, k, :], start=(k == 0), stop=(k == KD - 1))
                return last

            def modulation_turn(b, rows, n_m):
                for m in range(n_m):
                    last = nc.tensor.transpose(bank(b)[:, 2 * m:2 * m + 2], rows[:, m * P:(m + 1) * P], ident[0:2, 0:2])
                return last

            def first_modulation():
                pe.wait_ge(sem("sil_ready"), 1)
                for c in range(ADA_FIRST // ADA_M):
                    pe.wait_ge(sem(f"ada0_in{c}"), 16)
                    modulation_rows(c, region(R_H + c * ADA_M * D, KD, BANK)).then_inc(sem("ada0_made"), 1)
                pe.wait_ge(sem("ada0_kept"), ADA_FIRST // ADA_M)
                modulation_turn(4, ADA_ROWS0, ADA_FIRST).then_inc(sem("ada0_turned"), 1)
                handover("pe", pe)

            def norm(i):
                n = NORMS[i]
                c0 = n["c0"]
                for pas in range((n["y"] is not None) + (n["pre"] is not None)):
                    if pas:
                        pe.wait_ge(sem("rstd_ready"), rs_count[i] + pas)
                    for k in range(KD):
                        at = sq_count[i] + pas * KD + k
                        pe.wait_ge(sem("sq_ready"), at + 1)
                        for c, w in spans(c0):
                            last = mm(psum[:, c - c0:c - c0 + w], ones[:], region(N_SQ, 2, N)[:, k % 2, c:c + w],
                                      start=(k == 0), stop=(k == KD - 1))
                        last.then_inc(sem("sq_read"), 1)
                handover("pe", pe)

            def project(l):
                h = [region_r(at, KD, N) for at in (H_HI, H_LO)]
                with pe.Fori(0, IN_CHUNKS // 2) as u:
                    for s in range(2):
                        w = [region_r(at + s * KD * IN_C, KD, IN_C) for at in (WIN_HI, WIN_LO)]
                        pe.wait_ge(sem("win_ready"), l * IN_CHUNKS + 2 * u + s + 1)
                        for tt in range(NT):
                            n, par = 5 * s + tt // 2, tt % 2
                            pe.wait_ge(sem(f"in_kept{par}"), l * 40 + u * 10 + n + 1)
                            for k in range(KD):
                                last = mm3(bank(2 * par + n % 2, IN_C), [x[:, k, tt * P:(tt + 1) * P] for x in h],
                                           [x[:, k, :] for x in w], start=(k == 0), stop=(k == KD - 1))
                            last.then_inc(sem(f"in_made{par}"), 1)
                handover("pe", pe)

            def prepare(l):
                pe.wait_ge(sem("small_in"), 160 * (l + 1))
                with pe.Fori(0, NT // 2) as u:
                    for s in range(2):
                        T = l * NT + 2 * u + s
                        tile = T_IN[s]
                        pe.wait_ge(sem(f"tile_in{s}"), 16 * (l * (NT // 2) + u + 1))
                        pe.wait_ge(sem("roped"), T + 3)
                        pe.wait_ge(sem("qn_ready"), T + 3)
                        pe.wait_ge(sem("kept0"), T + 1)
                        pe.wait_ge(sem("kept12"), T + 1)
                        rd = T_RD.rearrange("p (j h) d -> p j (h d)", j=4)
                        rr = T_RR.rearrange("p (j h) d -> p j (h d)", j=2)
                        for j in range(4):
                            nc.tensor.transpose(bank(0)[:, j * P:(j + 1) * P], rd[:, j, :], ident[:])
                        gsrc = [tile[:, COL["gq"]:COL["gq"] + P], tile[:, COL["gk"]:COL["gk"] + P], rr[:, 0, :], rr[:, 1, :]]
                        for j in range(4):
                            nc.tensor.transpose(bank(1)[:, j * P:(j + 1) * P], gsrc[j], ident[:])
                        for j in range(3):
                            nc.tensor.transpose(bank(2)[:, j * P:(j + 1) * P], T_QN[:, j, :], ident[:])
                        nc.tensor.transpose(bank(2)[0:2 * GR, 3 * P:4 * P], tile[:, COL["gf"]:COL["gf"] + 2 * GR], ident[:]
                                            ).then_inc(sem("turned1"), 1)
                        pe.wait_ge(sem("kept12"), T + 2)
                        pe.wait_ge(sem("mq_ready"), T + 1)
                        pe.wait_ge(sem("mk_ready"), T + 1)
                        for k in range(2):
                            mm(bank(3, NH * MQ), T_QNT[:, k, :], wuq[:, k, :], start=(k == 0), stop=(k == 1))
                        mm(bank(4), T_QNT[:, 2, :], wukv, start=True, stop=True)
                        for d in range(2):
                            last = mm(bank(5)[:, d * P:(d + 1) * P], wgate[:, d, :], T_GT, start=True, stop=True)
                        last.then_inc(sem("made2"), 1)
                        pe.wait_ge(sem("mq_ready"), T + 2)
                        pe.wait_ge(sem("mk_ready"), T + 2)
                        pe.wait_ge(sem("kept6"), T + 1)
                        pe.wait_ge(sem("kept7"), T + 1)
                        for b, src in ((6, T_MQ), (7, T_MK)):
                            for h in range(NH):
                                last = nc.tensor.transpose(bank(b)[0:MQ, h * P:(h + 1) * P], src[:, h, :], ident[:])
                        last.then_inc(sem("turned3"), 1)
                handover("pe", pe)

            def scan(l, g):
                inst = 2 * l + g
                for a, b in SCANS:
                    with pe.Fori(0, (b - a) // 2) as pair:
                        i = a + 2 * pair
                        for p in range(2):
                            n = inst * NC + i + p
                            for d in range(2):
                                pe.wait_ge(sem(f"est_ready{d}"), n + 1)
                                pe.wait_ge(sem(f"scm_ready{d}"), n + 1)
                                mm(bank(d, NH * CH, CH), EST[d][p][:, KS, :], QBD[d][p].rearrange("p h i -> p (h i)"),
                                   start=True, stop=True).then_inc(sem(f"sc_made{d}"), 1)
                                pe.wait_ge(sem(f"kd_kept{d}"), n + 1)
                                nc.tensor.transpose(bank(2 + d, P), EST[d][p][:, KDE:QD + 1, :].rearrange("p a b -> p (a b)"), ident[:]
                                                    ).then_inc(sem(f"kd_turned{d}"), 1)
                            for d in range(2):
                                pe.wait_ge(sem(f"state_ready{d}"), n + inst + 1)
                                pe.wait_ge(sem(f"o_kept{d}"), n + 1)
                                mm(bank(4 + d, NH * HD, CH), EST[d][p][:, QD, :], STATE[d], start=True, stop=False,
                                   skip_group_check=True)
                            for d in range(2):
                                pe.wait_ge(sem(f"v_in{d}{p}"), 16 * (inst * (NC // 2) + a // 2 + pair + 1))
                                pe.wait_ge(sem(f"kd_kept{d}"), n + 2)
                                pe.wait_ge(sem(f"scm_ready{d}"), n + 2)
                                mm(bank(6 + d, NH * HD), KDT[d], V[d][p], start=True, stop=True
                                   ).then_inc(sem(f"u_made{d}"), 1)
                            for d in range(2):
                                for h in range(NH):
                                    last = mm(bank(4 + d, NH * HD, CH)[:, h * HD:(h + 1) * HD], SCM[d][:, h, :],
                                              V[d][p][:, h * HD:(h + 1) * HD], start=False, stop=(h == NH - 1),
                                              skip_group_check=True)
                                last.then_inc(sem(f"o_made{d}"), 1)
                handover("pe", pe)

            def attend(l):
                for first, count, base, nk in att_loops(l):
                    def scores(m, i):
                        M0 = (base + i) * MAPS
                        if m == 0:
                            pe.wait_ge(sem("qd_staged"), base + i + 1)
                        if m == 2 * NH:
                            pe.wait_ge(sem("qm_staged"), base + i + 1)
                        pe.wait_ge(sem("head_done"), M0 + m + 1)
                        if m < 2 * NH:
                            at = DK * (m % 4)
                            q, k = A_QD[at:at + DK, m // 4, :], region(R_QKD, 4, N)[at:at + DK, 2 + m // 4, :]
                        else:
                            q, k = A_QM[:, m - 8, :], region(R_KM, 4, N, parts=MQ)[:, m - 8, :]
                        waits = True
                        for c, w, n, tail in score_pieces(nk):
                            if tail and waits:
                                pe.wait_ge(sem("exp_done"), M0 + m + 1)
                                waits = False
                            mm(psum[:, c:c + w], q, k[:, c:c + w], start=True, stop=True).then_inc(sem("scored"), n)

                    def turn_probs(i, o):
                        T = base + i
                        if o < NH:
                            pe.wait_ge(sem("maps_joined"), NH * T + o + 1)
                        else:
                            pe.wait_ge(sem("exp_done"), T * MAPS + NH + o + 2)
                        pe.wait_ge(sem("pt_act"), OUTS * T + o + 1)
                        pe.wait_ge(sem("pt_dve"), OUTS * T + o + 1)
                        src = A_P[2 * (o % 2) if o < NH else o % 4]
                        for kt in range(nk):
                            at = TURNED + kt * P if nk == NT else TURNED + kt * BANK
                            last = nc.tensor.transpose(psum[:, at:at + P], src[:, kt * P:(kt + 1) * P], ident[:])
                        last.then_inc(sem("turned"), 1)

                    def values(i, o):
                        n = OUTS * (base + i) + o
                        pe.wait_ge(sem("pt_act"), n + 2)
                        pe.wait_ge(sem("pt_dve"), n + 2)
                        pe.wait_ge(sem("att_kept"), n + 1)
                        v = region(R_VD if o < NH else R_VM, NT, 256)
                        h = o % NH
                        for kt in range(nk):
                            last = mm(bank(6 + o % 2, HD), A_PT[o % 2][:, kt, :], v[:, kt, h * HD:(h + 1) * HD],
                                      start=(kt == 0), stop=(kt == nk - 1))
                        last.then_inc(sem("pv_made"), 1)

                    def step(m, i, of_values, of_turn):
                        if i is not None:
                            scores(m, i)
                        if of_values:
                            values(*of_values)
                        if of_turn:
                            turn_probs(*of_turn)
                    att_tiles(pe, count, step)
                handover("pe", pe)

            def finish(l):
                c0, count, base = fin_loop(l)
                with pe.Fori(0, count // 2) as u:
                    for s in range(2):
                        if l == 0:
                            pe.wait_ge(sem(f"ada_in{s}"), 16 * ADA_T * (u + 1))
                            pe.wait_ge(sem("rows_kept"), 2 * u + s + 1)
                            for j in range(ADA_T):
                                last = modulation_rows(4 + j, F_ADA[s][:, j])
                            last.then_inc(sem("rows_made"), 1)
                        pe.wait_ge(sem("fin_ready"), 2 * base + 2 * u + s + 2)
                        if l == 0:
                            pe.wait_ge(sem("rows_kept"), 2 * u + s + 2)
                            pe.wait_ge(sem("ada_kept"), 2 * u + s + 1)
                        pe.wait_ge(sem(f"fin_kept_a{s}"), base + u + 1)
                        pe.wait_ge(sem(f"fin_kept_v{s}"), base + u + 1)
                        for k in range(KD):
                            last = nc.tensor.transpose(bank(2 * s + k // 4)[:, (k % 4) * P:(k % 4 + 1) * P],
                                                       F_HM[s][:, k * P:(k + 1) * P], ident[:])
                        last.then_inc(sem(f"fin_turned{s}"), 1)
                        if l == 0:
                            modulation_turn(6, F_ROWS, ADA_T * ADA_M).then_inc(sem("rows_turned"), 1)
                handover("pe", pe)

            def project_back(l, block=None):
                per, kk, src_at, _, w_at, units, chunks, t0, n = back(l, block)
                src = [region_r(at, KD if per == 1 else KH, N if per == 1 else FFN_T) for at in src_at]
                pieces = spans(t0) if per == 1 else [(0, n)]
                first = t0 if per == 1 else 0
                _, hi, lo = unit_slots(w_at)
                with pe.Fori(0, KD // 2) as u:
                    for s in range(2):
                        for j in range(per):
                            slot = j if per == 2 else s
                            w = [region_r(at, kk, P) for at in (hi[slot], lo[slot])]
                            pe.wait_ge(sem("wb_ready"), units + per * (2 * u + s) + j + 2)
                            if j == 0:
                                pe.wait_ge(sem("yb_kept"), chunks + 2 * u + s + 1)
                            for a, m in pieces:
                                out = psum[:, 3 * s * BANK + a - first:3 * s * BANK + a - first + m]
                                for k in range(kk):
                                    last = mm3(out, [x[:, k, :] for x in w], [x[:, j * kk + k, a:a + m] for x in src],
                                               start=(j == 0 and k == 0), stop=(j == per - 1 and k == kk - 1))
                            last.then_inc(sem("yb_made"), 1)
                handover("pe", pe)

            def hidden(l, block):
                index, t0, n = block
                h = [region_r(at, KD, N) for at in (H_HI, H_LO)]
                with pe.Fori(0, KH) as u:
                    for half in range(2):
                        w = [region_r(at, KD, P) for at in WF[half][1:]]
                        pe.wait_ge(sem(f"wf_ready{half}"), index * KH + u + 2)
                        pe.wait_ge(sem("up_done" if half else "silu_done"), index * KH + u + 1)
                        for k in range(KD):
                            last = mm3(bank(half, n), [x[:, k, :] for x in w], [x[:, k, t0:t0 + n] for x in h],
                                       start=(k == 0), stop=(k == KD - 1))
                        last.then_inc(sem("up_made" if half else "gate_made"), 1)
                handover("pe", pe)

            first_modulation()
            norm(0)
            for l in range(DEPTH):
                project(l)
                prepare(l)
                for g in range(2):
                    handover("pe", pe)
                    scan(l, g)
                attend(l)
                finish(l)
                project_back(l)
                norm(2 * l + 1)
                for block_ in blocks(l):
                    hidden(l, block_)
                    project_back(l, block_)
                norm(2 * l + 2)

        @block.scalar
        def _(act):
            activation = nc.scalar.activation
            free("act", act)
            act.wait_ge(sem("const_in"), 16 * 9)
            act.wait_ge(sem("const_set"), 1)
            activation(sil[:], sil_in[:], ACT.Silu).then_inc(sem("sil_ready"), 1)

            def first_modulation():
                for c in range(ADA_FIRST // ADA_M):
                    act.wait_ge(sem("ada0_made"), c + 1)
                    nc.scalar.copy(ADA_ROWS0[:, c * BANK:(c + 1) * BANK], bank(c, parts=2)
                                   ).then_inc(sem("ada0_kept"), 1)
                handover("act", act)

            def norm(i):
                n = NORMS[i]
                c0 = n["c0"]
                at, rs = sq_count[i], rs_count[i]
                for pas, (src_at, last) in enumerate(([(n["y"], False)] if n["y"] is not None else []) +
                                                     ([(X_AT, True)] if n["pre"] is not None else [])):
                    for k in range(KD):
                        if src_at == X_AT:
                            if n["y"] is None:
                                act.wait_ge(sem(f"x_in{k}"), 16 * (i + 1))
                            else:
                                act.wait_ge(sem("x_new"), (i - 1) * KD + k + 1)
                        if k >= 2 or pas:
                            act.wait_ge(sem("sq_read"), at + pas * KD + k - 1)
                        activation(region(N_SQ, 2, N)[:, k % 2, c0:N], region(src_at, KD, N)[:, k, c0:N], ACT.Square
                                   ).then_inc(sem("sq_ready"), 1)
                    act.wait_ge(sem("sq_read"), at + pas * KD + KD)
                    r = region(N_RS + pas * N, N)
                    activation(r[:, c0:N], psum[:, 0:N - c0], ACT.Ln, scale=1.0 / D, bias=eps[:, 0:1])
                    act.drain()
                    activation(r[:, c0:N], r[:, c0:N], ACT.Exp, scale=-0.5).then_inc(sem("rstd_ready"), 1)
                if n["pre"] is not None:
                    for k in range(KD):
                        act.wait_ge(sem("h_normed"), KD * i + k + 1)
                        hk, hi = region(R_H, KD, N)[:, k, :], region_r(H_HI, KD, N)[:, k, :]
                        m = mods_v[:, n["pre_layer"]]
                        for dst in (hi, hk):
                            for st, a, b in streams(c0):
                                last = activation(dst[:, a:b], hk[:, a:b], ACT.Identity, bias=m[:, n["pre"], k, st:st + 1],
                                                  scale=m[:, n["pre"] + 1, k, st:st + 1])
                        last.then_inc(sem("h_made"), 1)
                handover("act", act)

            def project(l):
                def part(c, s):
                    act.wait_ge(sem(f"win_in{s}"), 16 * (l * (IN_CHUNKS // 2) + c + 1))
                    nc.scalar.copy(region_r(WIN_HI + s * KD * IN_C, KD * IN_C), region(WIN_LO + s * KD * IN_C, KD * IN_C)
                                   ).then_inc(sem("win_hi"), 1)

                def chunk(u, s, is_last):
                    for j in range(5):
                        n = 5 * s + j
                        if j == 2 and not is_last:
                            part(u + s, 1 - s)
                        act.wait_ge(sem("in_made0"), l * 40 + u * 10 + n + 1)
                        if j == 0:
                            act.wait_ge(sem("proj_out"), 16 * (l * IN_CHUNKS + 2 * u + s + 1))
                        nc.scalar.copy(region(WIN_OUT, NT, IN_C)[:, 2 * j, :], bank(n % 2, IN_C)
                                       ).then_inc(sem("in_kept0"), 1)
                    for par in range(2):
                        act.wait_ge(sem(f"in_kept{par}"), l * 40 + u * 10 + 5 * (s + 1) + 2)
                    act.dma_start(proj.rearrange("(t p) (c w) -> p t c w", p=P, w=IN_C)[:, :, 2 * u + s, :],
                                  region(WIN_OUT, NT, IN_C)).then_inc(sem("proj_out"), 16)
                part(0, 0)
                with act.Fori(0, IN_CHUNKS // 2 - 1) as u:
                    for s in range(2):
                        chunk(u, s, False)
                for s in range(2):
                    chunk(IN_CHUNKS // 2 - 1, s, s == 1)
                act.wait_ge(sem("proj_out"), 16 * (IN_CHUNKS * (l + 1) + 1))
                handover("act", act)

            def prepare(l):
                act.wait_ge(sem("small_in"), 160 * (l + 1))
                act.wait_ge(sem("dec_abs"), l + 1)
                activation(dec_t[:], dec_t[:], ACT.Exp, scale=-1.0)
                act.drain()
                activation(dec_t[:], dec_t[:], ACT.Ln, bias=1.0)
                activation(lam_e[:], lam_s[:], ACT.Exp).then_inc(sem("dec_ln"), 1)
                with act.Fori(0, NT // 2) as u:
                    for s in range(2):
                        T = l * NT + 2 * u + s
                        tok = 2 * u + s
                        tile = T_IN[s]
                        mq, mkv = tile[:, COL["mq"]:COL["mq"] + QR], tile[:, COL["mkv"]:COL["mkv"] + KVR]
                        qn = T_QN.rearrange("p j d -> p (j d)")
                        act.wait_ge(sem(f"tile_in{s}"), 16 * (l * (NT // 2) + u + 1))
                        act.wait_ge(sem("turned1"), T + 2)
                        activation(qn[:, 0:QR], mq, ACT.Square, accum_out=T_SS[:, 0:1])
                        activation(qn[:, QR:QR + KVR], mkv, ACT.Square, accum_out=T_SS[:, 1:2])
                        act.drain()
                        activation(T_RS[:, 0:1], T_SS[:, 0:1], ACT.Ln, scale=1.0 / QR, bias=eps[:, 0:1])
                        activation(T_RS[:, 1:2], T_SS[:, 1:2], ACT.Ln, scale=1.0 / KVR, bias=eps[:, 0:1])
                        act.drain()
                        activation(T_RS[:], T_RS[:], ACT.Exp, scale=-0.5)
                        act.drain()
                        nc.scalar.mul(qn[:, 0:QR], mq, T_RS[:, 0:1])
                        nc.scalar.mul(qn[:, QR:QR + KVR], mkv, T_RS[:, 1:2]).then_inc(sem("qn_ready"), 1)

                        act.wait_ge(sem("turned1"), T + 3)
                        nc.scalar.copy(region(R_GR, 4, NT, P)[:, :, tok, :], bank(1).rearrange("p (j c) -> p j c", j=4))
                        act.wait_ge(sem("made2"), T + 1)
                        for j in range(2):
                            nc.scalar.mul(T_QNT[:, j, :], bank(2)[:, j * P:(j + 1) * P], qnorm[:, j:j + 1])
                        nc.scalar.mul(T_QNT[:, 2, :], bank(2)[:, 2 * P:3 * P], kvnorm[:, 0:1])
                        nc.scalar.copy(T_GT, bank(2)[0:2 * GR, 3 * P:4 * P]).then_inc(sem("kept12"), 1)

                        act.wait_ge(sem("made2"), T + 2)
                        act.wait_ge(sem("turned3"), T + 1)
                        kv = bank(4).rearrange("p (h d) -> p h d", h=NH)
                        nc.scalar.copy(T_MK[:, :, 0:HD], kv[:, :, 0:HD])
                        nc.scalar.copy(region(R_VM, NT, NH, HD)[:, tok, :, :], kv[:, :, HD:2 * HD])
                        for d in range(2):
                            last = activation(region(R_GZ, 2, NT, P)[:, d, tok, :], bank(5)[:, d * P:(d + 1) * P],
                                              ACT.Identity, bias=bgate[:, d:d + 1])
                        last.then_inc(sem("mk_ready"), 1)

                        act.wait_ge(sem("turned3"), T + 2)
                        nc.scalar.copy(region(R_KM, 4, NT, P, parts=MQ)[:, :, tok, :],
                                       bank(7, parts=MQ).rearrange("p (j c) -> p j c", j=4)).then_inc(sem("kept7"), 1)
                handover("act", act)

            def scan_factors(l, g):
                if g == 0:
                    act.wait_ge(sem("gate_abs"), l + 1)
                    a, b = region(R_H, 2 * N), region(R_H + 2 * N, 2 * N)
                    activation(b, a, ACT.Exp, scale=-1.0)
                    act.drain()
                    activation(b, b, ACT.Ln, bias=1.0).then_inc(sem("gate_ln"), 1)
                    for d in range(2):
                        act.wait_ge(sem("exponents"), 2 * l + d + 1)
                        sign = 1.0 if d == 0 else -1.0
                        x1, x2, x3 = (x.rearrange("p (c i) -> p c i", c=NC) for x in (T1, T2, T3))
                        activation(E[d][:, :, QS, :], x2, ACT.Exp, scale=sign)
                        activation(E[d][:, :, KS, :], x2, ACT.Exp, scale=-sign)
                        if d == 0:
                            activation(E[d][:, :, QD, :], x1, ACT.Exp)
                            activation(E[d][:, :, KDE, :], x3, ACT.Exp, scale=-1.0)
                        else:
                            activation(E[d][:, :, QD, :], x3, ACT.Exp, scale=-1.0)
                            activation(E[d][:, :, KDE, :], region(R_GZ, 2, NC, CH)[:, 1], ACT.Exp)
                        activation(dec_v[:, d, :], x1[:, :, CH - 1], ACT.Exp).then_inc(sem("factors"), 1)
                else:
                    act.wait_ge(sem("log_dec_ready"), l + 1)
                    for d in range(2):
                        for h in range(NH):
                            activation(mask[:, (d * NH + h) * CH:(d * NH + h + 1) * CH], rel[:, d * CH:(d + 1) * CH],
                                       ACT.Exp, scale=log_dec[0:CH, d * NH + h:d * NH + h + 1])
                        activation(edge[:, 2 * d * CH:2 * (d + 1) * CH], steps[:, 2 * d * CH:2 * (d + 1) * CH], ACT.Exp,
                                   scale=log_dec[:, 8 + d:9 + d])
                        last = activation(dec_v[:, d, :], log_dec[:, 8 + d:9 + d].to_broadcast([P, NC]), ACT.Exp,
                                          scale=float(CH))
                    last.then_inc(sem("ret_factors"), 1)
                handover("act", act)

            def scan(l, g):
                inst = 2 * l + g
                for a, b in SCANS:
                    with act.Fori(0, (b - a) // 2) as pair:
                        i = a + 2 * pair
                        for p in range(2):
                            n = inst * NC + i + p
                            for d in range(2):
                                act.wait_ge(sem(f"kd_turned{d}"), n + 1)
                                act.wait_ge(sem(f"u_made{d}"), n + 1)
                                nc.scalar.copy(KDT[d], bank(2 + d, P, CH)).then_inc(sem(f"kd_kept{d}"), 1)
                            for d in range(2):
                                act.wait_ge(sem(f"o_made{d}"), n + 3)
                                nc.scalar.copy(in_turn(region(R_O, NC, 256)[d * CH:(d + 1) * CH], d, a, b)[:, 2 * pair + p, :], bank(4 + d, 256, CH)
                                               ).then_inc(sem(f"o_kept{d}"), 1)
                handover("act", act)

            def attend(l):
                for first, count, base, nk in att_loops(l):
                    def step(m, i, of_values, of_turn):
                        if i is not None:
                            T = base + i
                            act.wait_ge(sem("max_ready"), MAPS * T + m + 1)
                            act.wait_ge(sem("turned"), OUTS * T + (m + 1 if m < 4 else (m - 4) // 2 + 5))
                            for j, name in enumerate(("head_done", "exp_done")):
                                a, b = exp_parts(nk)[j:j + 2]
                                activation(A_P[m % 4][:, a:b], psum[:, a:b], ACT.Exp, bias=A_NM[:, m:m + 1],
                                           accum_out=A_L[:, m, j:j + 1]).then_inc(sem(name), 1)
                        if of_turn:
                            n, o = OUTS * (base + of_turn[0]) + of_turn[1], of_turn[1]
                            act.wait_ge(sem("turned"), n + 5)
                            act.wait_ge(sem("pv_made"), n + 1)
                            w = 4 if nk == NT else 1
                            nc.scalar.copy(A_PT[o % 2][:, 0:w, :].rearrange("p a b -> p (a b)"),
                                           psum[:, TURNED:TURNED + w * P]).then_inc(sem("pt_act"), 1)
                    att_tiles(act, count, step)
                handover("act", act)

            def finish(l):
                c0, count, base = fin_loop(l)
                with act.Fori(0, count // 2) as u:
                    for s in range(2):
                        T = 2 * base + 2 * u + s
                        tok = c0 + 2 * u + s
                        act.wait_ge(sem("fin_sum"), T + 1)
                        act.wait_ge(sem("fin_ready"), T + 1)
                        activation(F_SQ, F_HM[s], ACT.Square).then_inc(sem("fin_sq"), 1)
                        activation(F_SG, F_G[s], ACT.Silu)
                        act.wait_ge(sem("fin_ss"), T + 1)
                        activation(F_RS, F_SS, ACT.Ln, scale=1.0 / HD, bias=eps[:, 0:1])
                        act.drain()
                        activation(F_RS, F_RS, ACT.Exp, scale=-0.5).then_inc(sem("fin_rs"), 1)
                        if l == 0:
                            act.wait_ge(sem("rows_made"), 2 * u + s + 3)
                            act.wait_ge(sem("rows_turned"), 2 * u + s + 1)
                            nc.scalar.copy(F_ROWS, psum[0:2, 4 * BANK:(4 + ADA_T) * BANK]).then_inc(sem("rows_kept"), 1)
                        act.wait_ge(sem(f"fin_turned{s}"), base + u + 2)
                        for b in range(2):
                            last = nc.scalar.copy(region_r(MIX_HI, KD, NT, P)[:, 4 * b:4 * b + 4, tok, :],
                                                  bank(2 * s + b).rearrange("p (j c) -> p j c", j=4))
                        last.then_inc(sem(f"fin_kept_a{s}"), 1)
                handover("act", act)

            def project_back(l, block=None):
                per, kk, _, dst_at, w_at, units, chunks, t0, n = back(l, block)
                raw, hi, _ = unit_slots(w_at)

                def chunk(c, s, is_first):
                    for j in range(per):
                        m = units + per * c + j
                        act.wait_ge(sem("wb_in"), 16 * (m + 1))
                        act.wait_ge(sem("yb_made"), m + 1)
                        nc.scalar.copy(region_r(hi[j if per == 2 else s], kk * P), region(raw, kk * P)
                                       ).then_inc(sem("wb_hi"), 1)
                    if not is_first:
                        keep(c - 1, 1 - s)

                def keep(c, s):
                    act.wait_ge(sem("yb_made"), units + per * (c + 1) + 2)
                    nc.scalar.copy(region(dst_at, KD, N)[:, c, t0:t0 + n], psum[:, 3 * s * BANK:3 * s * BANK + n]
                                   ).then_inc(sem("yb_kept"), 1)
                for s in range(2):
                    chunk(s, s, s == 0)
                with act.Fori(1, KD // 2) as u:
                    for s in range(2):
                        chunk(2 * u + s, s, False)
                keep(KD - 1, 1)
                handover("act", act)

            def hidden(l, block):
                index, t0, n = block

                def part(u, half):
                    act.wait_ge(sem(f"wf_in{half}"), 16 * (index * KH + u + 1))
                    act.wait_ge(sem("up_made" if half else "gate_made"), index * KH + u + 1)
                    nc.scalar.copy(region_r(WF[half][1], KD * P), region(WF[half][0], KD * P)
                                   ).then_inc(sem(f"wf_hi{half}"), 1)

                def gate(u):
                    act.wait_ge(sem("gate_made"), index * KH + u + 2)
                    act.wait_ge(sem("up_done"), index * KH + u + 1)
                    activation(region(SILU_AT, n), bank(0, n), ACT.Silu).then_inc(sem("silu_done"), 1)

                def product_part(u):
                    act.wait_ge(sem("up_done"), index * KH + u + 2)
                    nc.scalar.copy(region_r(ACT_HI, KH, FFN_T)[:, u, 0:n], region(ACT_LO, KH, FFN_T)[:, u, 0:n]
                                   ).then_inc(sem("act_hi"), 1)
                part(0, 0)
                part(0, 1)
                with act.Fori(1, KH) as u:
                    part(u, 0)
                    gate(u - 1)
                    part(u, 1)
                    product_part(u - 1)
                gate(KH - 1)
                product_part(KH - 1)
                handover("act", act)

            first_modulation()
            norm(0)
            for l in range(DEPTH):
                project(l)
                prepare(l)
                for g in range(2):
                    scan_factors(l, g)
                    scan(l, g)
                attend(l)
                finish(l)
                project_back(l)
                norm(2 * l + 1)
                for block_ in blocks(l):
                    hidden(l, block_)
                    project_back(l, block_)
                norm(2 * l + 2)

        @block.vector
        def _(dve):
            v = nc.vector
            free("dve", dve)
            v.memset(eps[:], EPS)
            v.memset(ones[:], 1.0).then_inc(sem("const_set"), 1)
            dve.wait_ge(sem("const_in"), 16 * 9)

            def keep_modulation(src, first, n_m):
                return v.tensor_tensor(mods_f[:, bass.ds(first, n_m), :], src.rearrange("p (m s) -> p m s", s=2),
                                       ada_b[:, bass.ds(first, n_m)].unsqueeze(2).to_broadcast([P, n_m, 2]), ALU.add)

            def with_gain(l, row, gain):
                for st in range(2):
                    m = mods_v[:, l, row, :, st]
                    if row % 3 == 1:
                        v.scalar_tensor_tensor(out=m, in0=m, scalar=1.0, in1=gains_v[:, l, gain, :], op0=ALU.add, op1=ALU.mult)
                    else:
                        v.tensor_tensor(m, m, gains_v[:, l, gain, :], ALU.mult)

            def first_modulation():
                dve.wait_ge(sem("ada0_turned"), 1)
                keep_modulation(bank(4, 2 * ADA_FIRST), 0, ADA_FIRST)
                dve.drain()
                with_gain(0, 1, 0)
                handover("dve", dve)

            def rest(lo, x, hi):
                return v.tensor_tensor(lo, x, hi.bitcast(F32), ALU.subtract)

            def rest_of_h(i, k, c0):
                dve.wait_ge(sem("h_made"), KD * i + k + 1)
                rest(region_r(H_LO, KD, N)[:, k, c0:N], region(R_H, KD, N)[:, k, c0:N],
                     region_r(H_HI, KD, N)[:, k, c0:N])

            def norm(i):
                n = NORMS[i]
                c0 = n["c0"]
                x, h = region(X_AT, KD, N), region(R_H, KD, N)
                if n["y"] is not None:
                    y, r = region(n["y"], KD, N), region(N_RS, N)
                    dve.wait_ge(sem("rstd_ready"), rs_count[i] + 1)
                    for k in range(KD):
                        tmp = region(N_TMP, 2, N)[:, k % 2, :]
                        v.tensor_tensor(tmp[:, c0:N], y[:, k, c0:N], r[:, c0:N], ALU.mult)
                        dve.wait_ge(sem(f"x_in{k}"), 16 * (i + 1))
                        dve.drain()
                        for st, a, b in streams(c0):
                            last = v.scalar_tensor_tensor(out=x[:, k, a:b], in0=tmp[:, a:b],
                                                          scalar=mods_v[:, n["layer"], n["gate"], k, st:st + 1],
                                                          in1=x[:, k, a:b], op0=ALU.mult, op1=ALU.add)
                        last.then_inc(sem("x_new"), 1)
                if n["pre"] is not None:
                    pas = int(n["y"] is not None)
                    r = region(N_RS + pas * N, N)
                    dve.wait_ge(sem("rstd_ready"), rs_count[i] + pas + 1)
                    for k in range(KD):
                        dve.wait_ge(sem(f"x_in{k}"), 16 * (i + 1))
                        v.tensor_tensor(h[:, k, c0:N], x[:, k, c0:N], r[:, c0:N], ALU.mult).then_inc(sem("h_normed"), 1)
                        if k >= 1:
                            rest_of_h(i, k - 1, c0)
                    rest_of_h(i, KD - 1, c0)
                handover("dve", dve)

            def project(l):
                v.memset(wgate, 0.0).then_inc(sem("wgate_zero"), 1)

                def part(c, s):
                    dve.wait_ge(sem("win_hi"), l * IN_CHUNKS + c + 1)
                    lo = WIN_LO + s * KD * IN_C
                    rest(region_r(lo, KD * IN_C), region(lo, KD * IN_C), region_r(WIN_HI + s * KD * IN_C, KD * IN_C)
                         ).then_inc(sem("win_ready"), 1)

                def chunk(u, s, is_last):
                    for j in range(5):
                        n = 5 * s + j
                        if j == 2 and not is_last:
                            part(2 * u + s + 1, 1 - s)
                        if j == 0:
                            dve.wait_ge(sem("proj_out"), 16 * (l * IN_CHUNKS + 2 * u + s + 1))
                        dve.wait_ge(sem("in_made1"), l * 40 + u * 10 + n + 11)
                        v.tensor_copy(region(WIN_OUT, NT, IN_C)[:, 2 * j + 1, :], bank(2 + n % 2, IN_C)
                                      ).then_inc(sem("in_kept1"), 1)
                part(0, 0)
                with dve.Fori(0, IN_CHUNKS // 2 - 1) as u:
                    for s in range(2):
                        chunk(u, s, False)
                for s in range(2):
                    chunk(IN_CHUNKS // 2 - 1, s, s == 1)
                handover("dve", dve)

            def rotate(out, x, scratch, tok, nh):
                xc, xs = scratch
                half = DK // 2
                cos, sin = (rope_t[:, tok, w:w + 1, :].to_broadcast([P, nh, DK]) for w in range(2))
                v.tensor_tensor(xc, x, cos, ALU.mult)
                v.tensor_tensor(xs, x, sin, ALU.mult)
                dve.drain()
                v.tensor_tensor(out[:, :, 0:half], xc[:, :, 0:half], xs[:, :, half:DK], ALU.subtract)
                return v.tensor_tensor(out[:, :, half:DK], xc[:, :, half:DK], xs[:, :, 0:half], ALU.add)

            def prepare(l):
                dve.wait_ge(sem("small_in"), 160 * (l + 1))
                lam_q = lam_v.rearrange("p (m w d) -> p m w d", m=2, w=2)
                v.tensor_tensor(lam_p.rearrange("p (m d) -> p m d", m=2), lam_q[:, :, 0, :], lam_q[:, :, 1, :], ALU.mult)
                v.scalar_tensor_tensor(out=dec_t[:], in0=dec_in[:], scalar=-1.0, in1=dec_in[:], op0=ALU.mult, op1=ALU.max)
                dve.drain()
                v.tensor_reduce(lam_s[:], lam_p.rearrange("p (m d) -> p m d", m=2), AX.X, ALU.add
                                ).then_inc(sem("dec_abs"), 1)
                dve.wait_ge(sem("dec_ln"), l + 1)
                v.scalar_tensor_tensor(out=neg_lam[:], in0=lam_e[:, 1:2], scalar=-lambda_init(l), in1=lam_e[:, 0:1],
                                       op0=ALU.add, op1=ALU.subtract)
                v.scalar_tensor_tensor(out=log_dec[:], in0=dec_in[:], scalar=0.0, in1=dec_t[:], op0=ALU.min,
                                       op1=ALU.subtract).then_inc(sem("log_dec_ready"), 1)
                with dve.Fori(0, NT // 2) as u:
                    for s in range(2):
                        T = l * NT + 2 * u + s
                        tok = 2 * u + s
                        tile = T_IN[s]

                        def cols(name, n):
                            return tile[:, COL[name]:COL[name] + n * DK].rearrange("p (h d) -> p h d", h=n)
                        dve.wait_ge(sem(f"tile_in{s}"), 16 * (l * (NT // 2) + u + 1))
                        dve.wait_ge(sem("turned1"), T + 2)
                        rotate(T_RD, cols("dq", 16), T_S[0], tok, 16)
                        rotate(T_RM, cols("mr", 1), T_S[1], tok, 1)
                        rotate(T_RR, cols("rq", 8), T_S[2], tok, 8).then_inc(sem("roped"), 1)
                        dve.wait_ge(sem("turned1"), T + 3)
                        qk = region(R_QKD, 4, NT, P)
                        turned = bank(0).rearrange("p (j c) -> p j c", j=4)
                        v.tensor_scalar(qk[:, 0:2, tok, :], turned[:, 0:2, :], DK ** -0.5, None, ALU.mult)
                        v.tensor_copy(qk[:, 2:4, tok, :], turned[:, 2:4, :]).then_inc(sem("kept0"), 1)
                        dve.wait_ge(sem("turned3"), T + 1)
                        v.tensor_copy(T_MK[:, :, HD:MQ], T_RM.to_broadcast([P, NH, DK]))
                        dve.wait_ge(sem("made2"), T + 2)
                        q = bank(3, NH * MQ).rearrange("p (h d) -> p h d", h=NH)
                        v.tensor_copy(T_MQ[:, :, 0:HD], q[:, :, 0:HD])
                        rotate(T_MQ[:, :, HD:MQ], q[:, :, HD:MQ], T_S[3], tok, NH).then_inc(sem("mq_ready"), 1)
                        dve.wait_ge(sem("turned3"), T + 2)
                        v.tensor_scalar(region(R_QM, 4, NT, P, parts=MQ)[:, :, tok, :],
                                        bank(6, parts=MQ).rearrange("p (j c) -> p j c", j=4), MQ ** -0.5, None, ALU.mult
                                        ).then_inc(sem("kept6"), 1)
                handover("dve", dve)

            def scan_factors(l, g):
                q = region(R_GR, 4, NC, CH)[:, 2 * g]
                k = region(R_GR, 4, NC, CH)[:, 2 * g + 1]
                s = DK ** -0.5
                if g == 0:
                    z = region(R_GZ, 2 * N)
                    a, b = region(R_H, 2 * N), region(R_H + 2 * N, 2 * N)
                    v.scalar_tensor_tensor(out=a, in0=z, scalar=-1.0, in1=z, op0=ALU.mult, op1=ALU.max
                                           ).then_inc(sem("gate_abs"), 1)
                    v.memset(RESET, 1.0)
                    dve.drain()
                    v.memset(RESET.rearrange("p (c i) -> p c i", c=NC)[:, :, 0:1], 0.0)
                    v.tensor_copy(mask[:], causal[:])
                    dve.wait_ge(sem("gate_ln"), l + 1)
                    v.scalar_tensor_tensor(out=a, in0=z, scalar=0.0, in1=b, op0=ALU.min, op1=ALU.subtract)
                    dve.drain()
                    v.tensor_scalar(z, a, 1.0 / GATE_NORM, None, ALU.mult)
                    dve.drain()
                    x1, x2, x3 = (x.rearrange("p (c i) -> p c i", c=NC) for x in (T1, T2, T3))
                    for d in range(2):
                        if d:
                            dve.wait_ge(sem("factors"), 2 * l + d)
                        la = region(R_GZ, 2, N)[:, d, :]
                        v.tensor_tensor_scan(T1, RESET, la, 0.0, ALU.mult, ALU.add)
                        dve.drain()
                        if d == 0:
                            e, mid = x1, x1[:, :, CH // 2 - 1:CH // 2]
                        else:
                            v.tensor_tensor(la, T1, la, ALU.subtract)
                            dve.drain()
                            e = la.rearrange("p (c i) -> p c i", c=NC)
                            mid = e[:, :, CH // 2:CH // 2 + 1]
                        v.tensor_tensor(x2, e, mid.to_broadcast([P, NC, CH]), ALU.subtract)
                        v.tensor_tensor(x3, e, x1[:, :, CH - 1:CH].to_broadcast([P, NC, CH]), ALU.subtract)
                        dve.drain()
                        v.tensor_scalar(T2, T2, LIMIT, -LIMIT, ALU.min, ALU.max).then_inc(sem("exponents"), 1)
                        dve.wait_ge(sem("factors"), 2 * l + d + 1)
                        for j, src, f in ((QS, q, s), (KS, k, 1.0), (QD, q, s), (KDE, k, 1.0)):
                            v.scalar_tensor_tensor(out=E[d][:, :, j, :], in0=E[d][:, :, j, :], scalar=f, in1=src,
                                                   op0=ALU.mult, op1=ALU.mult)
                else:
                    dve.wait_ge(sem("ret_factors"), l + 1)
                    v.tensor_tensor(mask[:], mask[:], causal[:], ALU.mult)
                    for d in range(2):
                        eq, ek = (edge[:, (2 * d + w) * CH:(2 * d + w + 1) * CH].unsqueeze(1).to_broadcast([P, NC, CH])
                                  for w in range(2))
                        v.tensor_copy(E[d][:, :, QS, :], q)
                        v.tensor_scalar(E[d][:, :, KS, :], k, s, None, ALU.mult)
                        v.tensor_tensor(E[d][:, :, QD, :], q, eq, ALU.mult)
                        v.scalar_tensor_tensor(out=E[d][:, :, KDE, :], in0=k, scalar=s, in1=ek, op0=ALU.mult, op1=ALU.mult)
                handover("dve", dve)

            def scan(l, g):
                inst = 2 * l + g
                for d in range(2):
                    v.memset(STATE[d], 0.0).then_inc(sem(f"state_ready{d}"), 1)
                own = heads[:].unsqueeze(2).to_broadcast([P, NH, HD])
                for a, b in SCANS:
                    with dve.Fori(0, (b - a) // 2) as pair:
                        i = a + 2 * pair
                        for p in range(2):
                            n = inst * NC + i + p
                            for d in range(2):
                                dve.wait_ge(sem(f"sc_made{d}"), n + 1)
                                dve.wait_ge(sem(f"o_made{d}"), n + 2)
                                v.tensor_tensor(SCM[d].rearrange("p h i -> p (h i)"), bank(d, NH * CH, CH),
                                                mask[:, d * NH * CH:(d + 1) * NH * CH], ALU.mult
                                                ).then_inc(sem(f"scm_ready{d}"), 1)
                            for d in range(2):
                                dve.wait_ge(sem(f"u_made{d}"), n + 2)
                                v.tensor_tensor(UM[d], bank(6 + d, NH * HD).rearrange("p (h e) -> p h e", h=NH), own,
                                                ALU.mult)
                                dve.drain()
                                v.scalar_tensor_tensor(out=STATE[d], in0=STATE[d], scalar=in_turn(dec_v[:, d, :], d, a, b)[:, bass.ds(2 * pair + p, 1)],
                                                       in1=UM[d].rearrange("p h e -> p (h e)"), op0=ALU.mult, op1=ALU.add
                                                       ).then_inc(sem(f"state_ready{d}"), 1)
                handover("dve", dve)

            def attend(l):
                for first, count, base, nk in att_loops(l):
                    def join_maps(i, o):
                        dve.wait_ge(sem("exp_done"), (base + i) * MAPS + 2 * o + 3)
                        v.tensor_tensor(A_LS[:, 2 * o:2 * o + 2], A_L[:, 2 * o:2 * o + 2, 0], A_L[:, 2 * o:2 * o + 2, 1], ALU.add)
                        dve.drain()
                        v.reciprocal(A_SC[:, o:o + 1], A_LS[:, 2 * o + 1:2 * o + 2])
                        v.tensor_tensor(A_NL[:, o:o + 1], A_LS[:, 2 * o:2 * o + 1], neg_lam[:], ALU.mult)
                        dve.drain()
                        v.tensor_tensor(A_SC[:, o:o + 1], A_NL[:, o:o + 1], A_SC[:, o:o + 1], ALU.mult)
                        dve.drain()
                        a, b = (A_P[2 * (o % 2) + j][:, 0:nk * P] for j in range(2))
                        v.scalar_tensor_tensor(out=a, in0=b, scalar=A_SC[:, o:o + 1], in1=a, op0=ALU.mult, op1=ALU.add
                                               ).then_inc(sem("maps_joined"), 1)

                    def keep_values(i, o):
                        rl = A_RL[:, o:o + 1]
                        m = 2 * o if o < NH else o + NH
                        if o >= NH:
                            v.tensor_tensor(A_LS[:, m:m + 1], A_L[:, m, 0:1], A_L[:, m, 1:2], ALU.add)
                            dve.drain()
                        v.reciprocal(rl, A_LS[:, m:m + 1])
                        dve.drain()
                        dve.wait_ge(sem("pv_made"), OUTS * (base + i) + o + 3)
                        v.tensor_scalar(A_OUT[:, first + i, o * HD:(o + 1) * HD], bank(6 + o % 2, HD), rl, None, ALU.mult
                                        ).then_inc(sem("att_kept"), 1)

                    def step(m, i, of_values, of_turn):
                        if i is not None:
                            pieces = score_pieces(nk)
                            for j, (c, w, n, _) in enumerate(pieces):
                                dve.wait_ge(sem("scored"), 3 * (MAPS * (base + i) + m) + n * (j + 1))
                                v.tensor_reduce(A_CM[:, j:j + 1], psum[:, c:c + w], AX.X, ALU.max)
                            dve.drain()
                            v.tensor_reduce(A_NM[:, m:m + 1], A_CM[:, 0:len(pieces)], AX.X, ALU.max, negate=True
                                            ).then_inc(sem("max_ready"), 1)
                            if m in (2, 4, 6, 8):
                                join_maps(i, m // 2 - 1)
                        if of_values:
                            keep_values(*of_values)
                        if of_turn:
                            n, o = OUTS * (base + of_turn[0]) + of_turn[1], of_turn[1]
                            dve.wait_ge(sem("turned"), n + 5)
                            dve.wait_ge(sem("pv_made"), n + 1)
                            w0, w1 = (4, NT) if nk == NT else (1, 2)
                            v.tensor_copy(A_PT[o % 2][:, w0:w1, :].rearrange("p a b -> p (a b)"),
                                          psum[:, TURNED + BANK:TURNED + BANK + (w1 - w0) * P]).then_inc(sem("pt_dve"), 1)
                    att_tiles(dve, count, step)
                handover("dve", dve)

            def finish(l):
                c0, count, base = fin_loop(l)
                dve.wait_ge(sem("outg_in"), 16 * (l + 1))
                v.tensor_scalar(F_OUTG[:, 0:256], F_OUTG[:, 0:256], 1.0 - lambda_init(l), None, ALU.mult)
                dve.drain()
                with dve.Fori(0, count // 2) as u:
                    for s in range(2):
                        T = 2 * base + 2 * u + s
                        tok = c0 + 2 * u + s
                        hm = F_HM[s]
                        dve.wait_ge(sem(f"fin_in{s}"), 80 * (base + u + 1))
                        v.tensor_tensor(hm[:, 512:1024], hm[:, 512:1024], F_SB[s], ALU.add).then_inc(sem("fin_sum"), 1)
                        dve.wait_ge(sem("fin_sq"), T + 1)
                        v.tensor_reduce(F_SS, F_SQ.rearrange("p (h d) -> p h d", h=16), AX.X, ALU.add
                                        ).then_inc(sem("fin_ss"), 1)
                        dve.wait_ge(sem("fin_rs"), T + 1)
                        for a, b in ((0, 4), (8, 16)):
                            hv = hm[:, a * HD:b * HD].rearrange("p (h d) -> p h d", d=HD)
                            v.tensor_tensor(hv, hv, F_RS[:, a:b].unsqueeze(2).to_broadcast([P, b - a, HD]), ALU.mult)
                        dve.drain()
                        v.tensor_tensor(hm[:, 0:256], hm[:, 0:256], F_OUTG[:, 0:256], ALU.mult)
                        v.tensor_tensor(hm[:, 512:1024], hm[:, 512:1024], F_OUTG[:, 512:1024], ALU.mult)
                        dve.drain()
                        v.tensor_tensor(hm[:, 512:1024], hm[:, 512:1024], F_SG, ALU.mult).then_inc(sem("fin_ready"), 1)
                        dve.wait_ge(sem(f"fin_kept_a{s}"), base + u + 2)
                        for b in range(2):
                            last = rest(region_r(MIX_LO, KD, NT, P)[:, 4 * b:4 * b + 4, tok, :],
                                        bank(2 * s + b).rearrange("p (j c) -> p j c", j=4),
                                        region_r(MIX_HI, KD, NT, P)[:, 4 * b:4 * b + 4, tok, :])
                        last.then_inc(sem(f"fin_kept_v{s}"), 1)
                        if l == 0:
                            dve.wait_ge(sem("rows_turned"), 2 * u + s + 2)
                            n_m = ADA_T * ADA_M
                            keep_modulation(bank(6, 2 * n_m), ADA_FIRST + n_m * (2 * u + s), n_m
                                            ).then_inc(sem("ada_kept"), 1)
                if l == 0:
                    dve.drain()
                    for ll in range(DEPTH):
                        for row, gain in ((1, 0), (2, 1), (4, 2), (5, 3)):
                            if (ll, row) != (0, 1):
                                with_gain(ll, row, gain)
                handover("dve", dve)

            def project_back(l, block=None):
                per, kk, _, _, w_at, units, _, _, _ = back(l, block)
                raw, hi, lo = unit_slots(w_at)
                with dve.Fori(0, KD // 2) as u:
                    for s in range(2):
                        for j in range(per):
                            slot = j if per == 2 else s
                            dve.wait_ge(sem("wb_hi"), units + per * (2 * u + s) + j + 1)
                            rest(region_r(lo[slot], kk * P), region(raw, kk * P), region_r(hi[slot], kk * P)
                                 ).then_inc(sem("wb_ready"), 1)
                handover("dve", dve)

            def hidden(l, block):
                index, t0, n = block

                def part(u, half):
                    dve.wait_ge(sem(f"wf_hi{half}"), index * KH + u + 1)
                    raw, hi, lo = WF[half]
                    rest(region_r(lo, KD * P), region(raw, KD * P), region_r(hi, KD * P)
                         ).then_inc(sem(f"wf_ready{half}"), 1)

                def product(u):
                    dve.wait_ge(sem("up_made"), index * KH + u + 2)
                    dve.wait_ge(sem("silu_done"), index * KH + u + 2)
                    x = region(ACT_LO, KH, FFN_T)[:, u, 0:n]
                    v.tensor_tensor(x, region(SILU_AT, n), bank(1, n), ALU.mult).then_inc(sem("up_done"), 1)
                    dve.wait_ge(sem("act_hi"), index * KH + u + 1)
                    rest(region_r(ACT_LO, KH, FFN_T)[:, u, 0:n], x, region_r(ACT_HI, KH, FFN_T)[:, u, 0:n])
                part(0, 0)
                part(0, 1)
                with dve.Fori(1, KH) as u:
                    part(u, 0)
                    part(u, 1)
                    product(u - 1)
                product(KH - 1)
                handover("dve", dve)

            first_modulation()
            norm(0)
            for l in range(DEPTH):
                project(l)
                prepare(l)
                for g in range(2):
                    scan_factors(l, g)
                    scan(l, g)
                attend(l)
                finish(l)
                project_back(l)
                norm(2 * l + 1)
                for block_ in blocks(l):
                    hidden(l, block_)
                    project_back(l, block_)
                norm(2 * l + 2)

        @block.gpsimd
        def _(pool):
            def idle():
                handover("pool", pool)

            def scan(l, g):
                inst = 2 * l + g
                own = heads[:].unsqueeze(2).to_broadcast([P, NH, CH])
                for a, b in SCANS:
                    with pool.Fori(0, (b - a) // 2) as pair:
                        i = a + 2 * pair
                        for p in range(2):
                            n = inst * NC + i + p
                            for d in range(2):
                                pool.wait_ge(sem(f"o_made{d}"), n + 1)
                                nc.gpsimd.tensor_copy(EST[d][p], in_turn(E[d], d, a, b)[:, 2 * pair + p, 0:3, :])
                                nc.gpsimd.tensor_tensor(QBD[d][p], in_turn(E[d], d, a, b)[:, 2 * pair + p, QS:QS + 1, :].to_broadcast([P, NH, CH]), own,
                                                        ALU.mult).then_inc(sem(f"est_ready{d}"), 1)
                handover("pool", pool)

            def attend(l):
                for first, count, base, nk in att_loops(l):
                    def tile(i, is_first):
                        before = MAPS * (base + i)
                        if not is_first:
                            pool.wait_ge(sem("scored"), 3 * (before - NH))
                        elif before:
                            pool.wait_ge(sem("scored"), 3 * before)
                        nc.gpsimd.tensor_copy(A_QD, region(R_QKD, 4, NT, P)[:, 0:2, first + i, :]
                                              ).then_inc(sem("qd_staged"), 1)
                        if not is_first:
                            pool.wait_ge(sem("scored"), 3 * before)
                        nc.gpsimd.tensor_copy(A_QM, region(R_QM, 4, NT, P, parts=MQ)[:, :, first + i, :]
                                              ).then_inc(sem("qm_staged"), 1)
                    tile(0, True)
                    with pool.Fori(1, count) as i:
                        tile(i, False)
                handover("pool", pool)

            idle()
            idle()
            pool.wait_ge(sem("const_in"), 16 * 9)
            for l in range(DEPTH):
                idle()
                idle()
                for g in range(2):
                    idle()
                    scan(l, g)
                attend(l)
                for _ in range(4 + 2 * len(blocks(l))):
                    idle()


def constants():
    import numpy as np
    c = {"c_ident": np.eye(P, dtype=np.float32)}
    tok = np.arange(LAT)
    row, col = (tok // 64).astype(np.float32), (tok % 64).astype(np.float32)
    nf = DK // 4
    freqs = (np.float32(10000.0) ** (-np.arange(nf, dtype=np.float32) / nf)).astype(np.float32)
    ang = np.concatenate([row[:, None] * freqs, col[:, None] * freqs], -1).astype(np.float32)
    cos, sin = np.ones((N, DK), np.float32), np.zeros((N, DK), np.float32)
    cos[CTX:] = np.tile(np.cos(ang), (1, 2))
    sin[CTX:] = np.tile(np.sin(ang), (1, 2))
    both = np.stack([cos, sin], 1).reshape(NT, P, 2, DK)
    c["c_rope"] = np.ascontiguousarray(both.transpose(1, 0, 2, 3)).reshape(P, -1)
    part = np.arange(P)
    c["c_heads"] = (part[:, None] // DK == np.arange(NH)[None, :]).astype(np.float32)
    j, i = np.arange(CH)[:, None], np.arange(CH)[None, :]
    dist = np.stack([i - j, j - i], 1)
    seen = (dist >= 0).astype(np.float32)
    c["c_causal"] = np.ascontiguousarray(np.broadcast_to(seen[:, :, None, :], (CH, 2, NH, CH))).reshape(CH, -1)
    c["c_rel"] = np.maximum(dist, 0).astype(np.float32).reshape(CH, -1)
    at = np.arange(CH, dtype=np.float32)
    edges = np.stack([at + 1, CH - 1 - at, CH - at, at])
    c["c_steps"] = np.ascontiguousarray(np.broadcast_to(edges.reshape(1, -1), (P, 4 * CH)))
    return c


def laid_out(i):
    import numpy as np
    a = {k: np.asarray(v) for k, v in i.items()}

    def on_parts(w, lead):
        s = w.shape
        w = w.reshape(s[:lead] + (s[lead] // P, P) + s[lead + 1:])
        return np.moveaxis(w, lead + 1, lead)

    def chunked(w, n_chunks):
        w = on_parts(w, 1)
        w = w.reshape(w.shape[:3] + (n_chunks, -1)).transpose(0, 3, 1, 2, 4)
        return np.ascontiguousarray(w).reshape(DEPTH, n_chunks, P, -1)
    r = constants()
    r["x"] = np.ascontiguousarray(on_parts(np.concatenate([a["ctx"][0], a["x"][0]], 0).T, 0))
    r["cond"] = np.ascontiguousarray(on_parts(np.stack([a["c"][0], a["c_ctx"]], 1), 0)).reshape(P, -1)
    r["norm_g"] = np.ascontiguousarray(a["norm_g"].reshape(DEPTH, 4, KD, P).transpose(3, 0, 1, 2)).reshape(P, -1)
    r["ada_b"] = np.ascontiguousarray(a["ada_b"].reshape(DEPTH, 6 * KD, P).transpose(2, 0, 1)).reshape(P, -1)
    r["ada_w"] = chunked(a["ada_w"], 6 * KD // ADA_M).reshape(-1, P, KD * BANK)
    r["w_in"] = chunked(a["w_in"], IN_CHUNKS)
    r["w_out"] = chunked(a["w_out"], KD)
    r["ffn_out"] = chunked(a["ffn_w_out"], KD)
    g = on_parts(a["ffn_w_in"], 1).reshape(DEPTH, P, KD, 2, KH, P).transpose(0, 4, 3, 1, 2, 5)
    r["ffn_in"] = np.ascontiguousarray(g).reshape(DEPTH, KH, 2, P, -1)
    r["w_uq"] = np.ascontiguousarray(on_parts(a["mla_w_uq"], 1))
    r["w_ukv"] = a["mla_w_ukv"]
    r["w_gate"] = np.ascontiguousarray(a["gla_w_gate"].transpose(0, 2, 1, 3))
    r["b_gate"] = np.ascontiguousarray(a["gla_b_gate"].transpose(0, 2, 1))
    r["q_norm"] = np.ascontiguousarray(a["mla_q_norm"].reshape(DEPTH, 2, P).transpose(0, 2, 1))
    r["kv_norm"] = a["mla_kv_norm"].reshape(DEPTH, P, 1)
    r["decay"] = a["ret_decay"].reshape(DEPTH, 8)
    r["decay_col"] = np.ascontiguousarray(np.repeat(a["ret_decay"].transpose(0, 2, 1), DK, 1))
    r["lam"] = a["diff_lam"].reshape(DEPTH, 4 * DK)
    one = np.ones((DEPTH, 256), np.float32)
    r["out_g"] = np.concatenate([np.tile(a["diff_norm"], (1, NH)), one, np.tile(a["gla_norm"], (1, NH)),
                                 np.tile(a["ret_norm"], (1, NH))], 1)
    return r


def kernel(**inputs):
    import numpy as np
    import concourse.bacc as bacc
    from concourse.bass_utils import run_bass_kernel_spmd

    nc = bacc.Bacc("TRN2", target_bir_lowering=False, num_devices=1)
    arrays = laid_out(inputs)
    t = {n: nc.dram_tensor("in_" + n, a.shape, mybir.dt.from_np(a.dtype), kind="ExternalInput").ap() for n, a in arrays.items()}
    t["out"] = nc.dram_tensor("out_latent", (P, KD, LAT), F32, kind="ExternalOutput").ap()
    build(nc, t)
    r = run_bass_kernel_spmd(nc, [{"in_" + n: a for n, a in arrays.items()}], core_ids=[0])
    out = r.results[0]["out_latent"]
    return np.ascontiguousarray(out.transpose(2, 1, 0)).reshape(1, LAT, D)
```

```python
from contextlib import ExitStack

import concourse.bass as bass
from concourse import mybir

F32 = mybir.dt.float32
F32R = mybir.dt.float32r
ALU = mybir.AluOpType
ACT = mybir.ActivationFunctionType
AX = mybir.AxisListType

P = 128
BANK = 512
D = 1024
KD = D // P
CTX, LAT = 256, 1024
N = CTX + LAT
NT = N // P
CT = CTX // P
DEPTH = 2
NH = 4
HD = 64
DK = 32
QR, KVR = 256, 128
MQ = HD + DK
GR = 16
CH = 64
NC = N // CH
CC = CTX // CH
HID = 2816
KH = HID // P
EPS = 1e-6
GATE_NORM = 16.0
LIMIT = 80.0

SIZES = (("dq", 256), ("dk", 256), ("dv", 256), ("mq", QR), ("mkv", KVR), ("mr", DK), ("gq", 128), ("gk", 128),
         ("gv", 256), ("gr", 256), ("gf", GR), ("gb", GR), ("rq", 128), ("rk", 128), ("rv", 256), ("rg", 256))
COL = {}
IN_W = 0
for _name, _size in SIZES:
    COL[_name] = IN_W
    IN_W += _size
IN_CHUNKS = 8
IN_C = IN_W // IN_CHUNKS
ADA_FIRST = 2 * KD
ADA_M = BANK // P
ADA_T = 2

MAPS = 3 * NH
OUTS = 2 * NH

R_H = 0
R_A = KD * N
R_QKD = R_A
R_GR = R_QKD + 4 * N
R_QM = R_GR + 4 * N
R_KM = R_QM + 4 * N
R_VM = R_KM + 4 * N
R_VD = R_VM + NT * 256
R_GZ = R_VD + NT * 256
R_B = R_GZ + 2 * N
ARENA = 50048
H_LO, H_HI = R_H, R_A
MIX_LO, MIX_HI = R_H, ARENA - KD * N
FFN_T = BANK
ACT_HI = R_A + KD * N
ACT_LO = ACT_HI + KH * FFN_T
W_AT = ACT_LO + KH * FFN_T
UNIT = KH // 2 * P


def lambda_init(layer):
    import math
    return 0.8 - 0.6 * math.exp(-0.3 * layer)


def build(nc, t):
    ctx = ExitStack()
    with ctx:
        def sb(name, shape):
            return ctx.enter_context(nc.sbuf_tensor(name, shape, F32))

        made = {}

        def sem(name):
            if name not in made:
                made[name] = ctx.enter_context(nc.semaphore(name))
            return made[name]

        proj = nc.dram_tensor("proj", [N, IN_W], F32).ap()
        att = nc.dram_tensor("att", [N, 512], F32).ap()
        scans = nc.dram_tensor("scans", [2, N, 512], F32).ap()
        xdram = nc.dram_tensor("xdram", [P, KD, N], F32).ap()

        sb("arena", [P, ARENA])
        arena_at = nc.sbuf_base - 4 * ARENA
        placed = {}

        def region(start, *dims, parts=P, dtype=F32):
            size = 1
            for d in dims:
                size *= d
            assert start + size <= ARENA
            key = (start, size, dtype is F32R)
            if key not in placed:
                name = f"{'part' if dtype is F32R else 'region'}_{start}_{size}"
                placed[key] = nc.alloc_sbuf_tensor_at(name, [P, size], dtype, offset=arena_at + 4 * start)
            a = placed[key][0:parts, :]
            if len(dims) == 2:
                a = a.rearrange("p (a b) -> p a b", a=dims[0])
            if len(dims) == 3:
                a = a.rearrange("p (a b c) -> p a b c", a=dims[0], b=dims[1])
            if len(dims) == 4:
                a = a.rearrange("p (a b c d) -> p a b c d", a=dims[0], b=dims[1], c=dims[2])
            return a

        def region_r(start, *dims):
            return region(start, *dims, dtype=F32R)

        psum = ctx.enter_context(nc.psum_tensor("psum", [P, 8 * BANK], F32))

        def bank(b, n=BANK, parts=P):
            return psum[0:parts, b * BANK:b * BANK + n]

        ident = sb("ident", [P, P])
        ones = sb("ones", [P, P])
        eps = sb("eps", [P, 1])
        rope = sb("rope", [P, NT * 2 * DK])
        rope_t = rope[:].rearrange("p (t w d) -> p t w d", t=NT, w=2)
        heads = sb("heads", [P, NH])
        causal = sb("causal", [CH, 2 * NH * CH])
        rel = sb("rel", [CH, 2 * CH])
        steps = sb("steps", [P, 4 * CH])
        sil = sb("sil", [P, KD * 2])
        sil_in = sb("sil_in", [P, KD * 2])
        mods = sb("mods", [P, DEPTH * 6 * KD * 2])
        mods_v = mods[:].rearrange("p (l w k s) -> p l w k s", l=DEPTH, w=6, k=KD)
        gains = sb("gains", [P, DEPTH * 4 * KD])
        gains_v = gains[:].rearrange("p (l w k) -> p l w k", l=DEPTH, w=4)
        ada_b = sb("ada_b", [P, DEPTH * 6 * KD])
        mods_f = mods[:].rearrange("p (m s) -> p m s", s=2)
        wuq = region(R_B, 2, NH * MQ)
        wukv = region(R_B + 2 * NH * MQ, NH * 2 * HD)
        wgate = region(R_B + 2 * NH * MQ + NH * 2 * HD, 2, P, parts=2 * GR)
        silu_warm = sb("silu_warm", [P, 1])
        bgate = sb("bgate", [P, 2])
        qnorm = sb("qnorm", [P, 2])
        kvnorm = sb("kvnorm", [P, 1])
        lam_at = R_B + 2 * NH * MQ + NH * 2 * HD + 2 * P
        lam_v, lam_p = region(lam_at, 4 * DK), region(lam_at + 4 * DK, 2 * DK)
        lam_s = sb("lam_s", [P, 2])
        lam_e = sb("lam_e", [P, 2])
        neg_lam = sb("neg_lam", [P, 1])
        dec_in = sb("dec_in", [P, 10])
        dec_t = sb("dec_t", [P, 10])
        log_dec = sb("log_dec", [P, 10])
        mask = sb("mask", [CH, 2 * NH * CH])
        chunk_dec = sb("chunk_dec", [P, 2 * NC])
        dec_v = chunk_dec[:].rearrange("p (d c) -> p d c", d=2)
        edge = sb("edge", [P, 4 * CH])

        turn = {e: 0 for e in ("pe", "act", "dve", "pool", "sp")}

        def handover(who, eng):
            turn[who] += 1
            eng.drain().then_inc(sem("stage_done"), 1)
            eng.wait_ge(sem("stage_done"), 5 * turn[who])

        def first_token(layer, last_part):
            return CTX if last_part and layer == DEPTH - 1 else 0

        def spans(c0):
            return [(c, min(BANK, N - c)) for c in range(c0, N, BANK)]

        def streams(c0):
            return ([(1, 0, CTX)] if c0 == 0 else []) + [(0, CTX, N)]

        Y1 = R_A + KD * N
        X_AT = R_A + 2 * KD * N
        NORMS = [dict(y=None, pre=0, layer=0, c0=0)]
        for _l in range(DEPTH):
            NORMS.append(dict(y=Y1, gate=2, gain=1, pre=3, layer=_l, c0=first_token(_l, True)))
            NORMS.append(dict(y=R_H, gate=5, gain=3, pre=0 if _l < DEPTH - 1 else None, layer=_l,
                              c0=first_token(_l, True)))
        for _n in NORMS:
            _n["pre_layer"] = _n["layer"] + (_n.get("gate") == 5)
        sq_count, read_count, rs_count = [], [], []
        _a = _b = _c = 0
        for _n in NORMS:
            sq_count.append(_a)
            read_count.append(_b)
            rs_count.append(_c)
            _a += KD * (_n["pre"] is not None)
            _b += KD * (_n["pre"] is not None) + (_n["y"] is not None)
            _c += (_n["y"] is not None) + (_n["pre"] is not None)
        SQ_SUM, SQ_NEW = H_HI, H_HI + N
        N_SQ, N_TMP, N_RS = X_AT + KD * N, X_AT + (KD + 2) * N, X_AT + (KD + 4) * N


        WIN_LO, WIN_HI, WIN_OUT = Y1, Y1 + 2 * KD * IN_C, Y1 + 4 * KD * IN_C
        assert WIN_OUT + NT * IN_C <= R_B

        def blocks(l):
            before = len(spans(0)) if l else 0
            return [(before + j, a, n) for j, (a, n) in enumerate(spans(first_token(l, True)))]

        def back(l, block=None):
            j = 0 if block is None else block[0] - (len(spans(0)) if l else 0) + 1
            done = l * (len(spans(0)) + 1) + j
            mixers = l + (j > 0)
            units = KD * (2 * done - mixers)
            if block is None:
                c0 = first_token(l, True)
                return 1, KD, (MIX_HI, MIX_LO), Y1, R_A + 2 * N, units, KD * done, c0, N - c0
            return 2, KH // 2, (ACT_HI, ACT_LO), R_H, W_AT, units, KD * done, block[1], block[2]

        def unit_slots(w_at, block, size):
            second = w_at + 5 * size if block is None else H_HI + 2 * N if block[1] + block[2] == N else w_at
            return [w_at, second], [w_at + (1 + i) * size for i in range(2)], [w_at + (3 + i) * size for i in range(2)]
        assert W_AT + 5 * UNIT <= ARENA
        assert R_A + 2 * N + 6 * KD * P <= Y1

        WF = [[W_AT + (3 * half + i) * KD * P for i in range(3)] for half in range(2)]
        SILU_AT = W_AT + 6 * KD * P
        assert SILU_AT + FFN_T <= ARENA

        SCANS = ((0, CC), (CC, NC))

        def in_turn(x, d, a, b):
            if d == 0:
                return x[:, a:b]
            return x[:, b - 1:a - 1:-1] if a else x[:, b - 1::-1]

        _at = [R_H + 2 * IN_W]

        def take(*dims, parts=P):
            size = 1
            for d in dims:
                size *= d
            start = _at[0]
            _at[0] += -(-size // 8) * 8
            return region(start, *dims, parts=parts)
        T_IN = [region(R_H + s * IN_W, IN_W) for s in range(2)]
        T_RD, T_RM, T_RR = take(16, DK), [take(1, DK) for _ in range(2)], take(8, DK)
        T_S = [(take(n, DK), take(n, DK)) for n in (16, 1, 8, NH)]
        T_QN = [take(3, P) for _ in range(2)]
        T_QNT, T_GT = take(3, P), take(P, parts=2 * GR)
        T_G = [region(lam_at + 6 * DK + s * (2 * P + 2 * GR), 2 * P + 2 * GR) for s in range(2)]
        T_MQ, T_MK = take(NH, MQ), take(NH, MQ)

        def in_steps(eng, count, parts):
            lag = max(i for i, _ in parts)
            peeled = lag + lag % 2

            def step(t, s, known):
                for i, part in parts:
                    if known is None or 0 <= known - i < count:
                        part(t - i, (s - i) % 2)
            for t in range(peeled):
                step(t, t % 2, t)
            with eng.Fori(peeled // 2, count // 2) as u:
                for s in range(2):
                    step(2 * u + s, s, None)
            for t in range(count, count + lag):
                step(t, t % 2, t)
        T_SS = sb("ss", [P, 2])
        T_RS = sb("rs", [P, 2])
        assert _at[0] <= R_A

        E = [region(R_H + d * 4 * N, NC, 4, CH) for d in range(2)]
        KS, KDE, QD, QS = range(4)
        R_O = R_B
        RESET = region(R_B, N)
        R_T = R_B + NC * 256
        T1, T2, T3 = (region(R_T + i * N, N) for i in range(3))
        _at[0] = R_T
        R_V = R_T
        _at[0] += 4 * 256
        V = [[region(R_V + (2 * d + p) * 256, NH * HD, parts=CH) for p in range(2)] for d in range(2)]
        EST = [[take(3, CH) for p in range(2)] for d in range(2)]
        QBD = [[take(NH, CH) for p in range(2)] for d in range(2)]
        SCM = [take(NH, CH, parts=CH) for d in range(2)]
        UM = [take(NH, HD) for d in range(2)]
        STATE = [take(NH * HD) for d in range(2)]
        KDT = [take(P, parts=CH) for d in range(2)]

        _at[0] = R_H
        A_QM = take(NH, P, parts=MQ)
        A_P = [take(N) for _ in range(4)]
        A_PT = [take(NT, P) for _ in range(2)]
        A_CM, A_NM, A_L, A_LS = take(3), take(MAPS), take(MAPS, 2), take(MAPS)
        A_RL, A_SC, A_NL = take(OUTS), take(NH), take(NH)
        STACK = 3 * DK
        K_STACK = [region_r(at, NH, N)[0:STACK] for at in (R_GR, R_GZ)]
        A_OUT = region(R_GZ + NH * N, NT, OUTS * HD)
        Q_AT = R_GZ + NH * N + NT * OUTS * HD
        Q_STACK = region_r(Q_AT, 2, NH, P)[0:STACK]
        Q_HI = Q_AT + 2 * NH * P
        assert Q_HI + 2 * N <= ARENA
        K_HI, K_LO = R_H, R_H + 2 * N
        assert _at[0] <= R_A

        TURNED = 3 * BANK

        def score_pieces(nk):
            return [(c, w, 1, c > 0) for c, w in spans(0)] if nk == NT else [(0, CTX, 3, True)]

        def exp_parts(nk):
            return (0, BANK, N) if nk == NT else (0, P, CTX)

        JOIN_AT = {6: 4, 8: 5, 10: 6}
        VALUES_AT = {3: 0, 4: 1, 5: 2, 6: 3, 8: 4, 10: 5}
        TURN_AT = {2: 0, 3: 1, 4: 2, 5: 3, 7: 4, 9: 5, 11: 6}
        LATE_JOIN_AT = {0: 7}
        LATE_VALUES_AT = {0: 6, 2: 7}
        LATE_TURN_AT = {1: 7}

        def att_tiles(eng, count, step):
            tables = (JOIN_AT, LATE_JOIN_AT), (VALUES_AT, LATE_VALUES_AT), (TURN_AT, LATE_TURN_AT)

            def late(m, i):
                return [(i - 1, after[m]) if m in after else None for _, after in tables]

            def tile(i, first):
                for m in range(MAPS):
                    own = [(i, now[m]) if m in now else None for now, _ in tables]
                    step(m, i, *own if first else [b or a for a, b in zip(own, late(m, i))])
            tile(0, True)
            with eng.Fori(1, count) as i:
                tile(i, False)
            for m in range(3):
                step(m, None, *late(m, count))

        def att_loops(l):
            return ([] if l else [(0, CT, 0, CT)]) + [(CT, NT - CT, NT if l else CT, NT)]

        _at[0] = R_A
        F_HM = [take(D) for _ in range(2)]
        F_SB = [take(512) for _ in range(2)]
        F_G = [take(512) for _ in range(2)]
        F_SG = [take(512) for _ in range(2)]
        F_SQ, F_OUTG = take(D), take(D)
        F_SS, F_RS = take(16), [take(16) for _ in range(2)]
        ADA_ROWS0 = region(R_B, ADA_FIRST * P, parts=2)
        F_ADA = [take(ADA_T, KD, BANK) for _ in range(2)]
        F_ROWS = take(ADA_T * BANK, parts=2)

        def fin_loop(l):
            return (0, NT, 0) if l == 0 else (CT, NT - CT, NT // 2)

        FREE = {
            "pe": dict(rows_made=2, rows_turned=1, in_made1=10, turned1=2, made2=1, turned3=1, o_made0=2, o_made1=2,
                       u_made0=1, u_made1=1, turned=4, pv_made=2, fin_turned=2, yb_made=2, gate_made=1,
                       up_made=1),
            "act": dict(rows_kept=1, in_kept0=2, qn_ready=2, kept12=1, mk_ready=1, kept7=1, kd_kept0=1, kd_kept1=1, o_kept0=1,
                        o_kept1=1, exp_done=1, head_done=1, pt_act=1, fin_kept_a=2, fin_rs=1, yb_kept=2,
                        silu_done=1, proj_out=16),
            "dve": dict(ada_kept=1, in_kept1=2, roped=2, kept0=1, mq_ready=1, kept6=1, scm_ready0=1,
                        scm_ready1=1, pt_dve=1, att_kept=2, fin_kept_v=2, fin_ss=1, wb_ready=2, sq_added=1,
                        wf_ready0=1, wf_ready1=1, up_done=1, fin_ready=2),
        }

        def free(who, eng):
            for name, n in FREE[who].items():
                eng.sem_inc(sem(name), n)

        block = ctx.enter_context(nc.Block())

        @block.sync
        def _(sp):
            for dst, name in ((ident, "c_ident"), (rope, "c_rope"), (heads, "c_heads"), (causal, "c_causal"),
                              (rel, "c_rel"), (steps, "c_steps"), (sil_in, "cond")):
                sp.dma_start(dst[:], t[name]).then_inc(sem("const_in"), 16)

            for dst, name in ((gains, "norm_g"), (ada_b, "ada_b")):
                sp.dma_start(dst[:], t[name]).then_inc(sem("const_in"), 16)

            def first_modulation():
                for c in range(ADA_FIRST // ADA_M):
                    sp.dma_start(region(R_H + c * ADA_M * D, ADA_M * D), t["ada_w"][c]).then_inc(sem(f"ada0_in{c}"), 16)
                handover("sp", sp)

            def small(l):
                for dst, src in ((wuq, t["w_uq"][l]), (wukv, t["w_ukv"][l]), (bgate[:], t["b_gate"][l]),
                                 (qnorm[:], t["q_norm"][l]), (kvnorm[:], t["kv_norm"][l]),
                                 (dec_in[:, 8:10], t["decay_col"][l]), (lam_v, t["lam"][l].partition_broadcast(P)),
                                 (dec_in[:, 0:8], t["decay"][l].partition_broadcast(P))):
                    sp.dma_start(dst, src).then_inc(sem("small_in"), 16)
                sp.wait_ge(sem("wgate_zero"), l + 1)
                for d in range(2):
                    sp.dma_start(wgate[d * GR:(d + 1) * GR, d, :], t["w_gate"][l, :, d, :]).then_inc(sem("small_in"), 16)

            def load_win(l, u, s):
                sp.dma_start(region(WIN_LO + s * KD * IN_C, KD * IN_C), t["w_in"][l, 2 * u + s]
                             ).then_inc(sem(f"win_in{s}"), 16)

            def norm(i):
                n = NORMS[i]
                c0 = n["c0"]
                src = t["x"] if i <= 1 else xdram
                for k in range(KD):
                    sp.dma_start(region(X_AT, KD, N)[:, k, c0:N], src[:, k, c0:N]).then_inc(sem(f"x_in{k}"), 16)
                if n["pre"] == 0:
                    for s in range(2):
                        load_win(n["pre_layer"], 0, s)
                if n["y"] is not None:
                    last = n["pre"] is None
                    for k in range(KD):
                        sp.wait_ge(sem("x_new"), (i - 1) * KD + k + 1)
                        xk = region(X_AT, KD, N)[:, k, c0:N]
                        dst = t["out"][:, k, :] if last else xdram[:, k, c0:N]
                        sp.dma_start(dst, xk).then_inc(sem("x_out"), 16)
                    sp.wait_ge(sem("x_out"), 16 * KD * i)
                handover("sp", sp)

            def project(l):
                small(l)
                with sp.Fori(1, IN_CHUNKS // 2) as u:
                    for s in range(2):
                        sp.wait_ge(sem("in_made1"), l * 40 + u * 10 + 5 * (s + 1))
                        load_win(l, u, s)
                handover("sp", sp)

            def prepare(l):
                sp.dma_start(region(R_VD, NT, 256), proj.rearrange("(t p) c -> p t c", p=P)[:, :, COL["dv"]:COL["dv"] + 256]
                             ).then_inc(sem("vd_in"), 16)
                with sp.Fori(0, NT // 2) as u:
                    for s in range(2):
                        for read in ("roped", "qn_ready"):
                            sp.wait_ge(sem(read), l * NT + 2 * u + s + 1)
                        row = proj.rearrange("(t p) c -> p t c", p=P)[:, 2 * u + s, :]
                        sp.dma_start(region(R_H + s * IN_W, IN_W), row).then_inc(sem(f"tile_in{s}"), 16)
                        sp.wait_ge(sem("turned1"), l * NT + 2 * u + s + 1)
                        sp.dma_start(T_G[s][:, 0:2 * P], row[:, COL["gq"]:COL["gq"] + 2 * P]).then_inc(sem(f"g_in{s}"), 16)
                        sp.dma_start(T_G[s][:, 2 * P:], row[:, COL["gf"]:COL["gf"] + 2 * GR]).then_inc(sem(f"g_in{s}"), 16)
                sp.wait_ge(sem("vd_in"), 16 * (l + 1))
                handover("sp", sp)

            def scan(l, g):
                inst = 2 * l + g
                col = COL["rv" if g else "gv"]
                for a, b in SCANS:
                    with sp.Fori(0, (b - a) // 2) as pair:
                        i = a + 2 * pair
                        for p in range(2):
                            for d in range(2):
                                sp.wait_ge(sem(f"o_made{d}"), inst * NC + i + p + 1)
                                sp.dma_start(region(R_V + (2 * d + p) * 256, 256, parts=CH),
                                             in_turn(proj.rearrange("(c p) f -> p c f", p=CH)[:, :, col:col + 256], d, a, b)[:, 2 * pair + p, :]
                                             ).then_inc(sem(f"v_in{d}{p}"), 16)
                for d in range(2):
                    sp.wait_ge(sem(f"o_kept{d}"), (inst + 1) * NC + 1)
                    sp.dma_start(scans[d].rearrange("(c p) f -> p c f", p=CH)[:, :, g * 256:(g + 1) * 256],
                                 region(R_O, NC, 256)[d * CH:(d + 1) * CH]).then_inc(sem("o_out"), 16)
                sp.wait_ge(sem("o_out"), 32 * (inst + 1))
                handover("sp", sp)

            def attend(l):
                for first, count, base, nk in att_loops(l):
                    with sp.Fori(0, count) as i:
                        sp.wait_ge(sem("att_kept"), (base + i) * OUTS + OUTS + 2)
                        sp.dma_start(att.rearrange("(t p) c -> p t c", p=P)[:, first + i, :], A_OUT[:, first + i, :]
                                     ).then_inc(sem("att_out"), 16)
                    sp.wait_ge(sem("att_out"), 16 * (base + count))
                handover("sp", sp)

            def finish(l):
                c0, count, base = fin_loop(l)
                sp.dma_start(F_OUTG, t["out_g"][l].partition_broadcast(P)).then_inc(sem("outg_in"), 16)
                with sp.Fori(0, count // 2) as u:
                    for s in range(2):
                        sp.wait_ge(sem("fin_turned"), 2 * base + 2 * u + s + 1)
                        tok = c0 + 2 * u + s

                        def rows(a):
                            return a.rearrange("(t p) c -> p t c", p=P)[:, tok, :]
                        for dst, src in ((F_HM[s][:, 0:512], rows(att)), (F_HM[s][:, 512:1024], rows(scans[0])),
                                         (F_SB[s], rows(scans[1])),
                                         (F_G[s][:, 0:256], rows(proj)[:, COL["gr"]:COL["gr"] + 256]),
                                         (F_G[s][:, 256:512], rows(proj)[:, COL["rg"]:COL["rg"] + 256])):
                            sp.dma_start(dst, src).then_inc(sem(f"fin_in{s}"), 16)
                handover("sp", sp)

            def project_back(l, block=None):
                per, kk, _, _, w_at, units, _, _, _ = back(l, block)
                w = t["w_out"] if block is None else t["ffn_out"]
                raw = unit_slots(w_at, block, kk * P)[0]
                alone = int(raw[0] == raw[1])
                with sp.Fori(0, KD // 2) as u:
                    for s in range(2):
                        for j in range(per):
                            slot = j if per == 2 else s
                            sp.wait_ge(sem("wb_ready"), units + per * (2 * u + s) + j + 1 + alone)
                            sp.dma_start(region(raw[slot], kk * P), w[l, 2 * u + s, :, j * kk * P:(j + 1) * kk * P]
                                         ).then_inc(sem(f"wb_in{slot}"), 16)
                handover("sp", sp)

            def hidden(l, block):
                with sp.Fori(0, KH) as u:
                    for half in range(2):
                        sp.wait_ge(sem(f"wf_ready{half}"), block[0] * KH + u + 1)
                        sp.dma_start(region(WF[half][0], KD * P), t["ffn_in"][l, u, half]
                                     ).then_inc(sem(f"wf_in{half}"), 16)
                handover("sp", sp)

            first_modulation()
            norm(0)
            for l in range(DEPTH):
                project(l)
                prepare(l)
                for g in range(2):
                    handover("sp", sp)
                    scan(l, g)
                handover("sp", sp)
                attend(l)
                finish(l)
                project_back(l)
                norm(2 * l + 1)
                for block_ in blocks(l):
                    hidden(l, block_)
                    project_back(l, block_)
                norm(2 * l + 2)

        @block.tensor
        def _(pe):
            mm = nc.tensor.matmul

            def mm3(out, a, b, start, stop):
                mm(out, a[0], b[0], start=start, stop=False)
                mm(out, a[0], b[1], start=False, stop=False)
                return mm(out, a[1], b[0], start=False, stop=stop)
            free("pe", pe)
            pe.wait_ge(sem("const_in"), 16 * 9)
            pe.wait_ge(sem("const_set"), 1)

            def modulation_rows(b, w):
                for k in range(KD):
                    last = mm(bank(b, parts=2), sil[:, 2 * k:2 * k + 2], w[:, k, :], start=(k == 0), stop=(k == KD - 1))
                return last

            def modulation_turn(b, rows, n_m):
                for m in range(n_m):
                    last = nc.tensor.transpose(bank(b)[:, 2 * m:2 * m + 2], rows[:, m * P:(m + 1) * P], ident[0:2, 0:2])
                return last

            def first_modulation():
                pe.wait_ge(sem("sil_ready"), 1)
                for c in range(ADA_FIRST // ADA_M):
                    pe.wait_ge(sem(f"ada0_in{c}"), 16)
                    modulation_rows(c, region(R_H + c * ADA_M * D, KD, BANK)).then_inc(sem("ada0_made"), 1)
                pe.wait_ge(sem("ada0_kept"), ADA_FIRST // ADA_M)
                modulation_turn(4, ADA_ROWS0, ADA_FIRST).then_inc(sem("ada0_turned"), 1)
                handover("pe", pe)

            def norm(i):
                n = NORMS[i]
                c0 = n["c0"]
                if n["y"] is not None:
                    for c, w in spans(c0):
                        last = mm(psum[:, c - c0:c - c0 + w], ones[:], region(SQ_SUM, N)[:, c:c + w], start=True, stop=True)
                    last.then_inc(sem("sq_read"), 1)
                if n["pre"] is not None:
                    if n["y"] is not None:
                        pe.wait_ge(sem("rstd_ready"), rs_count[i] + 1)
                    for k in range(KD):
                        pe.wait_ge(sem("sq_ready"), sq_count[i] + k + 1)
                        for c, w in spans(c0):
                            last = mm(psum[:, c - c0:c - c0 + w], ones[:], region(N_SQ, 2, N)[:, k % 2, c:c + w],
                                      start=(k == 0), stop=(k == KD - 1))
                        last.then_inc(sem("sq_read"), 1)
                handover("pe", pe)

            def project(l):
                h = [region_r(at, KD, N) for at in (H_HI, H_LO)]
                with pe.Fori(0, IN_CHUNKS // 2) as u:
                    for s in range(2):
                        w = [region_r(at + s * KD * IN_C, KD, IN_C) for at in (WIN_HI, WIN_LO)]
                        pe.wait_ge(sem("win_ready"), l * IN_CHUNKS + 2 * u + s + 1)
                        for tt in range(NT):
                            n, par = 5 * s + tt // 2, tt % 2
                            pe.wait_ge(sem(f"in_kept{par}"), l * 40 + u * 10 + n + 1)
                            for k in range(KD):
                                last = mm3(bank(2 * par + n % 2, IN_C), [x[:, k, tt * P:(tt + 1) * P] for x in h],
                                           [x[:, k, :] for x in w], start=(k == 0), stop=(k == KD - 1))
                            last.then_inc(sem(f"in_made{par}"), 1)
                handover("pe", pe)

            def prepare(l):
                pe.wait_ge(sem("small_in"), 160 * (l + 1))

                def turn_first(t, s):
                    T = l * NT + t
                    pe.wait_ge(sem(f"g_in{s}"), 16 * (T - s) + 32)
                    pe.wait_ge(sem("roped"), T + 3)
                    pe.wait_ge(sem("qn_ready"), T + 3)
                    pe.wait_ge(sem("kept0"), T + 1)
                    pe.wait_ge(sem("kept12"), T + 1)
                    rd = T_RD.rearrange("p (j h) d -> p j (h d)", j=4)
                    rr = T_RR.rearrange("p (j h) d -> p j (h d)", j=2)
                    for j in range(4):
                        nc.tensor.transpose(bank(0)[:, j * P:(j + 1) * P], rd[:, j, :], ident[:])
                    gsrc = [T_G[s][:, 0:P], T_G[s][:, P:2 * P], rr[:, 0, :], rr[:, 1, :]]
                    for j in range(4):
                        nc.tensor.transpose(bank(1)[:, j * P:(j + 1) * P], gsrc[j], ident[:])
                    for j in range(3):
                        nc.tensor.transpose(bank(2)[:, j * P:(j + 1) * P], T_QN[s][:, j, :], ident[:])
                    nc.tensor.transpose(bank(2)[0:2 * GR, 3 * P:4 * P], T_G[s][:, 2 * P:], ident[:]
                                        ).then_inc(sem("turned1"), 1)

                def multiply(t, s):
                    T = l * NT + t
                    pe.wait_ge(sem("kept12"), T + 2)
                    pe.wait_ge(sem("mq_ready"), T + 1)
                    pe.wait_ge(sem("mk_ready"), T + 1)
                    for k in range(2):
                        mm(bank(3, NH * MQ), T_QNT[:, k, :], wuq[:, k, :], start=(k == 0), stop=(k == 1))
                    mm(bank(4), T_QNT[:, 2, :], wukv, start=True, stop=True)
                    for d in range(2):
                        last = mm(bank(5)[:, d * P:(d + 1) * P], wgate[:, d, :], T_GT, start=True, stop=True)
                    last.then_inc(sem("made2"), 1)

                def turn_last(t, s):
                    T = l * NT + t
                    pe.wait_ge(sem("mq_ready"), T + 2)
                    pe.wait_ge(sem("mk_ready"), T + 2)
                    pe.wait_ge(sem("kept6"), T + 1)
                    pe.wait_ge(sem("kept7"), T + 1)
                    for b, src in ((6, T_MQ), (7, T_MK)):
                        for h in range(NH):
                            last = nc.tensor.transpose(bank(b)[0:MQ, h * P:(h + 1) * P], src[:, h, :], ident[:])
                    last.then_inc(sem("turned3"), 1)
                in_steps(pe, NT, [(2, multiply), (3, turn_last), (1, turn_first)])
                handover("pe", pe)

            def scan(l, g):
                inst = 2 * l + g
                for a, b in SCANS:
                    with pe.Fori(0, (b - a) // 2) as pair:
                        i = a + 2 * pair
                        for p in range(2):
                            n = inst * NC + i + p
                            for d in range(2):
                                pe.wait_ge(sem(f"est_ready{d}"), n + 1)
                                pe.wait_ge(sem(f"scm_ready{d}"), n + 1)
                                mm(bank(d, NH * CH, CH), EST[d][p][:, KS, :], QBD[d][p].rearrange("p h i -> p (h i)"),
                                   start=True, stop=True).then_inc(sem(f"sc_made{d}"), 1)
                                pe.wait_ge(sem(f"kd_kept{d}"), n + 1)
                                nc.tensor.transpose(bank(2 + d, P), EST[d][p][:, KDE:QD + 1, :].rearrange("p a b -> p (a b)"), ident[:]
                                                    ).then_inc(sem(f"kd_turned{d}"), 1)
                            for d in range(2):
                                pe.wait_ge(sem(f"state_ready{d}"), n + inst + 1)
                                pe.wait_ge(sem(f"o_kept{d}"), n + 1)
                                mm(bank(4 + d, NH * HD, CH), EST[d][p][:, QD, :], STATE[d], start=True, stop=False,
                                   skip_group_check=True)
                            for d in range(2):
                                pe.wait_ge(sem(f"v_in{d}{p}"), 16 * (inst * (NC // 2) + a // 2 + pair + 1))
                                pe.wait_ge(sem(f"kd_kept{d}"), n + 2)
                                pe.wait_ge(sem(f"scm_ready{d}"), n + 2)
                                mm(bank(6 + d, NH * HD), KDT[d], V[d][p], start=True, stop=True
                                   ).then_inc(sem(f"u_made{d}"), 1)
                            for d in range(2):
                                for h in range(NH):
                                    last = mm(bank(4 + d, NH * HD, CH)[:, h * HD:(h + 1) * HD], SCM[d][:, h, :],
                                              V[d][p][:, h * HD:(h + 1) * HD], start=False, stop=(h == NH - 1),
                                              skip_group_check=True)
                                last.then_inc(sem(f"o_made{d}"), 1)
                handover("pe", pe)

            def attend(l):
                for first, count, base, nk in att_loops(l):
                    def scores(m, i):
                        M0 = (base + i) * MAPS
                        if m == 0:
                            pe.wait_ge(sem("qm_staged"), base + i + 1)
                        if m == NH:
                            pe.wait_ge(sem("qd_staged"), base + i + 1)
                        pe.wait_ge(sem("head_done"), M0 + m + 1)
                        if m < NH:
                            q, k = A_QM[:, m, :], region(R_KM, 4, N, parts=MQ)[:, m, :]
                        else:
                            c, j = (m - NH) // NH, m % NH
                            q, k = Q_STACK[:, c, j, :], K_STACK[c][:, j, :]
                        waits = True
                        for c, w, n, tail in score_pieces(nk):
                            if tail and waits:
                                pe.wait_ge(sem("exp_done"), M0 + m + 1)
                                waits = False
                            mm(psum[:, c:c + w], q, k[:, c:c + w], start=True, stop=True).then_inc(sem("scored"), n)

                    def turn_probs(i, o):
                        T = base + i
                        if o < NH:
                            pe.wait_ge(sem("exp_done"), T * MAPS + o + 2)
                        else:
                            pe.wait_ge(sem("maps_joined"), NH * T + o - NH + 1)
                        pe.wait_ge(sem("pt_act"), OUTS * T + o + 1)
                        pe.wait_ge(sem("pt_dve"), OUTS * T + o + 1)
                        src = A_P[o if o < NH else 2 * (o % 2)]
                        for kt in range(nk):
                            at = TURNED + kt * P if nk == NT else TURNED + kt * BANK
                            last = nc.tensor.transpose(psum[:, at:at + P], src[:, kt * P:(kt + 1) * P], ident[:])
                        last.then_inc(sem("turned"), 1)

                    def values(i, o):
                        n = OUTS * (base + i) + o
                        pe.wait_ge(sem("pt_act"), n + 2)
                        pe.wait_ge(sem("pt_dve"), n + 2)
                        pe.wait_ge(sem("att_kept"), n + 1)
                        v = region(R_VM if o < NH else R_VD, NT, 256)
                        h = o % NH
                        for kt in range(nk):
                            last = mm(bank(6 + o % 2, HD), A_PT[o % 2][:, kt, :], v[:, kt, h * HD:(h + 1) * HD],
                                      start=(kt == 0), stop=(kt == nk - 1))
                        last.then_inc(sem("pv_made"), 1)

                    def step(m, i, of_join, of_values, of_turn):
                        if i is not None:
                            scores(m, i)
                        if of_values:
                            values(*of_values)
                        if of_turn:
                            turn_probs(*of_turn)
                    att_tiles(pe, count, step)
                handover("pe", pe)

            def finish(l):
                c0, count, base = fin_loop(l)

                def modulate(t, s):
                    pe.wait_ge(sem(f"ada_in{s}"), 8 * ADA_T * (t - s) + 16 * ADA_T)
                    pe.wait_ge(sem("rows_kept"), t + 1)
                    for j in range(ADA_T):
                        last = modulation_rows(4 + j, F_ADA[s][:, j])
                    last.then_inc(sem("rows_made"), 1)

                def turn_tile(t, s):
                    T = 2 * base + t
                    pe.wait_ge(sem("fin_ready"), T + 3)
                    if l == 0:
                        pe.wait_ge(sem("rows_kept"), t + 2)
                        pe.wait_ge(sem("ada_kept"), t + 1)
                    pe.wait_ge(sem("fin_kept_a"), T + 1)
                    pe.wait_ge(sem("fin_kept_v"), T + 1)
                    for k in range(KD):
                        last = nc.tensor.transpose(bank(2 * s + k // 4)[:, (k % 4) * P:(k % 4 + 1) * P],
                                                   F_HM[s][:, k * P:(k + 1) * P], ident[:])
                    last.then_inc(sem("fin_turned"), 1)
                    if l == 0:
                        modulation_turn(6, F_ROWS, ADA_T * ADA_M).then_inc(sem("rows_turned"), 1)
                in_steps(pe, count, [(1, turn_tile)] + ([(0, modulate)] if l == 0 else []))
                handover("pe", pe)

            def project_back(l, block=None):
                per, kk, src_at, _, w_at, units, chunks, t0, n = back(l, block)
                src = [region_r(at, KD if per == 1 else KH, N if per == 1 else FFN_T) for at in src_at]
                pieces = spans(t0) if per == 1 else [(0, n)]
                first = t0 if per == 1 else 0
                _, hi, lo = unit_slots(w_at, block, kk * P)
                with pe.Fori(0, KD // 2) as u:
                    for s in range(2):
                        for j in range(per):
                            slot = j if per == 2 else s
                            w = [region_r(at, kk, P) for at in (hi[slot], lo[slot])]
                            pe.wait_ge(sem("wb_ready"), units + per * (2 * u + s) + j + 3)
                            if j == 0:
                                pe.wait_ge(sem("yb_kept"), chunks + 2 * u + s + 1)
                            for a, m in pieces:
                                out = psum[:, 3 * s * BANK + a - first:3 * s * BANK + a - first + m]
                                for k in range(kk):
                                    last = mm3(out, [x[:, k, :] for x in w], [x[:, j * kk + k, a:a + m] for x in src],
                                               start=(j == 0 and k == 0), stop=(j == per - 1 and k == kk - 1))
                            last.then_inc(sem("yb_made"), 1)
                handover("pe", pe)

            def hidden(l, block):
                index, t0, n = block
                h = [region_r(at, KD, N) for at in (H_HI, H_LO)]
                with pe.Fori(0, KH) as u:
                    for half in range(2):
                        w = [region_r(at, KD, P) for at in WF[half][1:]]
                        pe.wait_ge(sem(f"wf_ready{half}"), index * KH + u + 2)
                        pe.wait_ge(sem("up_done" if half else "silu_done"), index * KH + u + 1)
                        for k in range(KD):
                            last = mm3(bank(half, n), [x[:, k, :] for x in w], [x[:, k, t0:t0 + n] for x in h],
                                       start=(k == 0), stop=(k == KD - 1))
                        last.then_inc(sem("up_made" if half else "gate_made"), 1)
                handover("pe", pe)

            first_modulation()
            norm(0)
            for l in range(DEPTH):
                project(l)
                prepare(l)
                for g in range(2):
                    handover("pe", pe)
                    scan(l, g)
                handover("pe", pe)
                attend(l)
                finish(l)
                project_back(l)
                norm(2 * l + 1)
                for block_ in blocks(l):
                    hidden(l, block_)
                    project_back(l, block_)
                norm(2 * l + 2)

        @block.scalar
        def _(act):
            activation = nc.scalar.activation
            free("act", act)
            act.wait_ge(sem("const_in"), 16 * 9)
            act.wait_ge(sem("const_set"), 1)
            activation(sil[:], sil_in[:], ACT.Silu).then_inc(sem("sil_ready"), 1)

            def first_modulation():
                for c in range(ADA_FIRST // ADA_M):
                    act.wait_ge(sem("ada0_made"), c + 1)
                    nc.scalar.copy(ADA_ROWS0[:, c * BANK:(c + 1) * BANK], bank(c, parts=2)
                                   ).then_inc(sem("ada0_kept"), 1)
                handover("act", act)

            def norm(i):
                n = NORMS[i]
                c0 = n["c0"]
                reads = read_count[i]
                passes = [p for p in ("y", "pre") if n[p] is not None]
                for pas, which in enumerate(passes):
                    if which == "y":
                        reads += 1
                    else:
                        for k in range(KD):
                            if n["y"] is None:
                                act.wait_ge(sem(f"x_in{k}"), 16 * (i + 1))
                            else:
                                act.wait_ge(sem("x_new"), (i - 1) * KD + k + 1)
                            if k >= 2:
                                act.wait_ge(sem("sq_read"), reads + k - 1)
                            activation(region(N_SQ, 2, N)[:, k % 2, c0:N], region(X_AT, KD, N)[:, k, c0:N], ACT.Square
                                       ).then_inc(sem("sq_ready"), 1)
                        reads += KD
                    act.wait_ge(sem("sq_read"), reads)
                    r = region(N_RS + pas * N, N)
                    activation(r[:, c0:N], psum[:, 0:N - c0], ACT.Ln, scale=1.0 / D, bias=eps[:, 0:1])
                    act.drain()
                    activation(r[:, c0:N], r[:, c0:N], ACT.Exp, scale=-0.5).then_inc(sem("rstd_ready"), 1)
                if n["pre"] is not None:
                    for k in range(KD):
                        act.wait_ge(sem("h_normed"), KD * i + k + 1)
                        hk, hi = region(R_H, KD, N)[:, k, :], region_r(H_HI, KD, N)[:, k, :]
                        m = mods_v[:, n["pre_layer"]]
                        for st, a, b in streams(c0):
                            last = activation(hi[:, a:b], hk[:, a:b], ACT.Identity, bias=m[:, n["pre"], k, st:st + 1])
                        last.then_inc(sem("h_made"), 1)
                handover("act", act)

            def project(l):
                def part(c, s):
                    act.wait_ge(sem(f"win_in{s}"), 16 * (l * (IN_CHUNKS // 2) + c + 1))
                    nc.scalar.copy(region_r(WIN_HI + s * KD * IN_C, KD * IN_C), region(WIN_LO + s * KD * IN_C, KD * IN_C)
                                   ).then_inc(sem("win_hi"), 1)

                def chunk(u, s, is_last):
                    for j in range(5):
                        n = 5 * s + j
                        if j == 2 and not is_last:
                            part(u + s, 1 - s)
                        act.wait_ge(sem("in_made0"), l * 40 + u * 10 + n + 1)
                        if j == 0:
                            act.wait_ge(sem("proj_out"), 16 * (l * IN_CHUNKS + 2 * u + s + 1))
                        nc.scalar.copy(region(WIN_OUT, NT, IN_C)[:, 2 * j, :], bank(n % 2, IN_C)
                                       ).then_inc(sem("in_kept0"), 1)
                    for par in range(2):
                        act.wait_ge(sem(f"in_kept{par}"), l * 40 + u * 10 + 5 * (s + 1) + 2)
                    act.dma_start(proj.rearrange("(t p) (c w) -> p t c w", p=P, w=IN_C)[:, :, 2 * u + s, :],
                                  region(WIN_OUT, NT, IN_C)).then_inc(sem("proj_out"), 16)
                part(0, 0)
                with act.Fori(0, IN_CHUNKS // 2 - 1) as u:
                    for s in range(2):
                        chunk(u, s, False)
                for s in range(2):
                    chunk(IN_CHUNKS // 2 - 1, s, s == 1)
                act.wait_ge(sem("proj_out"), 16 * (IN_CHUNKS * (l + 1) + 1))
                handover("act", act)

            def prepare(l):
                act.wait_ge(sem("small_in"), 160 * (l + 1))
                act.wait_ge(sem("dec_abs"), l + 1)
                activation(dec_t[:], dec_t[:], ACT.Exp, scale=-1.0)
                act.drain()
                activation(dec_t[:], dec_t[:], ACT.Ln, bias=1.0)
                activation(lam_e[:], lam_s[:], ACT.Exp).then_inc(sem("dec_ln"), 1)

                def norm_ranks(t, s):
                    T = l * NT + t
                    mq, mkv = T_IN[s][:, COL["mq"]:COL["mq"] + QR], T_IN[s][:, COL["mkv"]:COL["mkv"] + KVR]
                    act.wait_ge(sem(f"tile_in{s}"), 8 * (T - s) + 16)
                    act.wait_ge(sem("turned1"), T + 1)
                    qn = T_QN[s].rearrange("p j d -> p (j d)")
                    activation(qn[:, 0:QR], mq, ACT.Square, accum_out=T_SS[:, 0:1])
                    activation(qn[:, QR:QR + KVR], mkv, ACT.Square, accum_out=T_SS[:, 1:2])
                    act.drain()
                    activation(T_RS[:, 0:1], T_SS[:, 0:1], ACT.Ln, scale=1.0 / QR, bias=eps[:, 0:1])
                    activation(T_RS[:, 1:2], T_SS[:, 1:2], ACT.Ln, scale=1.0 / KVR, bias=eps[:, 0:1])
                    act.drain()
                    activation(T_RS[:], T_RS[:], ACT.Exp, scale=-0.5)
                    act.drain()
                    nc.scalar.mul(qn[:, 0:QR], mq, T_RS[:, 0:1])
                    nc.scalar.mul(qn[:, QR:QR + KVR], mkv, T_RS[:, 1:2]).then_inc(sem("qn_ready"), 1)

                def keep_first(t, s):
                    T = l * NT + t
                    act.wait_ge(sem("turned1"), T + 3)
                    act.wait_ge(sem("made2"), T + 1)
                    for j in range(2):
                        nc.scalar.mul(T_QNT[:, j, :], bank(2)[:, j * P:(j + 1) * P], qnorm[:, j:j + 1])
                    nc.scalar.mul(T_QNT[:, 2, :], bank(2)[:, 2 * P:3 * P], kvnorm[:, 0:1])
                    nc.scalar.copy(T_GT, bank(2)[0:2 * GR, 3 * P:4 * P])
                    nc.scalar.copy(region(R_GR, 4, NT, P)[:, :, t, :], bank(1).rearrange("p (j c) -> p j c", j=4)
                                   ).then_inc(sem("kept12"), 1)

                def keep_products(t, s):
                    T = l * NT + t
                    act.wait_ge(sem("made2"), T + 2)
                    act.wait_ge(sem("turned3"), T + 1)
                    kv = bank(4).rearrange("p (h d) -> p h d", h=NH)
                    nc.scalar.copy(T_MK[:, :, 0:HD], kv[:, :, 0:HD])
                    nc.scalar.copy(region(R_VM, NT, NH, HD)[:, t, :, :], kv[:, :, HD:2 * HD])
                    for d in range(2):
                        last = activation(region(R_GZ, 2, NT, P)[:, d, t, :], bank(5)[:, d * P:(d + 1) * P],
                                          ACT.Identity, bias=bgate[:, d:d + 1])
                    last.then_inc(sem("mk_ready"), 1)

                def keep_keys(t, s):
                    act.wait_ge(sem("turned3"), l * NT + t + 2)
                    nc.scalar.copy(region(R_KM, 4, NT, P, parts=MQ)[:, :, t, :],
                                   bank(7, parts=MQ).rearrange("p (j c) -> p j c", j=4)).then_inc(sem("kept7"), 1)
                in_steps(act, NT, [(0, norm_ranks), (2, keep_products), (3, keep_keys), (1, keep_first)])
                handover("act", act)

            def scan_factors(l, g):
                if g == 0:
                    act.wait_ge(sem("gate_abs"), l + 1)
                    a, b = region(R_H, 2 * N), region(R_H + 2 * N, 2 * N)
                    activation(b, a, ACT.Exp, scale=-1.0)
                    act.drain()
                    activation(b, b, ACT.Ln, bias=1.0).then_inc(sem("gate_ln"), 1)
                    for d in range(2):
                        act.wait_ge(sem("exponents"), 2 * l + d + 1)
                        sign = 1.0 if d == 0 else -1.0
                        x1, x2, x3 = (x.rearrange("p (c i) -> p c i", c=NC) for x in (T1, T2, T3))
                        activation(E[d][:, :, QS, :], x2, ACT.Exp, scale=sign)
                        activation(E[d][:, :, KS, :], x2, ACT.Exp, scale=-sign)
                        if d == 0:
                            activation(E[d][:, :, QD, :], x1, ACT.Exp)
                            activation(E[d][:, :, KDE, :], x3, ACT.Exp, scale=-1.0)
                        else:
                            activation(E[d][:, :, QD, :], x3, ACT.Exp, scale=-1.0)
                            activation(E[d][:, :, KDE, :], region(R_GZ, 2, NC, CH)[:, 1], ACT.Exp)
                        activation(dec_v[:, d, :], x1[:, :, CH - 1], ACT.Exp).then_inc(sem("factors"), 1)
                else:
                    act.wait_ge(sem("log_dec_ready"), l + 1)
                    for d in range(2):
                        for h in range(NH):
                            activation(mask[:, (d * NH + h) * CH:(d * NH + h + 1) * CH], rel[:, d * CH:(d + 1) * CH],
                                       ACT.Exp, scale=log_dec[0:CH, d * NH + h:d * NH + h + 1])
                        activation(edge[:, 2 * d * CH:2 * (d + 1) * CH], steps[:, 2 * d * CH:2 * (d + 1) * CH], ACT.Exp,
                                   scale=log_dec[:, 8 + d:9 + d])
                        last = activation(dec_v[:, d, :], log_dec[:, 8 + d:9 + d].to_broadcast([P, NC]), ACT.Exp,
                                          scale=float(CH))
                    last.then_inc(sem("ret_factors"), 1)
                handover("act", act)

            def scan(l, g):
                inst = 2 * l + g
                for a, b in SCANS:
                    with act.Fori(0, (b - a) // 2) as pair:
                        i = a + 2 * pair
                        for p in range(2):
                            n = inst * NC + i + p
                            for d in range(2):
                                act.wait_ge(sem(f"kd_turned{d}"), n + 1)
                                act.wait_ge(sem(f"u_made{d}"), n + 1)
                                nc.scalar.copy(KDT[d], bank(2 + d, P, CH)).then_inc(sem(f"kd_kept{d}"), 1)
                            for d in range(2):
                                act.wait_ge(sem(f"o_made{d}"), n + 3)
                                nc.scalar.copy(in_turn(region(R_O, NC, 256)[d * CH:(d + 1) * CH], d, a, b)[:, 2 * pair + p, :], bank(4 + d, 256, CH)
                                               ).then_inc(sem(f"o_kept{d}"), 1)
                handover("act", act)

            def stack(l):
                qk = region(R_QKD, 4, N)
                nc.scalar.copy(region_r(K_HI, 2, N), qk[:, 2:4, :]).then_inc(sem("qk_hi"), 1)
                nc.scalar.copy(region_r(Q_HI, 2, N), qk[:, 0:2, :]).then_inc(sem("qk_hi"), 1)
                act.drain()
                for c in range(2):
                    for j in range(NH):
                        nc.scalar.copy(K_STACK[c][0:DK, j, :], region_r(K_HI, 2, N)[j * DK:(j + 1) * DK, c, :].bitcast(F32))
                handover("act", act)

            def attend(l):
                for first, count, base, nk in att_loops(l):
                    def step(m, i, of_join, of_values, of_turn):
                        if i is not None:
                            T = base + i
                            act.wait_ge(sem("max_ready"), MAPS * T + m + 1)
                            act.wait_ge(sem("turned"), OUTS * T + (m // 2 + 3 if m < 4 else m + 1 if m < 8 else m // 2 + 5))
                            for j, name in enumerate(("head_done", "exp_done")):
                                a, b = exp_parts(nk)[j:j + 2]
                                activation(A_P[m % 4][:, a:b], psum[:, a:b], ACT.Exp, bias=A_NM[:, m:m + 1],
                                           accum_out=A_L[:, m, j:j + 1]).then_inc(sem(name), 1)
                        if of_turn:
                            n, o = OUTS * (base + of_turn[0]) + of_turn[1], of_turn[1]
                            act.wait_ge(sem("turned"), n + 5)
                            act.wait_ge(sem("pv_made"), n + 1)
                            w = 4 if nk == NT else 1
                            nc.scalar.copy(A_PT[o % 2][:, 0:w, :].rearrange("p a b -> p (a b)"),
                                           psum[:, TURNED:TURNED + w * P]).then_inc(sem("pt_act"), 1)
                    att_tiles(act, count, step)
                handover("act", act)

            def finish(l):
                c0, count, base = fin_loop(l)

                def square(t, s):
                    T = 2 * base + t
                    act.wait_ge(sem("fin_sum"), T + 1)
                    act.wait_ge(sem("fin_ss"), T + 1)
                    activation(F_SQ, F_HM[s], ACT.Square).then_inc(sem("fin_sq"), 1)
                    act.wait_ge(sem("fin_ready"), T + 1)
                    activation(F_SG[s], F_G[s], ACT.Silu)

                def rstd(t, s):
                    T = 2 * base + t
                    act.wait_ge(sem("fin_ss"), T + 2)
                    activation(F_RS[s], F_SS, ACT.Ln, scale=1.0 / HD, bias=eps[:, 0:1])
                    act.drain()
                    activation(F_RS[s], F_RS[s], ACT.Exp, scale=-0.5).then_inc(sem("fin_rs"), 1)

                def keep_rows(t, s):
                    act.wait_ge(sem("rows_made"), t + 3)
                    act.wait_ge(sem("rows_turned"), t + 1)
                    nc.scalar.copy(F_ROWS, psum[0:2, 4 * BANK:(4 + ADA_T) * BANK]).then_inc(sem("rows_kept"), 1)

                def keep(t, s):
                    act.wait_ge(sem("fin_turned"), 2 * base + t + 3)
                    for b in range(2):
                        last = nc.scalar.copy(region_r(MIX_HI, KD, NT, P)[:, 4 * b:4 * b + 4, c0 + t, :],
                                              bank(2 * s + b).rearrange("p (j c) -> p j c", j=4))
                    last.then_inc(sem("fin_kept_a"), 1)
                in_steps(act, count, ([(1, keep_rows)] if l == 0 else []) + [(0, square), (0, rstd), (1, keep)])
                handover("act", act)

            def project_back(l, block=None):
                per, kk, _, dst_at, w_at, units, chunks, t0, n = back(l, block)
                raw, hi, _ = unit_slots(w_at, block, kk * P)

                def chunk(c, s, is_first):
                    for j in range(per):
                        m = units + per * c + j
                        slot = j if per == 2 else s
                        act.wait_ge(sem(f"wb_in{slot}"), 8 * (m - slot) + 16)
                        act.wait_ge(sem("yb_made"), m + 1)
                        nc.scalar.copy(region_r(hi[slot], kk * P), region(raw[slot], kk * P)
                                       ).then_inc(sem("wb_hi"), 1)
                    if not is_first:
                        keep(c - 1, 1 - s)

                def keep(c, s):
                    act.wait_ge(sem("sq_added"), chunks + c + 1)
                    act.wait_ge(sem("yb_made"), units + per * (c + 1) + 2)
                    activation(region(SQ_NEW, N)[:, t0:t0 + n], psum[:, 3 * s * BANK:3 * s * BANK + n], ACT.Square
                               ).then_inc(sem("sq_made"), 1)
                    nc.scalar.copy(region(dst_at, KD, N)[:, c, t0:t0 + n], psum[:, 3 * s * BANK:3 * s * BANK + n]
                                   ).then_inc(sem("yb_kept"), 1)
                for s in range(2):
                    chunk(s, s, s == 0)
                with act.Fori(1, KD // 2) as u:
                    for s in range(2):
                        chunk(2 * u + s, s, False)
                keep(KD - 1, 1)
                handover("act", act)

            def hidden(l, block):
                index, t0, n = block

                def part(u, half):
                    act.wait_ge(sem(f"wf_in{half}"), 16 * (index * KH + u + 1))
                    act.wait_ge(sem("up_made" if half else "gate_made"), index * KH + u + 1)
                    nc.scalar.copy(region_r(WF[half][1], KD * P), region(WF[half][0], KD * P)
                                   ).then_inc(sem(f"wf_hi{half}"), 1)

                def gate(u):
                    act.wait_ge(sem("gate_made"), index * KH + u + 2)
                    act.wait_ge(sem("up_done"), index * KH + u + 1)
                    activation(region(SILU_AT, n), bank(0, n), ACT.Silu).then_inc(sem("silu_done"), 1)

                def product_part(u):
                    act.wait_ge(sem("up_done"), index * KH + u + 2)
                    nc.scalar.copy(region_r(ACT_HI, KH, FFN_T)[:, u, 0:n], region(ACT_LO, KH, FFN_T)[:, u, 0:n]
                                   ).then_inc(sem("act_hi"), 1)
                part(0, 0)
                part(0, 1)
                activation(silu_warm[:], eps[:], ACT.Silu)
                with act.Fori(1, KH) as u:
                    part(u, 0)
                    gate(u - 1)
                    part(u, 1)
                    product_part(u - 1)
                gate(KH - 1)
                product_part(KH - 1)
                handover("act", act)

            first_modulation()
            norm(0)
            for l in range(DEPTH):
                project(l)
                prepare(l)
                for g in range(2):
                    scan_factors(l, g)
                    scan(l, g)
                stack(l)
                attend(l)
                finish(l)
                project_back(l)
                norm(2 * l + 1)
                for block_ in blocks(l):
                    hidden(l, block_)
                    project_back(l, block_)
                norm(2 * l + 2)

        @block.vector
        def _(dve):
            v = nc.vector
            free("dve", dve)
            v.memset(eps[:], EPS)
            v.memset(ones[:], 1.0).then_inc(sem("const_set"), 1)
            dve.wait_ge(sem("const_in"), 16 * 9)

            def keep_modulation(src, first, n_m):
                return v.tensor_tensor(mods_f[:, bass.ds(first, n_m), :], src.rearrange("p (m s) -> p m s", s=2),
                                       ada_b[:, bass.ds(first, n_m)].unsqueeze(2).to_broadcast([P, n_m, 2]), ALU.add)

            def with_gain(l, row, gain):
                for st in range(2):
                    m = mods_v[:, l, row, :, st]
                    if row % 3 == 1:
                        v.scalar_tensor_tensor(out=m, in0=m, scalar=1.0, in1=gains_v[:, l, gain, :], op0=ALU.add, op1=ALU.mult)
                    else:
                        v.tensor_tensor(m, m, gains_v[:, l, gain, :], ALU.mult)

            def first_modulation():
                dve.wait_ge(sem("ada0_turned"), 1)
                keep_modulation(bank(4, 2 * ADA_FIRST), 0, ADA_FIRST)
                dve.drain()
                with_gain(0, 1, 0)
                handover("dve", dve)

            def rest(lo, x, hi):
                return v.tensor_tensor(lo, x, hi.bitcast(F32), ALU.subtract)

            def rest_of_h(i, k, c0):
                dve.wait_ge(sem("h_made"), KD * i + k + 1)
                shift = mods_v[:, NORMS[i]["pre_layer"], NORMS[i]["pre"], k]
                for st, a, b in streams(c0):
                    v.scalar_tensor_tensor(out=region_r(H_LO, KD, N)[:, k, a:b], in0=region(R_H, KD, N)[:, k, a:b],
                                           scalar=shift[:, st:st + 1], in1=region_r(H_HI, KD, N)[:, k, a:b].bitcast(F32),
                                           op0=ALU.add, op1=ALU.subtract)

            def norm(i):
                n = NORMS[i]
                c0 = n["c0"]
                x, h = region(X_AT, KD, N), region(R_H, KD, N)
                if n["y"] is not None:
                    y, r = region(n["y"], KD, N), region(N_RS, N)
                    dve.wait_ge(sem("rstd_ready"), rs_count[i] + 1)
                    for k in range(KD):
                        tmp = region(N_TMP, 2, N)[:, k % 2, :]
                        v.tensor_tensor(tmp[:, c0:N], y[:, k, c0:N], r[:, c0:N], ALU.mult)
                        dve.wait_ge(sem(f"x_in{k}"), 16 * (i + 1))
                        dve.drain()
                        for st, a, b in streams(c0):
                            last = v.scalar_tensor_tensor(out=x[:, k, a:b], in0=tmp[:, a:b],
                                                          scalar=mods_v[:, n["layer"], n["gate"], k, st:st + 1],
                                                          in1=x[:, k, a:b], op0=ALU.mult, op1=ALU.add)
                        last.then_inc(sem("x_new"), 1)
                if n["pre"] is not None:
                    pas = int(n["y"] is not None)
                    r = region(N_RS + pas * N, N)
                    dve.wait_ge(sem("rstd_ready"), rs_count[i] + pas + 1)
                    for k in range(KD):
                        dve.wait_ge(sem(f"x_in{k}"), 16 * (i + 1))
                        scale = mods_v[:, n["pre_layer"], n["pre"] + 1, k]
                        for st, a, b in streams(c0):
                            last = v.scalar_tensor_tensor(out=h[:, k, a:b], in0=x[:, k, a:b], scalar=scale[:, st:st + 1],
                                                          in1=r[:, a:b], op0=ALU.mult, op1=ALU.mult)
                        last.then_inc(sem("h_normed"), 1)
                        if k >= 1:
                            rest_of_h(i, k - 1, c0)
                    rest_of_h(i, KD - 1, c0)
                handover("dve", dve)

            def project(l):
                v.memset(wgate, 0.0).then_inc(sem("wgate_zero"), 1)

                def part(c, s):
                    dve.wait_ge(sem("win_hi"), l * IN_CHUNKS + c + 1)
                    lo = WIN_LO + s * KD * IN_C
                    rest(region_r(lo, KD * IN_C), region(lo, KD * IN_C), region_r(WIN_HI + s * KD * IN_C, KD * IN_C)
                         ).then_inc(sem("win_ready"), 1)

                def chunk(u, s, is_last):
                    for j in range(5):
                        n = 5 * s + j
                        if j == 2 and not is_last:
                            part(2 * u + s + 1, 1 - s)
                        if j == 0:
                            dve.wait_ge(sem("proj_out"), 16 * (l * IN_CHUNKS + 2 * u + s + 1))
                        dve.wait_ge(sem("in_made1"), l * 40 + u * 10 + n + 11)
                        v.tensor_copy(region(WIN_OUT, NT, IN_C)[:, 2 * j + 1, :], bank(2 + n % 2, IN_C)
                                      ).then_inc(sem("in_kept1"), 1)
                part(0, 0)
                with dve.Fori(0, IN_CHUNKS // 2 - 1) as u:
                    for s in range(2):
                        chunk(u, s, False)
                for s in range(2):
                    chunk(IN_CHUNKS // 2 - 1, s, s == 1)
                handover("dve", dve)

            def rotate(out, x, scratch, tok, nh):
                xc, xs = scratch
                half = DK // 2
                cos, sin = (rope_t[:, tok, w:w + 1, :].to_broadcast([P, nh, DK]) for w in range(2))
                v.tensor_tensor(xc, x, cos, ALU.mult)
                v.tensor_tensor(xs, x, sin, ALU.mult)
                dve.drain()
                v.tensor_tensor(out[:, :, 0:half], xc[:, :, 0:half], xs[:, :, half:DK], ALU.subtract)
                return v.tensor_tensor(out[:, :, half:DK], xc[:, :, half:DK], xs[:, :, 0:half], ALU.add)

            def prepare(l):
                dve.wait_ge(sem("small_in"), 160 * (l + 1))
                lam_q = lam_v.rearrange("p (m w d) -> p m w d", m=2, w=2)
                v.tensor_tensor(lam_p.rearrange("p (m d) -> p m d", m=2), lam_q[:, :, 0, :], lam_q[:, :, 1, :], ALU.mult)
                v.scalar_tensor_tensor(out=dec_t[:], in0=dec_in[:], scalar=-1.0, in1=dec_in[:], op0=ALU.mult, op1=ALU.max)
                dve.drain()
                v.tensor_reduce(lam_s[:], lam_p.rearrange("p (m d) -> p m d", m=2), AX.X, ALU.add
                                ).then_inc(sem("dec_abs"), 1)
                dve.wait_ge(sem("dec_ln"), l + 1)
                v.scalar_tensor_tensor(out=neg_lam[:], in0=lam_e[:, 1:2], scalar=-lambda_init(l), in1=lam_e[:, 0:1],
                                       op0=ALU.add, op1=ALU.subtract)
                v.scalar_tensor_tensor(out=log_dec[:], in0=dec_in[:], scalar=0.0, in1=dec_t[:], op0=ALU.min,
                                       op1=ALU.subtract).then_inc(sem("log_dec_ready"), 1)

                def rotate_tile(t, s):
                    T = l * NT + t

                    def cols(name, n):
                        return T_IN[s][:, COL[name]:COL[name] + n * DK].rearrange("p (h d) -> p h d", h=n)
                    dve.wait_ge(sem(f"tile_in{s}"), 8 * (T - s) + 16)
                    dve.wait_ge(sem("turned1"), T + 2)
                    rotate(T_RD, cols("dq", 16), T_S[0], t, 16)
                    rotate(T_RM[s], cols("mr", 1), T_S[1], t, 1)
                    rotate(T_RR, cols("rq", 8), T_S[2], t, 8).then_inc(sem("roped"), 1)

                def keep_diff(t, s):
                    T = l * NT + t
                    dve.wait_ge(sem("turned1"), T + 3)
                    qk = region(R_QKD, 4, NT, P)
                    turned = bank(0).rearrange("p (j c) -> p j c", j=4)
                    v.tensor_scalar(qk[:, 0:2, t, :], turned[:, 0:2, :], DK ** -0.5, None, ALU.mult)
                    v.tensor_copy(qk[:, 2:4, t, :], turned[:, 2:4, :]).then_inc(sem("kept0"), 1)

                def keep_queries(t, s):
                    T = l * NT + t
                    dve.wait_ge(sem("turned3"), T + 1)
                    v.tensor_copy(T_MK[:, :, HD:MQ], T_RM[s].to_broadcast([P, NH, DK]))
                    dve.wait_ge(sem("made2"), T + 2)
                    q = bank(3, NH * MQ).rearrange("p (h d) -> p h d", h=NH)
                    v.tensor_copy(T_MQ[:, :, 0:HD], q[:, :, 0:HD])
                    rotate(T_MQ[:, :, HD:MQ], q[:, :, HD:MQ], T_S[3], t, NH).then_inc(sem("mq_ready"), 1)

                def keep_turned(t, s):
                    dve.wait_ge(sem("turned3"), l * NT + t + 2)
                    v.tensor_scalar(region(R_QM, 4, NT, P, parts=MQ)[:, :, t, :],
                                    bank(6, parts=MQ).rearrange("p (j c) -> p j c", j=4), MQ ** -0.5, None, ALU.mult
                                    ).then_inc(sem("kept6"), 1)
                in_steps(dve, NT, [(2, keep_queries), (3, keep_turned), (1, keep_diff), (0, rotate_tile)])
                handover("dve", dve)

            def scan_factors(l, g):
                q = region(R_GR, 4, NC, CH)[:, 2 * g]
                k = region(R_GR, 4, NC, CH)[:, 2 * g + 1]
                s = DK ** -0.5
                if g == 0:
                    z = region(R_GZ, 2 * N)
                    a, b = region(R_H, 2 * N), region(R_H + 2 * N, 2 * N)
                    v.scalar_tensor_tensor(out=a, in0=z, scalar=-1.0, in1=z, op0=ALU.mult, op1=ALU.max
                                           ).then_inc(sem("gate_abs"), 1)
                    v.memset(RESET, 1.0)
                    dve.drain()
                    v.memset(RESET.rearrange("p (c i) -> p c i", c=NC)[:, :, 0:1], 0.0)
                    v.tensor_copy(mask[:], causal[:])
                    dve.wait_ge(sem("gate_ln"), l + 1)
                    v.scalar_tensor_tensor(out=a, in0=z, scalar=0.0, in1=b, op0=ALU.min, op1=ALU.subtract)
                    dve.drain()
                    v.tensor_scalar(z, a, 1.0 / GATE_NORM, None, ALU.mult)
                    dve.drain()
                    x1, x2, x3 = (x.rearrange("p (c i) -> p c i", c=NC) for x in (T1, T2, T3))
                    for d in range(2):
                        if d:
                            dve.wait_ge(sem("factors"), 2 * l + d)
                        la = region(R_GZ, 2, N)[:, d, :]
                        v.tensor_tensor_scan(T1, RESET, la, 0.0, ALU.mult, ALU.add)
                        dve.drain()
                        if d == 0:
                            e, mid = x1, x1[:, :, CH // 2 - 1:CH // 2]
                        else:
                            v.tensor_tensor(la, T1, la, ALU.subtract)
                            dve.drain()
                            e = la.rearrange("p (c i) -> p c i", c=NC)
                            mid = e[:, :, CH // 2:CH // 2 + 1]
                        v.tensor_tensor(x2, e, mid.to_broadcast([P, NC, CH]), ALU.subtract)
                        v.tensor_tensor(x3, e, x1[:, :, CH - 1:CH].to_broadcast([P, NC, CH]), ALU.subtract)
                        dve.drain()
                        v.tensor_scalar(T2, T2, LIMIT, -LIMIT, ALU.min, ALU.max).then_inc(sem("exponents"), 1)
                        dve.wait_ge(sem("factors"), 2 * l + d + 1)
                        for j, src, f in ((QS, q, s), (KS, k, 1.0), (QD, q, s), (KDE, k, 1.0)):
                            v.scalar_tensor_tensor(out=E[d][:, :, j, :], in0=E[d][:, :, j, :], scalar=f, in1=src,
                                                   op0=ALU.mult, op1=ALU.mult)
                else:
                    dve.wait_ge(sem("ret_factors"), l + 1)
                    v.tensor_tensor(mask[:], mask[:], causal[:], ALU.mult)
                    for d in range(2):
                        eq, ek = (edge[:, (2 * d + w) * CH:(2 * d + w + 1) * CH].unsqueeze(1).to_broadcast([P, NC, CH])
                                  for w in range(2))
                        v.tensor_copy(E[d][:, :, QS, :], q)
                        v.tensor_scalar(E[d][:, :, KS, :], k, s, None, ALU.mult)
                        v.tensor_tensor(E[d][:, :, QD, :], q, eq, ALU.mult)
                        v.scalar_tensor_tensor(out=E[d][:, :, KDE, :], in0=k, scalar=s, in1=ek, op0=ALU.mult, op1=ALU.mult)
                handover("dve", dve)

            def scan(l, g):
                inst = 2 * l + g
                for d in range(2):
                    v.memset(STATE[d], 0.0).then_inc(sem(f"state_ready{d}"), 1)
                own = heads[:].unsqueeze(2).to_broadcast([P, NH, HD])
                for a, b in SCANS:
                    with dve.Fori(0, (b - a) // 2) as pair:
                        i = a + 2 * pair
                        for p in range(2):
                            n = inst * NC + i + p
                            for d in range(2):
                                dve.wait_ge(sem(f"sc_made{d}"), n + 1)
                                dve.wait_ge(sem(f"o_made{d}"), n + 2)
                                v.tensor_tensor(SCM[d].rearrange("p h i -> p (h i)"), bank(d, NH * CH, CH),
                                                mask[:, d * NH * CH:(d + 1) * NH * CH], ALU.mult
                                                ).then_inc(sem(f"scm_ready{d}"), 1)
                            for d in range(2):
                                dve.wait_ge(sem(f"u_made{d}"), n + 2)
                                v.tensor_tensor(UM[d], bank(6 + d, NH * HD).rearrange("p (h e) -> p h e", h=NH), own,
                                                ALU.mult)
                                dve.drain()
                                v.scalar_tensor_tensor(out=STATE[d], in0=STATE[d], scalar=in_turn(dec_v[:, d, :], d, a, b)[:, bass.ds(2 * pair + p, 1)],
                                                       in1=UM[d].rearrange("p h e -> p (h e)"), op0=ALU.mult, op1=ALU.add
                                                       ).then_inc(sem(f"state_ready{d}"), 1)
                handover("dve", dve)

            def stack(l):
                qk = region(R_QKD, 4, N)
                dve.wait_ge(sem("qk_hi"), 2 * l + 1)
                rest(region_r(K_LO, 2, N), qk[:, 2:4, :], region_r(K_HI, 2, N))
                dve.wait_ge(sem("qk_hi"), 2 * l + 2)
                rest(region_r(R_QKD, 2, N), qk[:, 0:2, :], region_r(Q_HI, 2, N))
                dve.drain()
                for c in range(2):
                    for j in range(NH):
                        v.tensor_copy(K_STACK[c][DK:2 * DK, j, :], region_r(K_LO, 2, N)[j * DK:(j + 1) * DK, c, :].bitcast(F32))
                handover("dve", dve)

            def attend(l):
                for first, count, base, nk in att_loops(l):
                    def join_maps(i, o):
                        m, c = NH + 2 * (o - NH), o - NH
                        dve.wait_ge(sem("exp_done"), (base + i) * MAPS + m + 3)
                        v.tensor_tensor(A_LS[:, m:m + 2], A_L[:, m:m + 2, 0], A_L[:, m:m + 2, 1], ALU.add)
                        dve.drain()
                        v.reciprocal(A_SC[:, c:c + 1], A_LS[:, m + 1:m + 2])
                        v.tensor_tensor(A_NL[:, c:c + 1], A_LS[:, m:m + 1], neg_lam[:], ALU.mult)
                        dve.drain()
                        v.tensor_tensor(A_SC[:, c:c + 1], A_NL[:, c:c + 1], A_SC[:, c:c + 1], ALU.mult)
                        dve.drain()
                        a, b = (A_P[2 * (o % 2) + j][:, 0:nk * P] for j in range(2))
                        v.scalar_tensor_tensor(out=a, in0=b, scalar=A_SC[:, c:c + 1], in1=a, op0=ALU.mult, op1=ALU.add
                                               ).then_inc(sem("maps_joined"), 1)

                    def keep_values(i, o):
                        rl = A_RL[:, o:o + 1]
                        m = o if o < NH else NH + 2 * (o - NH)
                        if o < NH:
                            v.tensor_tensor(A_LS[:, m:m + 1], A_L[:, m, 0:1], A_L[:, m, 1:2], ALU.add)
                            dve.drain()
                        v.reciprocal(rl, A_LS[:, m:m + 1])
                        dve.drain()
                        dve.wait_ge(sem("pv_made"), OUTS * (base + i) + o + 3)
                        at = (o + NH) % OUTS * HD
                        v.tensor_scalar(A_OUT[:, first + i, at:at + HD], bank(6 + o % 2, HD), rl, None, ALU.mult
                                        ).then_inc(sem("att_kept"), 1)

                    def step(m, i, of_join, of_values, of_turn):
                        if i is not None:
                            pieces = score_pieces(nk)
                            for j, (c, w, n, _) in enumerate(pieces):
                                dve.wait_ge(sem("scored"), 3 * (MAPS * (base + i) + m) + n * (j + 1))
                                v.tensor_reduce(A_CM[:, j:j + 1], psum[:, c:c + w], AX.X, ALU.max)
                            dve.drain()
                            v.tensor_reduce(A_NM[:, m:m + 1], A_CM[:, 0:len(pieces)], AX.X, ALU.max, negate=True
                                            ).then_inc(sem("max_ready"), 1)
                        if of_join:
                            join_maps(*of_join)
                        if of_values:
                            keep_values(*of_values)
                        if of_turn:
                            n, o = OUTS * (base + of_turn[0]) + of_turn[1], of_turn[1]
                            dve.wait_ge(sem("turned"), n + 5)
                            dve.wait_ge(sem("pv_made"), n + 1)
                            w0, w1 = (4, NT) if nk == NT else (1, 2)
                            v.tensor_copy(A_PT[o % 2][:, w0:w1, :].rearrange("p a b -> p (a b)"),
                                          psum[:, TURNED + BANK:TURNED + BANK + (w1 - w0) * P]).then_inc(sem("pt_dve"), 1)
                    att_tiles(dve, count, step)
                handover("dve", dve)

            def finish(l):
                c0, count, base = fin_loop(l)
                dve.wait_ge(sem("outg_in"), 16 * (l + 1))
                v.tensor_scalar(F_OUTG[:, 0:256], F_OUTG[:, 0:256], 1.0 - lambda_init(l), None, ALU.mult)
                dve.drain()

                def sum_scans(t, s):
                    hm = F_HM[s]
                    dve.wait_ge(sem(f"fin_in{s}"), 80 * base + 40 * (t - s) + 80)
                    v.tensor_tensor(hm[:, 512:1024], hm[:, 512:1024], F_SB[s], ALU.add).then_inc(sem("fin_sum"), 1)

                def sum_squares(t, s):
                    T = 2 * base + t
                    dve.wait_ge(sem("fin_rs"), T + 1)
                    dve.wait_ge(sem("fin_sq"), T + 1)
                    v.tensor_reduce(F_SS, F_SQ.rearrange("p (h d) -> p h d", h=16), AX.X, ALU.add
                                    ).then_inc(sem("fin_ss"), 1)

                def scale(t, s):
                    T = 2 * base + t
                    hm = F_HM[s]
                    dve.wait_ge(sem("fin_rs"), T + 2)
                    for a, b in ((0, 4), (8, 16)):
                        hv = hm[:, a * HD:b * HD].rearrange("p (h d) -> p h d", d=HD)
                        v.tensor_tensor(hv, hv, F_RS[s][:, a:b].unsqueeze(2).to_broadcast([P, b - a, HD]), ALU.mult)
                    dve.drain()
                    v.tensor_tensor(hm[:, 0:256], hm[:, 0:256], F_OUTG[:, 0:256], ALU.mult)
                    v.tensor_tensor(hm[:, 512:1024], hm[:, 512:1024], F_OUTG[:, 512:1024], ALU.mult)
                    dve.drain()
                    v.tensor_tensor(hm[:, 512:1024], hm[:, 512:1024], F_SG[s], ALU.mult).then_inc(sem("fin_ready"), 1)

                def keep(t, s):
                    dve.wait_ge(sem("fin_kept_a"), 2 * base + t + 3)
                    for b in range(2):
                        last = rest(region_r(MIX_LO, KD, NT, P)[:, 4 * b:4 * b + 4, c0 + t, :],
                                    bank(2 * s + b).rearrange("p (j c) -> p j c", j=4),
                                    region_r(MIX_HI, KD, NT, P)[:, 4 * b:4 * b + 4, c0 + t, :])
                    last.then_inc(sem("fin_kept_v"), 1)

                def keep_columns(t, s):
                    dve.wait_ge(sem("rows_turned"), t + 2)
                    n_m = ADA_T * ADA_M
                    keep_modulation(bank(6, 2 * n_m), ADA_FIRST + n_m * t, n_m).then_inc(sem("ada_kept"), 1)
                in_steps(dve, count, [(1, scale), (0, sum_scans), (2, keep)] + ([(2, keep_columns)] if l == 0 else [])
                         + [(0, sum_squares)])
                if l == 0:
                    dve.drain()
                    for ll in range(DEPTH):
                        for row, gain in ((1, 0), (2, 1), (4, 2), (5, 3)):
                            if (ll, row) != (0, 1):
                                with_gain(ll, row, gain)
                handover("dve", dve)

            def project_back(l, block=None):
                per, kk, _, _, w_at, units, chunks, t0, n = back(l, block)
                raw, hi, lo = unit_slots(w_at, block, kk * P)
                total, new = (region(at, N)[:, t0:t0 + n] for at in (SQ_SUM, SQ_NEW))

                def chunk(c, s):
                    for j in range(per):
                        slot = j if per == 2 else s
                        dve.wait_ge(sem("wb_hi"), units + per * c + j + 1)
                        rest(region_r(lo[slot], kk * P), region(raw[slot], kk * P), region_r(hi[slot], kk * P)
                             ).then_inc(sem("wb_ready"), 1)

                def add(c):
                    dve.wait_ge(sem("sq_made"), chunks + c + 1)
                    v.tensor_tensor(total, total, new, ALU.add).then_inc(sem("sq_added"), 1)
                chunk(0, 0)
                chunk(1, 1)
                dve.wait_ge(sem("sq_made"), chunks + 1)
                v.tensor_copy(total, new).then_inc(sem("sq_added"), 1)
                with dve.Fori(1, KD // 2) as u:
                    for s in range(2):
                        chunk(2 * u + s, s)
                        add(2 * u + s - 1)
                add(KD - 1)
                handover("dve", dve)

            def hidden(l, block):
                index, t0, n = block

                def part(u, half):
                    dve.wait_ge(sem(f"wf_hi{half}"), index * KH + u + 1)
                    raw, hi, lo = WF[half]
                    rest(region_r(lo, KD * P), region(raw, KD * P), region_r(hi, KD * P)
                         ).then_inc(sem(f"wf_ready{half}"), 1)

                def product(u):
                    dve.wait_ge(sem("up_made"), index * KH + u + 2)
                    dve.wait_ge(sem("silu_done"), index * KH + u + 2)
                    x = region(ACT_LO, KH, FFN_T)[:, u, 0:n]
                    v.tensor_tensor(x, region(SILU_AT, n), bank(1, n), ALU.mult).then_inc(sem("up_done"), 1)
                    dve.wait_ge(sem("act_hi"), index * KH + u + 1)
                    rest(region_r(ACT_LO, KH, FFN_T)[:, u, 0:n], x, region_r(ACT_HI, KH, FFN_T)[:, u, 0:n])
                part(0, 0)
                part(0, 1)
                with dve.Fori(1, KH) as u:
                    part(u, 0)
                    part(u, 1)
                    product(u - 1)
                product(KH - 1)
                handover("dve", dve)

            first_modulation()
            norm(0)
            for l in range(DEPTH):
                project(l)
                prepare(l)
                for g in range(2):
                    scan_factors(l, g)
                    scan(l, g)
                stack(l)
                attend(l)
                finish(l)
                project_back(l)
                norm(2 * l + 1)
                for block_ in blocks(l):
                    hidden(l, block_)
                    project_back(l, block_)
                norm(2 * l + 2)

        @block.gpsimd
        def _(pool):
            def idle():
                handover("pool", pool)

            def scan(l, g):
                inst = 2 * l + g
                own = heads[:].unsqueeze(2).to_broadcast([P, NH, CH])
                for a, b in SCANS:
                    with pool.Fori(0, (b - a) // 2) as pair:
                        i = a + 2 * pair
                        for p in range(2):
                            n = inst * NC + i + p
                            for d in range(2):
                                pool.wait_ge(sem(f"o_made{d}"), n + 1)
                                nc.gpsimd.tensor_copy(EST[d][p], in_turn(E[d], d, a, b)[:, 2 * pair + p, 0:3, :])
                                nc.gpsimd.tensor_tensor(QBD[d][p], in_turn(E[d], d, a, b)[:, 2 * pair + p, QS:QS + 1, :].to_broadcast([P, NH, CH]), own,
                                                        ALU.mult).then_inc(sem(f"est_ready{d}"), 1)
                handover("pool", pool)

            def stack(l):
                pool.wait_ge(sem("qk_hi"), 2 * l + 1)
                for c in range(2):
                    for j in range(NH):
                        pool.drain()
                        nc.gpsimd.tensor_copy(K_STACK[c][2 * DK:3 * DK, j, :], region_r(K_HI, 2, N)[j * DK:(j + 1) * DK, c, :].bitcast(F32))
                handover("pool", pool)

            def attend(l):
                for first, count, base, nk in att_loops(l):
                    def tile(i, is_first):
                        before = MAPS * (base + i)
                        if not is_first:
                            pool.wait_ge(sem("scored"), 3 * (before - 2 * NH))
                        elif before:
                            pool.wait_ge(sem("scored"), 3 * before)
                        nc.gpsimd.tensor_copy(A_QM, region(R_QM, 4, NT, P, parts=MQ)[:, :, first + i, :]
                                              ).then_inc(sem("qm_staged"), 1)
                        pool.drain()
                        if not is_first:
                            pool.wait_ge(sem("scored"), 3 * before)
                        for part, at in enumerate((Q_HI, Q_HI, R_QKD)):
                            for j in range(NH):
                                src = region_r(at, 2, NT, P)[j * DK:(j + 1) * DK, :, first + i, :]
                                nc.gpsimd.tensor_copy(Q_STACK[part * DK:(part + 1) * DK, :, j, :], src.bitcast(F32))
                                last = pool.drain()
                        last.then_inc(sem("qd_staged"), 1)
                    tile(0, True)
                    with pool.Fori(1, count) as i:
                        tile(i, False)
                handover("pool", pool)

            def finish(l):
                if l == 0:
                    with pool.Fori(0, NT // 2) as u:
                        for s in range(2):
                            pool.wait_ge(sem("rows_made"), 2 * u + s + 1)
                            for j in range(ADA_T):
                                pool.dma_start(F_ADA[s][:, j, :, :].rearrange("p k n -> p (k n)"),
                                               t["ada_w"][ADA_FIRST // ADA_M + ADA_T * (2 * u + s) + j]
                                               ).then_inc(sem(f"ada_in{s}"), 16)
                handover("pool", pool)

            idle()
            idle()
            pool.wait_ge(sem("const_in"), 16 * 9)
            for l in range(DEPTH):
                idle()
                idle()
                for g in range(2):
                    idle()
                    scan(l, g)
                stack(l)
                attend(l)
                finish(l)
                for _ in range(3 + 2 * len(blocks(l))):
                    idle()


def constants():
    import numpy as np
    c = {"c_ident": np.eye(P, dtype=np.float32)}
    tok = np.arange(LAT)
    row, col = (tok // 64).astype(np.float32), (tok % 64).astype(np.float32)
    nf = DK // 4
    freqs = (np.float32(10000.0) ** (-np.arange(nf, dtype=np.float32) / nf)).astype(np.float32)
    ang = np.concatenate([row[:, None] * freqs, col[:, None] * freqs], -1).astype(np.float32)
    cos, sin = np.ones((N, DK), np.float32), np.zeros((N, DK), np.float32)
    cos[CTX:] = np.tile(np.cos(ang), (1, 2))
    sin[CTX:] = np.tile(np.sin(ang), (1, 2))
    both = np.stack([cos, sin], 1).reshape(NT, P, 2, DK)
    c["c_rope"] = np.ascontiguousarray(both.transpose(1, 0, 2, 3)).reshape(P, -1)
    part = np.arange(P)
    c["c_heads"] = (part[:, None] // DK == np.arange(NH)[None, :]).astype(np.float32)
    j, i = np.arange(CH)[:, None], np.arange(CH)[None, :]
    dist = np.stack([i - j, j - i], 1)
    seen = (dist >= 0).astype(np.float32)
    c["c_causal"] = np.ascontiguousarray(np.broadcast_to(seen[:, :, None, :], (CH, 2, NH, CH))).reshape(CH, -1)
    c["c_rel"] = np.maximum(dist, 0).astype(np.float32).reshape(CH, -1)
    at = np.arange(CH, dtype=np.float32)
    edges = np.stack([at + 1, CH - 1 - at, CH - at, at])
    c["c_steps"] = np.ascontiguousarray(np.broadcast_to(edges.reshape(1, -1), (P, 4 * CH)))
    return c


def laid_out(i):
    import numpy as np
    a = {k: np.asarray(v) for k, v in i.items()}

    def on_parts(w, lead):
        s = w.shape
        w = w.reshape(s[:lead] + (s[lead] // P, P) + s[lead + 1:])
        return np.moveaxis(w, lead + 1, lead)

    def chunked(w, n_chunks):
        w = on_parts(w, 1)
        w = w.reshape(w.shape[:3] + (n_chunks, -1)).transpose(0, 3, 1, 2, 4)
        return np.ascontiguousarray(w).reshape(DEPTH, n_chunks, P, -1)
    r = constants()
    r["x"] = np.ascontiguousarray(on_parts(np.concatenate([a["ctx"][0], a["x"][0]], 0).T, 0))
    r["cond"] = np.ascontiguousarray(on_parts(np.stack([a["c"][0], a["c_ctx"]], 1), 0)).reshape(P, -1)
    r["norm_g"] = np.ascontiguousarray(a["norm_g"].reshape(DEPTH, 4, KD, P).transpose(3, 0, 1, 2)).reshape(P, -1)
    r["ada_b"] = np.ascontiguousarray(a["ada_b"].reshape(DEPTH, 6 * KD, P).transpose(2, 0, 1)).reshape(P, -1)
    r["ada_w"] = chunked(a["ada_w"], 6 * KD // ADA_M).reshape(-1, P, KD * BANK)
    r["w_in"] = chunked(a["w_in"], IN_CHUNKS)
    r["w_out"] = chunked(a["w_out"], KD)
    r["ffn_out"] = chunked(a["ffn_w_out"], KD)
    g = on_parts(a["ffn_w_in"], 1).reshape(DEPTH, P, KD, 2, KH, P).transpose(0, 4, 3, 1, 2, 5)
    r["ffn_in"] = np.ascontiguousarray(g).reshape(DEPTH, KH, 2, P, -1)
    r["w_uq"] = np.ascontiguousarray(on_parts(a["mla_w_uq"], 1))
    r["w_ukv"] = a["mla_w_ukv"]
    r["w_gate"] = np.ascontiguousarray(a["gla_w_gate"].transpose(0, 2, 1, 3))
    r["b_gate"] = np.ascontiguousarray(a["gla_b_gate"].transpose(0, 2, 1))
    r["q_norm"] = np.ascontiguousarray(a["mla_q_norm"].reshape(DEPTH, 2, P).transpose(0, 2, 1))
    r["kv_norm"] = a["mla_kv_norm"].reshape(DEPTH, P, 1)
    r["decay"] = a["ret_decay"].reshape(DEPTH, 8)
    r["decay_col"] = np.ascontiguousarray(np.repeat(a["ret_decay"].transpose(0, 2, 1), DK, 1))
    r["lam"] = a["diff_lam"].reshape(DEPTH, 4 * DK)
    one = np.ones((DEPTH, 256), np.float32)
    r["out_g"] = np.concatenate([np.tile(a["diff_norm"], (1, NH)), one, np.tile(a["gla_norm"], (1, NH)),
                                 np.tile(a["ret_norm"], (1, NH))], 1)
    return r


def kernel(**inputs):
    import numpy as np
    import concourse.bacc as bacc
    from concourse.bass_utils import run_bass_kernel_spmd

    nc = bacc.Bacc("TRN2", target_bir_lowering=False, num_devices=1)
    arrays = laid_out(inputs)
    t = {n: nc.dram_tensor("in_" + n, a.shape, mybir.dt.from_np(a.dtype), kind="ExternalInput").ap() for n, a in arrays.items()}
    t["out"] = nc.dram_tensor("out_latent", (P, KD, LAT), F32, kind="ExternalOutput").ap()
    build(nc, t)
    r = run_bass_kernel_spmd(nc, [{"in_" + n: a for n, a in arrays.items()}], core_ids=[0])
    out = r.results[0]["out_latent"]
    return np.ascontiguousarray(out.transpose(2, 1, 0)).reshape(1, LAT, D)
```
